# Optimizing a Trainium2 kernel written in Bass

```python
import jax
import jax.numpy as jnp
from jax import lax
import numpy as np

D_MODEL = 1024
BATCH = 1
SEQ = 2048
DEPTH = 1
DEC_BATCH = 8
DEC_SEQ = 4
PAST_LEN = 8192
PAGE_SIZE = 128

N_MIXERS = 4
D_BRANCH = D_MODEL // N_MIXERS
HEAD_DIM = 64
N_HEADS_A = D_BRANCH // HEAD_DIM
N_HEADS_B = D_BRANCH // HEAD_DIM
LORA_W = 64
LORA_A = 64
B_SHIFT_W = 3 * D_BRANCH + LORA_W + LORA_A
RWKV_SPLITS = (D_BRANCH, 2 * D_BRANCH, 3 * D_BRANCH, 3 * D_BRANCH + LORA_W)
POOL_WINDOWS = (2, 4, 8, 16)
N_POOL_GROUPS = len(POOL_WINDOWS)
POOL_GROUP_DIM = D_BRANCH // N_POOL_GROUPS
POOL_BUF = max(POOL_WINDOWS) - 1
CONV_WIDTH = 31
CONV_BUF = CONV_WIDTH - 1
Q_BLOCK = 128
IN_SIZES = (D_BRANCH, D_BRANCH, D_BRANCH, N_HEADS_A, D_BRANCH,
            B_SHIFT_W, D_BRANCH,
            D_BRANCH, D_BRANCH,
            2 * D_BRANCH, D_BRANCH)
D_IN = sum(IN_SIZES)
D_MIX = N_MIXERS * D_BRANCH
RMS_EPS = 1e-6
LN_EPS = 1e-5
GN_EPS = 64e-5
ATTN_SCALE = HEAD_DIM ** -0.5

kernel_name = 'hymba_fox_rwkv7_pool_conformer_step'

def rmsnorm(x, g):
    x32 = x.astype(jnp.float32)
    y = x32 * lax.rsqrt(jnp.mean(x32 * x32, axis=-1, keepdims=True) + RMS_EPS)
    return (y * g.astype(jnp.float32)).astype(x.dtype)

def split_cols(z):
    bounds = []
    acc = 0
    for s in IN_SIZES[:-1]:
        acc += s
        bounds.append(acc)
    return jnp.split(z, bounds, axis=-1)

def heads(t, n_heads):
    return t.reshape(t.shape[0], t.shape[1], n_heads, HEAD_DIM)

def fox_block(q, k, v, c_q, c_k, q_pos, k_pos):
    s = jnp.einsum('bqhd,bkhd->bhqk', q, k, preferred_element_type=jnp.float32) * ATTN_SCALE
    s = s + jnp.swapaxes(c_q, 1, 2)[:, :, :, None] - jnp.swapaxes(c_k, 1, 2)[:, :, None, :]
    s = jnp.where(k_pos[None, :] <= q_pos[:, None], s, -jnp.inf)
    p = jax.nn.softmax(s, axis=-1)
    return jnp.einsum('bhqk,bkhd->bqhd', p.astype(v.dtype), v)

def fox_prompt(q, k, v, logf):
    t = q.shape[1]
    c = jnp.cumsum(logf, axis=1)
    pos = jnp.arange(t)
    outs = []
    for i in range(t // Q_BLOCK):
        lo, hi = i * Q_BLOCK, (i + 1) * Q_BLOCK
        outs.append(fox_block(q[:, lo:hi], k[:, :hi], v[:, :hi], c[:, lo:hi], c[:, :hi], pos[lo:hi], pos[:hi]))
    return jnp.concatenate(outs, axis=1)

def fox_sample(q, k, v, logf, cache_k, cache_v, cache_logf, page_table, layer):
    db, t = q.shape[0], q.shape[1]
    past = page_table.shape[1] * PAGE_SIZE
    k_past = cache_k[page_table, layer].reshape(db, past, N_HEADS_A, HEAD_DIM)
    v_past = cache_v[page_table, layer].reshape(db, past, N_HEADS_A, HEAD_DIM)
    lf_past = cache_logf[page_table, layer].reshape(db, past, N_HEADS_A).astype(jnp.float32)
    k_all = jnp.concatenate([k_past.astype(k.dtype), k], axis=1)
    v_all = jnp.concatenate([v_past.astype(v.dtype), v], axis=1)
    c = jnp.cumsum(jnp.concatenate([lf_past, logf], axis=1), axis=1)
    q_pos = past + jnp.arange(t)
    k_pos = jnp.arange(past + t)
    return fox_block(q, k_all, v_all, c[:, past:], c, q_pos, k_pos)

def rwkv7_step(s, inp):
    r_t, w_t, k_t, v_t, kk_t, a_t = inp
    s_kk = jnp.einsum('bhvk,bhk->bhv', s, kk_t)
    s = s * w_t[:, :, None, :] - s_kk[..., None] * (kk_t * a_t)[:, :, None, :] + v_t[..., None] * k_t[:, :, None, :]
    o = jnp.einsum('bhvk,bhk->bhv', s, r_t)
    return s, o

def rwkv7_mix(sh, shift_prev, s0, rw_mu, rw_w0, rw_wup, rw_a0, rw_aup, rw_kk, rw_ka, rw_rk, rw_gn_g, rw_gn_b):
    b, t, _ = sh.shape
    f32 = jnp.float32
    prev = jnp.concatenate([shift_prev[:, None, :].astype(sh.dtype), sh[:, :-1]], axis=1)
    xm = sh + rw_mu * (prev - sh)
    r, k, v, wd, ad = jnp.split(xm.astype(f32), RWKV_SPLITS, axis=-1)
    w = -jax.nn.softplus(-(rw_w0 + jnp.tanh(wd) @ rw_wup.astype(f32))) - 0.5
    decay = jnp.exp(-jnp.exp(w))
    a = jax.nn.sigmoid(rw_a0 + ad @ rw_aup.astype(f32))
    kk = heads(k * rw_kk, N_HEADS_B)
    kk = kk * lax.rsqrt(jnp.maximum(jnp.sum(kk * kk, axis=-1, keepdims=True), 1e-12))
    k = k * (1.0 + (a - 1.0) * rw_ka)
    rh, dh, kh, vh, ah = (heads(z, N_HEADS_B) for z in (r, decay, k, v, a))
    xs = tuple(jnp.moveaxis(z, 1, 0) for z in (rh, dh, kh, vh, kk, ah))
    s_final, o = lax.scan(rwkv7_step, s0.astype(f32), xs)
    o = jnp.moveaxis(o, 0, 1)
    mean = jnp.mean(o, axis=-1, keepdims=True)
    var = jnp.mean(jnp.square(o - mean), axis=-1, keepdims=True)
    o = ((o - mean) * lax.rsqrt(var + GN_EPS)).reshape(b, t, D_BRANCH) * rw_gn_g + rw_gn_b
    bonus = jnp.sum(rh * kh * rw_rk, axis=-1, keepdims=True) * vh
    o = o + bonus.reshape(b, t, D_BRANCH)
    return o.astype(sh.dtype), s_final, sh[:, -1]

def pool_mixer(u, buf, pos, pool_w, pool_scale):
    b, t, _ = u.shape
    ext = jnp.concatenate([buf.astype(u.dtype), u], axis=1)
    cs = jnp.cumsum(ext.astype(jnp.float32), axis=1)
    cs = jnp.concatenate([jnp.zeros_like(cs[:, :1]), cs], axis=1)
    groups = []
    for g, w in enumerate(POOL_WINDOWS):
        lo, hi = g * POOL_GROUP_DIM, (g + 1) * POOL_GROUP_DIM
        win = cs[:, POOL_BUF + 1:POOL_BUF + 1 + t, lo:hi] - cs[:, POOL_BUF + 1 - w:POOL_BUF + 1 - w + t, lo:hi]
        cnt = jnp.minimum(pos + 1, w).astype(jnp.float32)
        groups.append(win / cnt[None, :, None])
    pooled = jnp.concatenate(groups, axis=-1) - u.astype(jnp.float32)
    y = jnp.einsum('btgc,gcd->btgd', pooled.reshape(b, t, N_POOL_GROUPS, POOL_GROUP_DIM), pool_w.astype(jnp.float32))
    y = y.reshape(b, t, D_BRANCH) * pool_scale
    return y.astype(u.dtype), ext[:, -POOL_BUF:]

def conv_module(u, buf, conv_w, conv_b, ln_g, ln_b, pw_out):
    u1, u2 = jnp.split(u, 2, axis=-1)
    glu = u1 * jax.nn.sigmoid(u2)
    ext = jnp.concatenate([buf.astype(glu.dtype), glu], axis=1)
    y = lax.conv_general_dilated(ext, conv_w[:, None, :].astype(ext.dtype), window_strides=(1,), padding='VALID',
                                 dimension_numbers=('NWC', 'WIO', 'NWC'), feature_group_count=D_BRANCH) + conv_b
    y32 = y.astype(jnp.float32)
    mean = jnp.mean(y32, axis=-1, keepdims=True)
    var = jnp.mean(jnp.square(y32 - mean), axis=-1, keepdims=True)
    yn = (y32 - mean) * lax.rsqrt(var + LN_EPS) * ln_g + ln_b
    out = jax.nn.silu(yn).astype(u.dtype) @ pw_out
    return out, ext[:, -CONV_BUF:]

def mixer_layer(x, pos, attend, wkv0, shift0, pool0, conv0,
                norm_g, w_in, fox_bf, rw_mu, rw_w0, rw_wup, rw_a0, rw_aup, rw_kk, rw_ka, rw_rk, rw_gn_g, rw_gn_b,
                pool_w, pool_scale, conv_w, conv_b, ln_g, ln_b, pw_out, w_out):
    b, t, _ = x.shape
    h = rmsnorm(x, norm_g)
    z = jnp.einsum('btd,de->bte', h, w_in)
    q_a, k_att, v_a, f_a, g_a, sh_b, g_b, u_c, g_c, u_d, g_d = split_cols(z)
    logf = jax.nn.log_sigmoid((f_a + fox_bf).astype(jnp.float32))
    qh, kh, vh = heads(q_a, N_HEADS_A), heads(k_att, N_HEADS_A), heads(v_a, N_HEADS_A)
    o_a = attend(qh, kh, vh, logf).reshape(b, t, D_BRANCH)
    o_b, wkv1, shift1 = rwkv7_mix(sh_b, shift0, wkv0, rw_mu, rw_w0, rw_wup, rw_a0, rw_aup, rw_kk, rw_ka, rw_rk, rw_gn_g, rw_gn_b)
    o_c, pool1 = pool_mixer(u_c, pool0, pos, pool_w, pool_scale)
    o_d, conv1 = conv_module(u_d, conv0, conv_w, conv_b, ln_g, ln_b, pw_out)
    mixed = jnp.concatenate([o_a * jax.nn.silu(g_a), o_b * jax.nn.silu(g_b),
                             o_c * jax.nn.silu(g_c), o_d * jax.nn.silu(g_d)], axis=-1)
    x = x + jnp.einsum('bte,ed->btd', mixed, w_out)
    return x, kh, vh, logf, wkv1, shift1, pool1, conv1

def setup_inputs(seed: int = 0) -> dict:
    key = jax.random.key(seed)
    ks = jax.random.split(key, 40)
    f32 = jnp.float32
    n_pages = PAST_LEN // PAGE_SIZE
    n_used = DEC_BATCH * n_pages
    n_phys = n_used + n_used // 4

    def nrm(k, shape, s):
        return s * jax.random.normal(k, shape, f32)

    page_table = jax.random.permutation(ks[0], n_phys)[:n_used].reshape(DEC_BATCH, n_pages).astype(jnp.int32)
    return {
        'x_prompt': nrm(ks[1], (BATCH, SEQ, D_MODEL), 1.0),
        'x_sample': nrm(ks[2], (DEC_BATCH, DEC_SEQ, D_MODEL), 1.0),
        'cache_k': nrm(ks[3], (n_phys, DEPTH, PAGE_SIZE, N_HEADS_A, HEAD_DIM), 1.0),
        'cache_v': nrm(ks[4], (n_phys, DEPTH, PAGE_SIZE, N_HEADS_A, HEAD_DIM), 1.0),
        'cache_logf': jax.nn.log_sigmoid(3.0 + jax.random.normal(ks[5], (n_phys, DEPTH, PAGE_SIZE, N_HEADS_A), f32)),
        'state_wkv': nrm(ks[6], (DEC_BATCH, DEPTH, N_HEADS_B, HEAD_DIM, HEAD_DIM), 0.1),
        'state_shift': nrm(ks[7], (DEC_BATCH, DEPTH, B_SHIFT_W), 1.0),
        'state_pool': nrm(ks[8], (DEC_BATCH, DEPTH, POOL_BUF, D_BRANCH), 1.0),
        'state_conv': nrm(ks[9], (DEC_BATCH, DEPTH, CONV_BUF, D_BRANCH), 0.5),
        'page_table': page_table,
        'norm_g': 1.0 + nrm(ks[10], (DEPTH, D_MODEL), 0.05),
        'w_in': nrm(ks[11], (DEPTH, D_MODEL, D_IN), D_MODEL ** -0.5),
        'fox_bf': jax.random.uniform(ks[12], (DEPTH, N_HEADS_A), f32, 1.0, 5.0),
        'rw_mu': jax.random.uniform(ks[13], (DEPTH, B_SHIFT_W), f32, 0.0, 1.0),
        'rw_w0': nrm(ks[14], (DEPTH, D_BRANCH), 0.5) - 0.5,
        'rw_wup': nrm(ks[15], (DEPTH, LORA_W, D_BRANCH), 0.5 * LORA_W ** -0.5),
        'rw_a0': nrm(ks[16], (DEPTH, D_BRANCH), 0.1),
        'rw_aup': nrm(ks[17], (DEPTH, LORA_A, D_BRANCH), 0.5 * LORA_A ** -0.5),
        'rw_kk': 0.85 + nrm(ks[18], (DEPTH, D_BRANCH), 0.05),
        'rw_ka': 1.0 + nrm(ks[19], (DEPTH, D_BRANCH), 0.05),
        'rw_rk': nrm(ks[20], (DEPTH, N_HEADS_B, HEAD_DIM), 0.1),
        'rw_gn_g': 1.0 + nrm(ks[21], (DEPTH, D_BRANCH), 0.05),
        'rw_gn_b': nrm(ks[22], (DEPTH, D_BRANCH), 0.02),
        'pool_w': nrm(ks[23], (DEPTH, N_POOL_GROUPS, POOL_GROUP_DIM, POOL_GROUP_DIM), POOL_GROUP_DIM ** -0.5),
        'pool_scale': 1.0 + nrm(ks[24], (DEPTH, D_BRANCH), 0.05),
        'conv_w': nrm(ks[25], (DEPTH, CONV_WIDTH, D_BRANCH), CONV_WIDTH ** -0.5),
        'conv_b': nrm(ks[26], (DEPTH, D_BRANCH), 0.02),
        'ln_g': 1.0 + nrm(ks[27], (DEPTH, D_BRANCH), 0.05),
        'ln_b': nrm(ks[28], (DEPTH, D_BRANCH), 0.02),
        'pw_out': nrm(ks[29], (DEPTH, D_BRANCH, D_BRANCH), D_BRANCH ** -0.5),
        'w_out': nrm(ks[30], (DEPTH, D_MIX, D_MODEL), D_MIX ** -0.5),
        'final_norm_g': 1.0 + nrm(ks[31], (D_MODEL,), 0.05),
    }

def reference(x_prompt, x_sample, cache_k, cache_v, cache_logf, state_wkv, state_shift, state_pool, state_conv,
              page_table, norm_g, w_in, fox_bf, rw_mu, rw_w0, rw_wup, rw_a0, rw_aup, rw_kk, rw_ka, rw_rk,
              rw_gn_g, rw_gn_b, pool_w, pool_scale, conv_w, conv_b, ln_g, ln_b, pw_out, w_out, final_norm_g):
    weights = (norm_g, w_in, fox_bf, rw_mu, rw_w0, rw_wup, rw_a0, rw_aup, rw_kk, rw_ka, rw_rk, rw_gn_g, rw_gn_b,
               pool_w, pool_scale, conv_w, conv_b, ln_g, ln_b, pw_out, w_out)
    b_p, t_p = x_prompt.shape[0], x_prompt.shape[1]
    past = page_table.shape[1] * PAGE_SIZE
    pos_p = jnp.arange(t_p)
    pos_s = past + jnp.arange(x_sample.shape[1])
    wkv_zero = jnp.zeros((b_p, N_HEADS_B, HEAD_DIM, HEAD_DIM), jnp.float32)
    shift_zero = jnp.zeros((b_p, B_SHIFT_W), x_prompt.dtype)
    pool_zero = jnp.zeros((b_p, POOL_BUF, D_BRANCH), x_prompt.dtype)
    conv_zero = jnp.zeros((b_p, CONV_BUF, D_BRANCH), x_prompt.dtype)

    xp, xs = x_prompt, x_sample
    outs_p, outs_s = [], []
    for l in range(DEPTH):
        lw = tuple(w[l] for w in weights)
        xp, *st_p = mixer_layer(xp, pos_p, fox_prompt, wkv_zero, shift_zero, pool_zero, conv_zero, *lw)
        attend_s = lambda q, k, v, lf, l=l: fox_sample(q, k, v, lf, cache_k, cache_v, cache_logf, page_table, l)
        xs, *st_s = mixer_layer(xs, pos_s, attend_s, state_wkv[:, l], state_shift[:, l], state_pool[:, l],
                                state_conv[:, l], *lw)
        outs_p.append(st_p)
        outs_s.append(st_s)

    def stk(outs, i):
        return jnp.stack([o[i] for o in outs], axis=1)

    y_prompt = rmsnorm(xp, final_norm_g)
    y_sample = rmsnorm(xs, final_norm_g)
    return (y_prompt, y_sample,
            stk(outs_p, 0), stk(outs_p, 1), stk(outs_p, 2), stk(outs_p, 3), stk(outs_p, 4), stk(outs_p, 5), stk(outs_p, 6),
            stk(outs_s, 0), stk(outs_s, 1), stk(outs_s, 2), stk(outs_s, 3), stk(outs_s, 4), stk(outs_s, 5), stk(outs_s, 6))


_drawn_inputs = setup_inputs


def setup_inputs(seed=0):
    import zlib

    import numpy as np

    out = dict(_drawn_inputs(seed))
    spreads = {}
    factors = {'cache_logf': 20.528,
     'rw_kk': 22.628,
     'rw_gn_g': 4.137,
     'rw_gn_b': 24.49,
     'pool_scale': 4.435,
     'conv_b': 8.0,
     'ln_g': 5.793,
     'ln_b': 29.014}
    for name, (base, spread) in spreads.items():
        noise = np.random.default_rng([zlib.crc32(name.encode()), seed]).standard_normal(out[name].shape)
        drawn = base * np.exp(spread * noise) if base else spread * noise
        out[name] = jnp.asarray(drawn.astype(out[name].dtype))
    for name, factor in factors.items():
        out[name] = (out[name] * factor).astype(out[name].dtype)
    return out
```

```python
import concourse.bass as bass
from concourse import mybir
from contextlib import ExitStack, contextmanager

F32 = mybir.dt.float32
BF16 = mybir.dt.bfloat16
I32 = mybir.dt.int32
ALU = mybir.AluOpType
ACT = mybir.ActivationFunctionType
AX = mybir.AxisListType

P = 128
D_MODEL, SEQ, DEC_BATCH, DEC_SEQ = 1024, 2048, 8, 4
SMP = DEC_BATCH * DEC_SEQ
T_ALL = SEQ + SMP
KT = D_MODEL // P
TT = SEQ // P
CHUNKS = 5
CW = T_ALL // CHUNKS
RMS_EPS, LN_EPS, GN_EPS = 1e-6, 1e-5, 64e-5

UC0, GC0, U1D, U2D, GD0, R0, K0, V0, WA, GB0, FG, QA, KA, VA, GA = 0, 2, 4, 6, 8, 10, 12, 14, 16, 17, 19, 20, 22, 24, 26
N_SLOTS = 28
COL_CD, COL_B, COL_GB1, COL_F, COL_A, COL_GA = 2180, 1028, 2052, 768, 0, 772
MIX_A, MIX_B, MIX_C, MIX_D = 0, 2, 4, 6
ROWS256 = ['rw_w0', 'rw_a0', 'rw_kk', 'rw_ka', 'rw_rk', 'rw_gn_g', 'rw_gn_b', 'pool_scale', 'conv_b', 'ln_g', 'ln_b']
PW0, PA0, PKK, PKA, PRK, PGG, PGB, PPS, PCB, PLG, PLB = range(11)
PCW = 11
CONV_WIDTH, POOL_BUF = 31, 15
CONV_BUF = CONV_WIDTH - 1
POOL_WINDOWS = ((2, 4), (8, 16))
POOL_S = POOL_BUF + DEC_SEQ
CONV_S = CONV_BUF + DEC_SEQ
POOL_EXT = POOL_BUF + SEQ + DEC_BATCH * POOL_S
CONV_EXT = CONV_BUF + SEQ + DEC_BATCH * CONV_S
SHIFT_S = 1 + DEC_SEQ
SHIFT_EXT = 1 + SEQ + DEC_BATCH * SHIFT_S
RT = 16
PAGE, N_PAGES = 128, 64
PT = P // RT
TJ = PAGE // RT
DT = N_PAGES // PT
KV_ROW = TJ * 256
SC = DT * TJ * 16
CH = 64
NCH = SEQ // CH
DECAY = -0.6065306597126334
NROW = PCW + CONV_WIDTH


class Chain:

    def __init__(self, eng, sem):
        self.eng, self.sem, self.base, self.n = eng, sem, 0, 0

    def link(self, ins):
        ins.then_inc(self.sem, 1)
        self.n += 1
        self.eng.wait_ge(self.sem, self.base + self.n)

    def mark(self, ins):
        ins.then_inc(self.sem, 1)
        self.n += 1

    def join(self):
        self.eng.wait_ge(self.sem, self.base + self.n)

    @contextmanager
    def body(self, i, lo, hi, per):
        start = self.n
        assert isinstance(self.base, int)
        self.base, self.n = (i - lo) * per + (self.base + start), 0
        yield
        assert self.n == per, self.n
        self.base, self.n = 0, start + (hi - lo) * per


def build(nc, I, O):
    ctx = ExitStack()
    with ctx:
        ctx.enter_context(nc.allow_non_contiguous_dma(reason="states are small: a few rows per sequence"))

        def sb(name, shape, dt=F32):
            return ctx.enter_context(nc.sbuf_tensor(name, shape, dt))

        def sem(name):
            return ctx.enter_context(nc.semaphore(name))

        zT = nc.dram_tensor("zT", [N_SLOTS, P, T_ALL], F32, kind="Internal").ap()

        psum = ctx.enter_context(nc.psum_tensor("psum", [P, 8, 512], F32))
        zT_r = zT.rearrange("s p t -> p s t")
        mixT = nc.dram_tensor("mixT", [8, P, T_ALL], F32, kind="Internal").ap()
        rkv = nc.dram_tensor("rkv", [6, P, T_ALL], F32, kind="Internal").ap()
        rwS = nc.dram_tensor("rwS", [4, 2, P, SEQ], F32, kind="Internal").ap()
        rkk = nc.dram_tensor("rkk", [2, P, T_ALL], F32, kind="Internal").ap()
        ident = sb("ident", [P, P])
        ones_ln = sb("ones_ln", [P, P])
        ones_head = sb("ones_head", [P, P])
        pw_diag = sb("pw_diag", [P, 2, P])
        pwo = sb("pwo", [P, 2, 256])
        lora = sb("lora", [P, 2, 256])
        cnt = sb("cnt", [P, 2, 16])
        fix = sb("fix", [P, 2, 16])
        one_m_ka = sb("one_m_ka", [P, 2])
        ones_s = sb("ones_s", [P, 1])
        pend = sb("pend", [P, 2, NCH])
        smp = sb("smp", [P, 6, 2, SMP])
        par = sb("par", [P, 2, NROW])
        par7 = sb("par7", [P, 15])
        st_pool = sb("st_pool", [P, 2, 120])
        st_conv = sb("st_conv", [P, 2, 240])
        st_shift = sb("st_shift", [P, 7, DEC_BATCH])
        HT = KT * T_ALL
        ARENA = 26200
        big = sb("big", [P, HT + ARENA])

        def area(off, *shape):
            n = 1
            for d in shape:
                n *= d
            a = big[:, off:off + n]
            assert off + n <= HT + ARENA
            if len(shape) == 2:
                a = a.rearrange("p (a b) -> p a b", a=shape[0])
            if len(shape) == 3:
                a = a.rearrange("p (a b c) -> p a b c", a=shape[0], b=shape[1])
            return a

        hT = area(0, KT, T_ALL)
        EC, ED, PO, AC = HT, HT + 4430, HT + 9130, HT + 13330
        SA, U2 = HT + 17490, HT + 21920
        xt = area(SA, 2, D_MODEL)
        xh = area(U2, 2, D_MODEL)
        ext_c = area(EC, 2, POOL_EXT)
        sums = area(SA, 2, POOL_EXT)
        pooled = area(PO, 2, T_ALL)
        ext_d = area(ED, 2, CONV_EXT)
        u2d = area(U2, 2, T_ALL)
        conv = area(AC, 2, T_ALL)
        rows256 = area(AC, 256)[0:NROW]
        rows128 = area(AC + 256, P)[0:15]
        st_rows = area(AC + 384, 3, 256)[0:120]
        sh_rows = area(AC + 1152, 896)[0:DEC_BATCH]
        gate_c = area(SA, 2, T_ALL)
        gate_d = area(U2, 2, T_ALL)
        sh_ext = area(EC, 2, SHIFT_EXT)
        sh_mix = area(PO, 2, SHIFT_EXT)
        wa = area(ED, T_ALL)
        ksq = area(SA, 2, T_ALL)
        ln_sq = area(EC, 2, T_ALL)
        ln_inv = area(PO, T_ALL)
        kinv = area(SA, 2, T_ALL)
        sig_w = area(PO, 2, T_ALL)
        rate = area(EC, 2, T_ALL)
        rw_r = area(AC, T_ALL)
        rw_k = area(AC + T_ALL, T_ALL)
        rw_L = area(ED, T_ALL)
        rw_t = area(ED + T_ALL, T_ALL)
        rw_kk = area(U2, T_ALL)
        seg = area(U2 + T_ALL, SEQ)
        ss = sb("ss", [P, 2])
        rstd = sb("rstd", [P, 2])
        wbuf = sb("wbuf", [P, 2, KT, P])
        zst = sb("zst", [P, 2, T_ALL])

        made = sem("made")
        IDENT, ONES, COUNTS, PADS, RMASKS, MASKS, LANE, DCONST = 0, 2, 8, 9, 13, 24, 28, 29
        rows_in = sem("rows_in")
        par_tr = sem("par_tr")
        par_ready = sem("par_ready")
        x_in = [sem("x_in0"), sem("x_in1")]
        sq_done = sem("sq_done")
        inv_ready = sem("inv_ready")
        rstd_ready = sem("rstd_ready")
        h_ready = sem("h_ready")
        h_tr = sem("h_tr")
        hT_ready = sem("hT_ready")
        w_in = [sem("w_in0"), sem("w_in1")]
        z_mm = sem("z_mm")
        z_evac = sem("z_evac")
        z_stored = [sem("z_stored0"), sem("z_stored1")]
        dve_chain = sem("dve_chain")
        consts_in = sem("consts_in")
        c_in = sem("c_in")
        d_in = sem("d_in")
        pooled_ready = sem("pooled_ready")
        gc_in = sem("gc_in")
        gates = sem("gates")
        GATE_C, GATE_D, GATE_A, GATE_S, GATE_B = 0, 2, 4, 6, 7
        d_sig = sem("d_sig")
        glu_ready = sem("glu_ready")
        conv_done = sem("conv_done")
        gd_in = sem("gd_in")
        small_mm = sem("small_mm")
        small_read = sem("small_read")
        mix_stored = sem("mix_stored")
        out_stored = sem("out_stored")
        d_sq = sem("d_sq")
        d_inv = sem("d_inv")
        d_root = sem("d_root")
        d_norm = sem("d_norm")
        d_act = sem("d_act")
        sh_in = [sem("sh_in0"), sem("sh_in1")]
        sh_done = sem("sh_done")
        sh_stored = [sem("sh_stored0"), sem("sh_stored1")]
        ksq_ready = sem("ksq_ready")
        wa_ready = sem("wa_ready")
        kinv_pre = sem("kinv_pre")
        kinv_ready = sem("kinv_ready")
        lora_mm = sem("lora_mm")
        lora_read = sem("lora_read")
        rk_in = sem("rk_in")
        rkk_ready = sem("rkk_ready")
        rkk_stored = sem("rkk_stored")
        L_ready = sem("L_ready")
        exp_ready = sem("exp_ready")
        rw_ready = sem("rw_ready")
        rw_stored = sem("rw_stored")
        st_stored = sem("st_stored")

        w_v = I['w_in'][0].rearrange("(k p) c -> p k c", p=P)

        def slot_columns(p, u):
            if isinstance(p, int):
                if p == 9:
                    return (COL_GB1, COL_F)[u]
                if p == 13:
                    return COL_GA + P * u
            raise AssertionError

        def reads_through(g):
            return g + 1 + min(max(g + 1 - 10, 0), 5)

        kaug = area(0, 4, SEQ)
        vtok = area(4 * SEQ, TT, 256)
        gate_a = area(4 * SEQ + TT * 256, 2, T_ALL)
        probs = zst
        probsT = wbuf[:, :, :, :].rearrange("p a b c -> p (a b c)")
        kvt = area(HT, 2, 4, P)
        kvs = area(HT + 1024, 2, 512)
        fx = area(HT + 2048, T_ALL)[0:4]
        fa = area(HT + 4128, T_ALL)[0:4]
        nc_ = area(HT + 6208, T_ALL)[0:4]
        ones_t = area(HT + 8288, SEQ)[0:4]
        qaug = area(HT + 10336, 2, 4, P)
        lg = area(HT + 11360, P)
        lbc = area(HT + 11488, P)
        lft = area(HT + 11616, TT, 4)
        kT_s = sb("kT_s", [P, 2, SMP])
        qT_s = sb("qT_s", [P, 2, SMP])
        kv_s = sb("kv_s", [SMP, 512])
        lf_s = sb("lf_s", [SMP, 8])
        bf_col = sb("bf_col", [4, 1])
        maskb = area(HT + 11700, (512 + 3 * P) // 2).bitcast(BF16)
        identb = area(HT + 12160, P // 2).bitcast(BF16)
        oc = area(HT + 12240, P)
        mx = sb("mx", [P, 2])
        nb = sb("nb", [P, 2])
        lsum = sb("lsum", [P, 2])
        linv = sb("linv", [P, 2])

        a_in = sem("a_in")
        kr_in = sem("kr_in")
        f_pre = sem("f_pre")
        f_abs = sem("f_abs")
        nl_ready = sem("nl_ready")
        nc_ready = sem("nc_ready")
        kvt_in = [sem("kvt_in0"), sem("kvt_in1")]
        kv_tr = sem("kv_tr")
        kv_copied = sem("kv_copied")
        v_kept = sem("v_kept")
        kv_stored = [sem("kv_stored0"), sem("kv_stored1")]
        f_tr = sem("f_tr")
        f_copied = sem("f_copied")
        kvs_tr = sem("kvs_tr")
        kvs_copied = sem("kvs_copied")
        q_in = [sem("q_in0"), sem("q_in1")]
        ga_in = sem("ga_in")
        qones_ready = sem("qones_ready")
        s_mm = sem("s_mm")
        s_max = sem("s_max")
        p_ready = sem("p_ready")
        p_tr = sem("p_tr")
        pT_ready = sem("pT_ready")
        o_mm = sem("o_mm")
        lb_ready = sem("lb_ready")
        lb_tr = sem("lb_tr")
        lg_ready = sem("lg_ready")
        o_read = sem("o_read")
        o_copied = sem("o_copied")
        mixa_stored = sem("mixa_stored")

        RHO, ALP, KTI, BTI, VAL = 0, 2, 4, 6, 8
        rin = area(0, 2, 10, P)
        tok_k = area(9984, 2, 256)
        tok_b = area(2560, 2, 256)
        tok_v = area(3072, 256)
        gb = area(3328, 4, 2, P)
        gk = area(4352, 4, 2, P)
        mpow = area(5376, 3, 4, P)
        mpowT = area(6912, 2, 4, P)
        sol = area(7936, 4, P)
        qT_r = area(8448, 2, P)
        trans = area(HT + 13704, 4, P)
        state = area(8960, 2 * 2 * 2, P)
        pcur = sb("pcur", [P, 2, 2])
        o_rw = area(10496, 2, T_ALL)
        mneg = area(HT + 13000, 2, P)
        mpos = area(HT + 13256, 2, P)
        mrow = area(HT + 13512, P)
        id64 = area(HT + 13640, 64)
        wkv_o = area(HT + 14216, 2, 64)
        s_wkv = area(HT + 14350, DEC_BATCH, 2 * 64)
        z_exp = area(0, 5, DEC_BATCH * 2 * 64)
        s_tmp = area(5120, DEC_BATCH * 2 * 64)
        s_tm2 = area(6144, DEC_BATCH * 2 * 64)
        s_kk = area(7168, 16)
        gn_sq = area(0, 2, T_ALL)
        gn_inv = area(4160, 2, T_ALL)
        g_rkk = area(14656, 2, T_ALL)
        g_v = area(18816, 2, T_ALL)
        gate_b = area(22976, 2, T_ALL)

        id64_ready = sem("id64_ready")
        r_in = [sem("r_in0"), sem("r_in1")]
        R = {n: sem("r_" + n) for n in ('gram_b', 'gram_k', 'gram_m', 'tok_tr', 'kv_mm', 'sqT_mm', 'sq_mm', 'app_mm', 'q_mm',
                                        'tr_mm', 'st_mm', 'o_mm', 'gb', 'gk', 'gm', 'tok', 'kv', 'sqT', 'sq', 'app', 'q',
                                        'tr', 'st', 'pcur', 'o')}
        state_zero = sem("state_zero")
        wkv_tr = sem("wkv_tr")
        wkv_copied = sem("wkv_copied")
        wkv_stored = sem("wkv_stored")
        s_in = sem("s_in")
        s_dec = sem("s_dec")
        s_z = sem("s_z")
        s_mm2 = sem("s_mm2")
        s_used = sem("s_used")
        s_done = sem("s_done")
        gn_in = sem("gn_in")
        gn_mm = sem("gn_mm")
        gn_read = sem("gn_read")
        gn_sq_ready = sem("gn_sq_ready")
        gn_pre = sem("gn_pre")
        gn_root = sem("gn_root")
        mixb_ready = sem("mixb_ready")

        NSLOT = 4
        lf_past = area(HT + 15400, DEC_BATCH * DT, TJ * 4)
        k_slot = area(HT + 17448, NSLOT, KV_ROW)
        bias = area(0, DEC_BATCH * DT, TJ * 4)
        v_slot = area(2048, NSLOT, KV_ROW)
        kT_d = area(10240, 2, 2, 512)
        s_rows = area(12288, DT * 512 + SMP)
        nm_cur = area(12288 + DT * 512 + SMP, P)
        q_cur = area(16544, 2, 8)
        sel_r = area(16560, 2, 8)
        p_new = area(16576, 16)
        bias_w = area(HT + 11200, DT * 4, P)
        wo = area(HT, 8, D_MODEL)
        gf = area(HT + 8192, D_MODEL)
        mt = area(HT + 15296, 2, 8, P)
        later = area(HT + 9216, P)
        ones_a = area(HT + 9344, P)
        tot = area(HT + 9472, DEC_BATCH * DT * 4)
        tsum = area(HT + 9728, DEC_BATCH * DT * 4)
        tsuf = area(HT + 9984, DEC_BATCH, DT, 4)
        nmask = area(HT + 10240, DEC_BATCH, 16)[0:SMP]
        v_new = area(HT + 10368, 256)
        qbd = area(HT + 10624, DEC_BATCH, 2, 8)
        sel = area(HT + 10752, 16)
        m8 = area(HT + 10768, DT + 1)
        m1 = area(HT + 10784, 1)
        neg_m = area(HT + 10785, 1)
        l_row = area(HT + 10786, 1)
        li = area(HT + 10817, 16)
        pv = area(HT + 10833, 256)
        o_s = area(HT + 11089, 2, SMP)
        yb = wbuf[:, :, :, :].rearrange("p a b c -> p a (b c)")
        wb = wbuf[:, :, :, :].rearrange("p a b c -> p (a b c)")
        pT_d = wb[:, 0:DT * 128].rearrange("p (c g x) -> p c g x", g=4, x=8)
        l_all = wb[:, 1024:1024 + P]
        m_row = wb[0:1, 1024 + P:1024 + 2 * P]
        m_half = wb[0:1, 1024 + 2 * P:1024 + 2 * P + 64]
        gate_s = sb("gate_s", [P, 2, SMP])
        pidx = sb("pidx", [P, DEC_BATCH * DT], I32)
        pidf = sb("pidf", [P, DEC_BATCH * DT])
        lane = sb("lane", [P, 1], I32)
        lanef = sb("lanef", [P, 1])

        idx_ready = sem("idx_ready")
        lf_in = sem("lf_in")
        k_in = [sem(f"k_in{n}") for n in range(NSLOT)]
        v_in = [sem(f"v_in{n}") for n in range(NSLOT)]
        tot_ready = sem("tot_ready")
        bias_ready = sem("bias_ready")
        after = dict(k_tr=('sqT_mm', 5), sc_mm=('sq_mm', 4), new_mm=('gram_b', 1), m_tr=('gram_k', 1), m_mm=('gram_m', 1),
                     pv_mm=('app_mm', 6), o_mm=('o_mm', 1), suf_mm=('kv_mm', 1), y_mm=('q_mm', 1), p_tr=('tok_tr', 1), b_mm=('tr_mm', 1),
                     prep=('gb', 1), pT=('gk', 1), m1=('gm', 1), m_row=('pcur', 1), neg_m=('kv', 1), l_all=('sqT', 5), pv=('app', 6),
                     li=('q', 1), o=('st', 4), y_sum=('tr', 2), s=('tok', 6), p=('sq', 4), kT1=('o', 1))
        D = {n: R[old] for n, (old, per) in after.items()}
        D0 = {n: per * TT for n, (old, per) in after.items()}
        D['kT0'], D0['kT0'] = sem("d_kT0"), 0
        mixas_ready = sem("mixas_ready")

        def samples(row):
            return row[:, SEQ:T_ALL].rearrange("p (b i) -> p b i", i=DEC_SEQ)

        def history(row, start, width):
            return row[:, start:start + DEC_BATCH * width].rearrange("p (b w) -> p b w", w=width)

        def shifted_samples(row):
            return history(row, SEQ + 1, SHIFT_S)[:, :, 0:DEC_SEQ]

        block = ctx.enter_context(nc.Block())

        @block.sync
        def _(sp):
            for r, name in enumerate(ROWS256):
                src = I[name][0].rearrange("h d -> (h d)") if name == 'rw_rk' else I[name][0]
                sp.dma_start(rows256[r:r + 1, :], src.rearrange("(o c) -> o c", o=1)).then_inc(rows_in, 16)
            sp.dma_start(rows256[PCW:NROW, :], I['conv_w'][0]).then_inc(rows_in, 16)
            sp.dma_start(rows128[0:8, :], I['norm_g'][0].rearrange("(k p) -> k p", p=P)).then_inc(rows_in, 16)
            sp.dma_start(rows128[8:15, :], I['rw_mu'][0].rearrange("(k p) -> k p", p=P)).then_inc(rows_in, 16)
            sp.dma_start(st_rows[:, 0, :], I['state_pool'].rearrange("b l s c -> (b l s) c")).then_inc(rows_in, 16)
            conv_rows = I['state_conv'].rearrange("b l s c -> (b l s) c")
            sp.dma_start(st_rows[:, 1, :], conv_rows[0:120, :]).then_inc(rows_in, 16)
            sp.dma_start(st_rows[:, 2, :], conv_rows[120:240, :]).then_inc(rows_in, 16)
            sp.dma_start(sh_rows[:, :], I['state_shift'].rearrange("b l c -> (b l) c")).then_inc(rows_in, 16)
            xp = I['x_prompt'][0]
            xs = I['x_sample'].rearrange("b t d -> (b t) d")
            for u in range(2):
                sp.dma_start(xt[:, u, :], xp[u * P:(u + 1) * P, :]).then_inc(x_in[u], 16)
            for u in range(2):
                sp.dma_start(wbuf[:, u], w_v[:, :, COL_CD + u * P:COL_CD + (u + 1) * P]).then_inc(w_in[u], 16)
            with sp.Fori(1, TT // 2) as i:
                for u in range(2):
                    sp.wait_ge(h_ready, i * 2 + (u - 1))
                    sp.dma_start(xt[:, u, :], xp[bass.ds(i * 2 * P + u * P, P), :]).then_inc(x_in[u], 16)
            sp.wait_ge(h_ready, TT - 1)
            sp.dma_start(xt[0:SMP, 0, :], xs).then_inc(x_in[0], 16)

            def weights(p, col, u):
                sp.wait_ge(z_mm, p * 10 + (5 * u - 5))
                sp.dma_start(wbuf[:, u], w_v[:, :, bass.ds(col, P)]).then_inc(w_in[u], 16)

            with sp.Fori(1, 5) as p:
                for u in range(2):
                    weights(p, p * (2 * P) + (COL_CD + P * u), u)
            with sp.Fori(5, 9) as p:
                for u in range(2):
                    weights(p, p * (2 * P) + (COL_B + P * u - 10 * P), u)
            for u in range(2):
                weights(9, slot_columns(9, u), u)
            with sp.Fori(10, 13) as p:
                for u in range(2):
                    weights(p, p * (2 * P) + (P * u - 20 * P), u)
            for u in range(2):
                weights(13, slot_columns(13, u), u)
            sp.dma_start(O['pool_sample'][:, 0, 0:POOL_BUF - DEC_SEQ, :], I['state_pool'][:, 0, DEC_SEQ:, :]).then_inc(st_stored, 16)
            sp.dma_start(O['conv_sample'][:, 0, 0:CONV_BUF - DEC_SEQ, :], I['state_conv'][:, 0, DEC_SEQ:, :]).then_inc(st_stored, 16)
            for u in range(2):
                sp.wait_ge(z_stored[u], 16 * 14)
            for n in range(7):
                cs = slice(n * P, (n + 1) * P)
                sp.dma_start(O['shift_prompt'][0, :, cs].rearrange("o p -> p o"), zT[R0 + n][:, SEQ - 1:SEQ]).then_inc(st_stored, 16)
                sp.dma_start(O['shift_sample'][:, 0, cs].rearrange("b p -> p b"),
                             zT[R0 + n][:, SEQ:T_ALL].rearrange("p (b i) -> p b i", i=DEC_SEQ)[:, :, DEC_SEQ - 1]).then_inc(st_stored, 16)
            pt = I['page_table'].rearrange("b (t n) -> n (b t)", n=PT)
            for n in range(PT):
                sp.dma_start(pidx[n * RT:(n + 1) * RT, :], pt[n:n + 1, :].to_broadcast([RT, DEC_BATCH * DT])).then_inc(rows_in, 16)
            sp.dma_start(bf_col[:, :], I['fox_bf'][0].rearrange("(h o) -> h o", o=1)).then_inc(a_in, 16)
            sp.wait_ge(z_mm, 10 * 14)
            for t in range(2):
                sp.dma_start(qT_s[:, t, :], zT[QA + t][:, SEQ:T_ALL]).then_inc(a_in, 16)
                sp.dma_start(kT_s[:, t, :], zT[KA + t][:, SEQ:T_ALL]).then_inc(a_in, 16)
                sp.dma_start(gate_a[:, t, :], zT[GA + t]).then_inc(ga_in, 16)
                sp.dma_start(kaug[0:64, 2 * t:2 * t + 2, :],
                             zT[KA + t][:, 0:SEQ].rearrange("(h p) t -> p h t", p=64)).then_inc(a_in, 16)
            sp.wait_ge(rw_stored, 128)
            sp.dma_start(fx, zT[FG][0:4, :]).then_inc(a_in, 16)

            def kv_load(col, n, u):
                sp.dma_start(kvt[:, u, :, 0:n], zT[KA:KA + 4, :, bass.ds(col, n)].rearrange("s p t -> p s t")).then_inc(kvt_in[u], 16)

            def kv_store(i, u):
                for j, name in enumerate(('k_prompt', 'v_prompt')):
                    rows = O[name][0, 0].rearrange("t h d -> t (h d)")
                    sp.dma_start(rows[bass.ds(i * (2 * P) + u * P, P), :], kvs[:, u, j * 256:(j + 1) * 256]).then_inc(kv_stored[u], 16)

            for u in range(2):
                kv_load(u * P, P, u)
            for u in range(2):
                sp.wait_ge(kv_tr, u + 1)
                kv_load((2 + u) * P, P, u)
            for u in range(2):
                sp.wait_ge(kv_copied, u + 1)
                kv_store(0, u)
            with sp.Fori(1, TT // 2 - 1) as i:
                for u in range(2):
                    sp.wait_ge(kv_tr, i * 2 + (u + 1))
                    kv_load(i * (2 * P) + (2 + u) * P, P, u)
                    sp.wait_ge(kv_copied, i * 2 + (u + 1))
                    kv_store(i, u)
            sp.wait_ge(kv_tr, TT - 1)
            kv_load(SEQ, SMP, 0)
            for u in range(2):
                sp.wait_ge(kv_copied, TT - 1 + u)
                kv_store(TT // 2 - 1, u)
            sp.wait_ge(kvs_copied, 1)
            for j, name in enumerate(('k_sample', 'v_sample')):
                sp.dma_start(O[name].rearrange("b l t h d -> (b l t) (h d)"), kv_s[:, j * 256:(j + 1) * 256]).then_inc(st_stored, 16)
            sp.wait_ge(f_copied, 2)
            sp.dma_start(O['logf_prompt'][0, 0].rearrange("(n p) h -> p n h", p=P), lft[:, :, :]).then_inc(st_stored, 16)
            sp.dma_start(O['logf_sample'].rearrange("b l t h -> (b l t) h"), lf_s[:, 0:4]).then_inc(st_stored, 16)
            sp.wait_ge(nc_ready, 1)
            for h in range(4):
                sp.dma_start(kaug[64:65, h, :], nc_[h:h + 1, 0:SEQ]).then_inc(kr_in, 16)

            def q_load(col, u):
                sp.dma_start(qaug[0:64, u, :, :], zT[QA:QA + 2, :, bass.ds(col, P)].rearrange("s (h p) t -> p (s h) t", p=64)).then_inc(q_in[u], 16)

            for u in range(2):
                q_load(u * P, u)
            with sp.Fori(1, TT // 2) as i:
                for u in range(2):
                    sp.wait_ge(s_mm, i * 8 + (4 * u - 4))
                    q_load(i * (2 * P) + u * P, u)
            sp.wait_ge(o_read, 2 * TT)
            for t in range(2):
                sp.dma_start(mixT[MIX_A + t][:, 0:SEQ], gate_a[:, t, 0:SEQ]).then_inc(mixa_stored, 16)
            sp.wait_ge(mixa_stored, 32)

            def chunk_load(col, u):
                sp.dma_start(rin[:, u, 0:8, :], rwS.rearrange("m t p c -> p (m t) c")[:, :, bass.ds(col, P)]).then_inc(r_in[u], 16)
                sp.dma_start(rin[:, u, 8:10, :], rkv[4:6].rearrange("t p c -> p t c")[:, :, bass.ds(col, P)]).then_inc(r_in[u], 16)

            for u in range(2):
                chunk_load(u * P, u)
            for t in range(2):
                sp.dma_start(s_wkv[:, :, t * 64:(t + 1) * 64],
                             I['state_wkv'][:, 0, 2 * t:2 * t + 2].rearrange("b h v k -> (h v) b k")).then_inc(s_in, 16)
                sp.dma_start(g_rkk[:, t, :], rkk[t]).then_inc(gn_in, 16)
                sp.dma_start(g_v[:, t, :], rkv[4 + t]).then_inc(gn_in, 16)
                sp.dma_start(gate_b[:, t, :], zT[GB0 + t]).then_inc(gn_in, 16)
            with sp.Fori(1, TT // 2) as i:
                for u in range(2):
                    sp.wait_ge(R['q'], i * 2 + (u - 1))
                    chunk_load(i * (2 * P) + u * P, u)
            sp.wait_ge(wkv_copied, 2)
            sp.dma_start(O['wkv_prompt'][0, 0].rearrange("(t h) v k -> (h v) t k", h=2), wkv_o[:, :, :]).then_inc(wkv_stored, 16)
            sp.wait_ge(s_done, 1)
            for t in range(2):
                sp.dma_start(O['wkv_sample'][:, 0, 2 * t:2 * t + 2].rearrange("b h v k -> (h v) b k"),
                             s_wkv[:, :, t * 64:(t + 1) * 64]).then_inc(wkv_stored, 16)
            sp.wait_ge(mixb_ready, 1)
            for t in range(2):
                sp.dma_start(mixT[MIX_B + t], o_rw[:, t, :]).then_inc(mixa_stored, 16)
            sp.dma_start(wo[:, :, :], I['w_out'][0].rearrange("(e p) d -> p e d", p=P)).then_inc(rows_in, 16)
            sp.dma_start(gf[:, :], I['final_norm_g'].unsqueeze(0).to_broadcast([P, D_MODEL])).then_inc(rows_in, 16)
            sp.wait_ge(mixa_stored, 32 + 32)
            sp.wait_ge(wkv_stored, 48)
            sp.wait_ge(bias_ready, 1)
            for u in range(2):
                sp.dma_start(zst[:, u, 0:D_MODEL], xp[u * P:(u + 1) * P, :]).then_inc(kvt_in[u], 16)
                sp.dma_start(mt[:, u], mixT.rearrange("e p t -> p e t")[:, :, u * P:(u + 1) * P]).then_inc(q_in[u], 16)
            sp.wait_ge(mixas_ready, 1)
            for t in range(2):
                sp.dma_start(mixT[MIX_A + t][:, SEQ:T_ALL], o_s[:, t, :]).then_inc(mixa_stored, 16)
            sp.wait_ge(mixa_stored, 64 + 32)

            for u in range(2):
                sp.wait_ge(kv_stored[u], 32 * (TT // 2))

            def y_out(rows, u, n=P):
                sp.dma_start(rows, yb[0:n, u, :]).then_inc(kv_stored[u], 16)

            yp = O['y_prompt'][0]
            with sp.Fori(1, TT // 2) as i:
                for u in range(2):
                    sp.wait_ge(D['y_mm'], D0['y_mm'] + i * 2 + (u - 1))
                    sp.dma_start(mt[:, u], mixT.rearrange("e p t -> p e t")[:, :, bass.ds(i * (2 * P) + u * P, P)]).then_inc(q_in[u], 16)
                for u in range(2):
                    sp.wait_ge(h_ready, (TT + 1) + i * 2 + (u - 1))
                    y_out(yp[bass.ds(i * (2 * P) + (u - 2) * P, P), :], u)
                    sp.dma_start(zst[:, u, 0:D_MODEL], xp[bass.ds(i * (2 * P) + u * P, P), :]).then_inc(kvt_in[u], 16)
            sp.wait_ge(D['y_mm'], D0['y_mm'] + TT - 1)
            sp.dma_start(mt[:, 0, :, 0:SMP], mixT.rearrange("e p t -> p e t")[:, :, SEQ:T_ALL]).then_inc(q_in[0], 16)
            for u in range(2):
                sp.wait_ge(h_ready, (TT + 1) + TT - 1 + u)
                y_out(yp[SEQ - (2 - u) * P:SEQ - (1 - u) * P, :], u)
                if u == 0:
                    sp.dma_start(zst[0:SMP, 0, 0:D_MODEL], xs).then_inc(kvt_in[0], 16)
            sp.wait_ge(h_ready, (TT + 1) + TT + 1)
            y_out(O['y_sample'].rearrange("b t d -> (b t) d"), 0, SMP)
            sp.wait_ge(kv_stored[0], 32 * (TT // 2) + 16 * (TT // 2 + 1))
            sp.wait_ge(kv_stored[1], 32 * (TT // 2) + 16 * (TT // 2))
            sp.wait_ge(st_stored, 16 * 20)
            sp.wait_ge(out_stored, 16 * 20)
            sp.wait_ge(mix_stored, 64)
            sp.wait_ge(rw_stored, 128)
            sp.wait_ge(rkk_stored, 32)

        @block.gpsimd
        def _(pool):
            nc.gpsimd.memset(ident[:], 0.0).then_inc(made, 1)
            pool.wait_ge(made, IDENT + 1)
            nc.gpsimd.affine_select(out=ident[:], in_=ident[:], compare_op=ALU.not_equal, fill=1.0, base=0,
                                    pattern=[[-1, P]], channel_multiplier=1).then_inc(made, 1)
            g = nc.gpsimd
            g.memset(ones_ln[:], 1.0 / 256).then_inc(made, 1)
            g.memset(ones_head[:], 0.0).then_inc(made, 1)
            g.memset(pw_diag[:], 0.0).then_inc(made, 1)
            g.memset(lora[:], 0.0).then_inc(made, 1)
            pool.wait_ge(made, ONES + 4)
            for h in range(2):
                g.memset(ones_head[h * 64:h * 64 + 64, h * 64:h * 64 + 64], 1.0).then_inc(made, 1)
            for q in range(4):
                t, h = q // 2, q % 2
                pool.dma_start(pw_diag[h * 64:h * 64 + 64, t, h * 64:h * 64 + 64], I['pool_w'][0, q]).then_inc(consts_in, 16)
            pool.dma_start(pwo[:, :, :], I['pw_out'][0].rearrange("(t p) o -> p t o", p=P)).then_inc(consts_in, 16)
            pool.dma_start(lora[0:64, 0, :], I['rw_wup'][0]).then_inc(consts_in, 16)
            pool.dma_start(lora[64:P, 1, :], I['rw_aup'][0]).then_inc(consts_in, 16)
            pool.wait_ge(made, ONES + 6)
            g.iota(cnt[:, :, :], pattern=[[0, 2], [1, 16]], base=1, channel_multiplier=0,
                   allow_small_or_imprecise_dtypes=True).then_inc(made, 1)
            for t in range(2):
                g.memset(ext_c[:, t, 0:POOL_BUF], 0.0).then_inc(made, 1)
                g.memset(ext_d[:, t, 0:CONV_BUF], 0.0).then_inc(made, 1)

            def z_ready(slot):
                pool.wait_ge(z_stored[slot % 2], 16 * (slot // 2 + 1))

            def load_ext(dst, slot, buf, width, s):
                z_ready(slot)
                pool.dma_start(dst[:, buf:buf + SEQ], zT[slot][:, 0:SEQ]).then_inc(s, 16)
                pool.dma_start(history(dst, buf + SEQ, width)[:, :, buf:buf + DEC_SEQ], samples(zT[slot])).then_inc(s, 16)

            for t in range(2):
                load_ext(ext_c[:, t], UC0 + t, POOL_BUF, POOL_S, c_in)
            for t in range(2):
                load_ext(ext_d[:, t], U1D + t, CONV_BUF, CONV_S, d_in)
            pool.wait_ge(hT_ready, TT + 1)
            for t in range(2):
                z_ready(U2D + t)
                pool.dma_start(u2d[:, t, :], zT[U2D + t]).then_inc(d_in, 16)

            pool.wait_ge(glu_ready, 6)
            for t in range(2):
                cs = slice(t * P, (t + 1) * P)
                pool.dma_start(O['pool_prompt'][0, 0, :, cs].rearrange("s p -> p s"), ext_c[:, t, SEQ:SEQ + POOL_BUF]).then_inc(out_stored, 16)
                for i in range(DEC_SEQ):
                    pool.dma_start(O['pool_sample'][:, 0, POOL_BUF - DEC_SEQ + i, cs].rearrange("b p -> p b"),
                                   history(ext_c[:, t], POOL_BUF + SEQ, POOL_S)[:, :, POOL_BUF + i]).then_inc(out_stored, 16)
                pool.dma_start(O['conv_prompt'][0, 0, :, cs].rearrange("s p -> p s"), ext_d[:, t, SEQ:SEQ + CONV_BUF]).then_inc(out_stored, 16)
                for i in range(DEC_SEQ):
                    pool.dma_start(O['conv_sample'][:, 0, CONV_BUF - DEC_SEQ + i, cs].rearrange("b p -> p b"),
                                   history(ext_d[:, t], CONV_BUF + SEQ, CONV_S)[:, :, CONV_BUF + i]).then_inc(out_stored, 16)

            pool.wait_ge(pooled_ready, 2)
            for t in range(2):
                z_ready(GC0 + t)
                pool.dma_start(gate_c[:, t, :], zT[GC0 + t]).then_inc(gc_in, 16)
            pool.wait_ge(glu_ready, 6)
            for t in range(2):
                z_ready(GD0 + t)
                pool.dma_start(gate_d[:, t, :], zT[GD0 + t]).then_inc(gd_in, 16)
            pool.wait_ge(small_read, reads_through(9))
            for t in range(2):
                pool.dma_start(mixT[MIX_C + t], pooled[:, t, :]).then_inc(mix_stored, 16)

            pool.wait_ge(out_stored, 16 * 20)
            for n in range(9):
                if n < 7:
                    if n >= 2:
                        pool.wait_ge(sh_done, n - 1)
                    load_ext(sh_ext[:, n % 2], R0 + n, 1, SHIFT_S, sh_in[n % 2])
                if n >= 2 and n - 2 < 6:
                    m = n - 2
                    pool.wait_ge(sh_done, m + 1)
                    pool.dma_start(rkv[m][:, 0:SEQ], sh_mix[:, m % 2, 0:SEQ]).then_inc(sh_stored[m % 2], 16)
                    pool.dma_start(samples(rkv[m]), shifted_samples(sh_mix[:, m % 2])).then_inc(sh_stored[m % 2], 16)

            pool.wait_ge(small_read, reads_through(29))
            for t in range(2):
                pool.dma_start(mixT[MIX_D + t], conv[:, t, :]).then_inc(mix_stored, 16)

            pool.wait_ge(mix_stored, 64)
            pool.wait_ge(sh_stored[0], 96)
            pool.wait_ge(sh_stored[1], 96)
            for t in range(2):
                pool.dma_start(rw_r[:, :], rkv[t]).then_inc(rk_in, 16)
                pool.dma_start(rw_k[:, :], rkv[2 + t]).then_inc(rk_in, 16)
                pool.dma_start(smp[:, 5, t, :], rkv[4 + t][:, SEQ:T_ALL]).then_inc(rk_in, 16)
                pool.wait_ge(rkk_ready, t + 1)
                pool.dma_start(rkk[t], rw_t[:, :]).then_inc(rkk_stored, 16)
                for n, (m, src) in enumerate(((1, rw_kk), (0, rw_r), (2, rw_k), (3, rate[:, t]))):
                    pool.wait_ge(rw_ready, 4 * t + n + 1)
                    pool.dma_start(rwS[m, t], src[:, 0:SEQ]).then_inc(rw_stored, 16)
                pool.wait_ge(rw_stored, 64 * (t + 1))

            for m, val in ((mneg, -1.0), (mpos, 1.0)):
                g.memset(m[:, :, :], val).then_inc(made, 1)
            g.memset(mrow[:, :], -1.0).then_inc(made, 1)
            pool.wait_ge(made, RMASKS + 3)
            for m in (mneg, mpos):
                for n in range(2):
                    g.affine_select(out=m[:, n, :], in_=m[:, n, :], compare_op=ALU.is_ge, fill=0.0, base=-n,
                                    pattern=[[1, P]], channel_multiplier=-1).then_inc(made, 1)
            g.affine_select(out=mrow[:, :], in_=mrow[:, :], compare_op=ALU.is_ge, fill=0.0, base=-1,
                            pattern=[[-1, P]], channel_multiplier=1).then_inc(made, 1)
            pool.wait_ge(made, RMASKS + 8)
            for m in (mneg, mpos):
                g.memset(m[0:64, :, 64:P], 0.0).then_inc(made, 1)
            g.memset(mrow[64:P, 0:64], 0.0).then_inc(made, 1)
            pool.wait_ge(made, RMASKS + 11)
            g.memset(maskb[:, :], 0.0).then_inc(made, 1)
            pool.wait_ge(made, MASKS + 1)
            g.affine_select(out=maskb[:, :], in_=maskb[:, :], compare_op=ALU.is_ge, fill=-1e30, base=3 * P,
                            pattern=[[-1, 512 + 3 * P]], channel_multiplier=1).then_inc(made, 1)
            g.memset(identb[:, :], 0.0).then_inc(made, 1)
            pool.wait_ge(made, MASKS + 3)
            g.affine_select(out=identb[:, :], in_=identb[:, :], compare_op=ALU.not_equal, fill=1.0, base=0,
                            pattern=[[-1, P]], channel_multiplier=1).then_inc(made, 1)

            g.iota(lane[:, :], pattern=[[0, 1]], base=0, channel_multiplier=1).then_inc(made, 1)
            pool.wait_ge(idx_ready, 1)

            def gather(dst, cache, bt, s):
                g.indirect_dma_start(out=dst, out_offset=None, in_=cache,
                                     in_offset=bass.IndirectOffsetOnAxis(ap=pidx[:, bt:bt + 1], axis=0)).then_inc(s, 16)

            ck = I['cache_k'].rearrange("n l (r j) h d -> (n l r) (j h d)", r=RT)
            cv = I['cache_v'].rearrange("n l (r j) h d -> (n l r) (j h d)", r=RT)
            cf = I['cache_logf'].rearrange("n l (r j) h -> (n l r) (j h)", r=RT)
            for bt in range(DEC_BATCH * DT):
                gather(lf_past[:, bt, :], cf, bt, lf_in)

            def gather_k(b, t):
                if b * DT + t >= NSLOT:
                    pool.wait_ge(D['k_tr'], D0['k_tr'] + 2 * (b * DT + t - NSLOT) + 2)
                gather(k_slot[:, t % NSLOT, :], ck, b * DT + t, k_in[t % NSLOT])

            def gather_v(b, t):
                if b * DT + t >= NSLOT:
                    pool.wait_ge(D['pv_mm'], D0['pv_mm'] + b * DT + t - NSLOT + 1)
                gather(v_slot[:, t % NSLOT, :], cv, b * DT + t, v_in[t % NSLOT])

            for t in range(NSLOT):
                gather_k(0, t)
            pool.wait_ge(mixa_stored, 32 + 32)
            pool.wait_ge(wkv_stored, 48)
            g.memset(later[:, :], 1.0).then_inc(made, 1)
            g.memset(ones_a[:, :], 1.0).then_inc(made, 1)
            g.memset(nmask[:, :, :], 0.0).then_inc(made, 1)
            g.memset(qbd[:, :, :, :], 0.0).then_inc(made, 1)
            g.memset(v_new[:, :], 0.0).then_inc(made, 1)
            g.memset(bias_w[:, :, :], 0.0).then_inc(made, 1)
            g.memset(nm_cur[:, :], 0.0).then_inc(made, 1)
            g.memset(p_new[:, :], 0.0).then_inc(made, 1)
            pool.wait_ge(made, DCONST + 8)
            g.memset(nm_cur[0:SMP, 64:P], -1e30).then_inc(made, 1)
            g.affine_select(out=later[:, :], in_=later[:, :], compare_op=ALU.is_ge, fill=0.0, base=-1,
                            pattern=[[-1, P]], channel_multiplier=1).then_inc(made, 1)
            nm = nmask[:, :, :].rearrange("p b (h q) -> p b h q", h=4)
            g.affine_select(out=nm, in_=nm, compare_op=ALU.is_ge, fill=-1e30, base=0,
                            pattern=[[-DEC_SEQ, DEC_BATCH], [0, 4], [0, DEC_SEQ]], channel_multiplier=1).then_inc(made, 1)
            pool.wait_ge(made, DCONST + 11)
            g.affine_select(out=nm, in_=nm, compare_op=ALU.is_ge, fill=-1e30, base=0,
                            pattern=[[DEC_SEQ, DEC_BATCH], [0, 4], [1, DEC_SEQ]], channel_multiplier=-1).then_inc(made, 1)
            for t in range(NSLOT, DT):
                gather_k(0, t)
            for b in range(1, DEC_BATCH + 1):
                for t in range(DT if b < DEC_BATCH else 0):
                    gather_k(b, t)
                for t in range(DT):
                    gather_v(b - 1, t)

        @block.tensor
        def _(pe):
            def transpose(out, in_):
                k = in_.shape[0]
                return nc.tensor.transpose(out, in_, ident[0:k, 0:k])

            pe.wait_ge(made, IDENT + 2)
            pe.wait_ge(rows_in, 16 * (len(ROWS256) + 7))
            for t in range(2):
                cs = slice(t * P, (t + 1) * P)
                transpose(psum[:, 5, t * NROW:(t + 1) * NROW], rows256[:, cs])
                transpose(psum[:, 5, 160 + t * 120:280 + t * 120], st_rows[:, 0, cs])
                for hf in range(2):
                    transpose(psum[:, 6, t * 240 + hf * 120:t * 240 + hf * 120 + 120], st_rows[:, 1 + hf, cs])
            transpose(psum[:, 5, 84:99], rows128[:, :])
            for t in range(7):
                last = transpose(psum[:, 5, 100 + 8 * t:108 + 8 * t], sh_rows[:, t * P:(t + 1) * P])
            last.then_inc(par_tr, 1)

            def h_tile(u, rows):
                for k in range(KT):
                    last = transpose(psum[:, 2 * u + k // 4, (k % 4) * P:(k % 4) * P + rows],
                                     xh[0:rows, u, k * P:(k + 1) * P])
                last.then_inc(h_tr, 1)

            for u in range(2):
                pe.wait_ge(h_ready, u + 1)
                h_tile(u, P)
            with pe.Fori(1, TT // 2) as i:
                for u in range(2):
                    pe.wait_ge(h_ready, i * 2 + (u + 1))
                    pe.wait_ge(hT_ready, i * 2 + (u - 1))
                    h_tile(u, P)
            pe.wait_ge(h_ready, TT + 1)
            pe.wait_ge(hT_ready, TT - 1)
            h_tile(0, SMP)
            pe.wait_ge(hT_ready, TT + 1)

            def pair(p):
                for u in range(2):
                    pe.wait_ge(w_in[u], p * 16 + 16)
                    for c in range(CHUNKS):
                        if not (isinstance(p, int) and p == 0 and u == 0):
                            pe.wait_ge(z_evac, p * 10 + (5 * u + c - 4))
                        for k in range(KT):
                            last = nc.tensor.matmul(psum[:, c, 0:CW], wbuf[:, u, k, :],
                                                    hT[:, k, c * CW:(c + 1) * CW], start=(k == 0), stop=(k == KT - 1))
                        last.then_inc(z_mm, 1)

            small = [0]

            def small_group(mms, w=CW):
                g = small[0]
                if g >= 3:
                    pe.wait_ge(small_read, reads_through(g - 3))
                elif g == 0:
                    pe.wait_ge(par_ready, 5)
                for n, (l, r) in enumerate(mms):
                    last = nc.tensor.matmul(psum[:, 5 + g % 3, 0:w], l, r, start=(n == 0), stop=(n == len(mms) - 1))
                last.then_inc(small_mm, 1)
                small[0] += 1

            def pool_post():
                pe.wait_ge(made, ONES + 6)
                pe.wait_ge(consts_in, 16 * 7)
                pe.wait_ge(pooled_ready, 2)
                for t in range(2):
                    for c in range(CHUNKS):
                        small_group([(pw_diag[:, t, :], pooled[:, t, c * CW:(c + 1) * CW])])

            def conv_post():
                pe.wait_ge(conv_done, CONV_WIDTH * 4)
                for c in range(CHUNKS):
                    small_group([(ones_ln[:, :], conv[:, t, c * CW:(c + 1) * CW]) for t in range(2)])
                for c in range(CHUNKS):
                    pe.wait_ge(d_sq, 2 * c + 2)
                    small_group([(ones_ln[:, :], ln_sq[:, t, c * CW:(c + 1) * CW]) for t in range(2)])
                for c in range(CHUNKS):
                    pe.wait_ge(d_act, 2 * c + 2)
                    for o in range(2):
                        small_group([(pwo[:, t, o * P:(o + 1) * P], ln_sq[:, t, c * CW:(c + 1) * CW]) for t in range(2)])

            def key_norms():
                pe.wait_ge(ksq_ready, 4)
                for t in range(2):
                    for c in range(CHUNKS):
                        small_group([(ones_head[:, :], ksq[:, t, c * CW:(c + 1) * CW])])

            def loras():
                pe.wait_ge(wa_ready, 4)
                pe.wait_ge(small_read, reads_through(39))
                n = 0
                for m in range(2):
                    for t in range(2):
                        for c in range(CHUNKS):
                            if n >= 3:
                                pe.wait_ge(lora_read, n - 2)
                            nc.tensor.matmul(psum[:, 5 + n % 3, 0:CW], lora[:, m, t * P:(t + 1) * P],
                                             wa[:, c * CW:(c + 1) * CW], start=True, stop=True).then_inc(lora_mm, 1)
                            n += 1

            pair(0)
            with pe.Fori(1, 5) as p:
                pair(p)
            with pe.Fori(5, 7) as p:
                pair(p)
            pool_post()
            with pe.Fori(7, 9) as p:
                pair(p)
            pair(9)
            conv_post()
            key_norms()
            loras()
            with pe.Fori(10, 13) as p:
                pair(p)
            pair(13)

            pe.wait_ge(z_evac, 10 * 14)

            def kv_tile(u, n):
                for m in range(4):
                    last = transpose(psum[0:n, u, m * P:(m + 1) * P], kvt[:, u, m, 0:n])
                return last

            for u in range(2):
                pe.wait_ge(kvt_in[u], 16)
                kv_tile(u, P).then_inc(kv_tr, 1)
            with pe.Fori(1, TT // 2) as i:
                for u in range(2):
                    pe.wait_ge(kvt_in[u], i * 16 + 16)
                    pe.wait_ge(kv_copied, i * 2 + (u - 1))
                    kv_tile(u, P).then_inc(kv_tr, 1)
            pe.wait_ge(kvt_in[0], 16 * (TT // 2 + 1))
            pe.wait_ge(kv_copied, TT - 1)
            kv_tile(0, SMP).then_inc(kvs_tr, 1)
            pe.wait_ge(nl_ready, 2)
            for n in range(TT):
                transpose(psum[:, 2, 4 * n:4 * n + 4], fa[:, n * P:(n + 1) * P])
            pe.wait_ge(nc_ready, 1)
            transpose(psum[0:SMP, 2, 64:68], fa[:, SEQ:T_ALL])
            transpose(psum[0:SMP, 2, 68:72], nc_[:, SEQ:T_ALL]).then_inc(f_tr, 1)

            pe.wait_ge(f_copied, 2)
            pe.wait_ge(kvs_copied, 1)
            pe.wait_ge(kv_copied, TT)
            pe.wait_ge(v_kept, TT)
            pe.wait_ge(a_in, 16 * 8)
            pe.wait_ge(kr_in, 64)
            pe.wait_ge(made, MASKS + 4)
            pe.wait_ge(qones_ready, 1)

            def scores(i, g, j):
                w, u, h = j % 2, j // 4, j % 4
                if h == 0:
                    pe.wait_ge(q_in[u], i * 16 + 16)
                for c in range(g + 1):
                    nc.tensor.matmul(psum[:, 4 * w + c, :], qaug[0:65, u, h, :], kaug[0:65, h, c * 512:(c + 1) * 512],
                                     start=True, stop=(c < g))
                x = i * (-2 * P) + (4 * g * P + (3 - u) * P)
                nc.tensor.matmul(psum[:, 4 * w + g, :], identb[:, :], maskb[:, bass.ds(x, 512)],
                                 start=False, stop=True).then_inc(s_mm, 1)

            def values(i, g, j):
                w, h = j % 2, j % 4
                pe.wait_ge(p_ready, i * 8 + (j + 1))
                for k in range(4 * (g + 1)):
                    last = transpose(psum[:, 4 * w + k // 4, (k % 4) * P:(k % 4 + 1) * P], probs[:, w, k * P:(k + 1) * P])
                last.then_inc(p_tr, 1)
                pe.wait_ge(pT_ready, i * 8 + (j + 1))
                for k in range(4 * (g + 1)):
                    last = nc.tensor.matmul(psum[w * 64:w * 64 + 64, 4 * w, 0:P], vtok[:, k, h * 64:(h + 1) * 64],
                                            probsT[:, k * P:(k + 1) * P], start=(k == 0), stop=(k == 4 * g + 3))
                last.then_inc(o_mm, 1)
                if w == 1:
                    pe.wait_ge(lb_ready, i * 4 + (j // 2 + 1))
                    transpose(psum[:, 7, 0:P], lbc[:, :]).then_inc(lb_tr, 1)

            def attention(i, g, first):
                for j in range(8):
                    if not (first and j < 2):
                        pe.wait_ge(o_copied, i * 8 + (j - 1))
                        if j % 2 == 1:
                            pe.wait_ge(lg_ready, i * 4 + (j // 2))
                    scores(i, g, j)
                    if j > 0:
                        values(i, g, j - 1)
                values(i, g, 7)

            attention(0, 0, True)
            attention(1, 0, False)
            for g in range(1, 4):
                with pe.Fori(2 * g, 2 * g + 2) as i:
                    attention(i, g, False)

            pe.wait_ge(o_copied, 64)
            pe.wait_ge(lg_ready, 32)
            pe.wait_ge(made, RMASKS + 11)

            def rwkv_tile(i, u, first):
                def at(n, k=1, per=1, back=False):
                    if back and first:
                        return
                    pe.wait_ge(R[n], i * (2 * per) + (u * per + k - (per if back else 0)))

                def mm(out, l, r, start=True, stop=True):
                    return nc.tensor.matmul(out, l, r, start=start, stop=stop, skip_group_check=True)

                hs = [slice((h % 2) * 64, (h % 2) * 64 + 64) for h in range(4)]
                hc = [slice(h * 64, h * 64 + 64) for h in range(4)]
                pe.wait_ge(r_in[u], i * 32 + 32)
                both = [rin[hs[h], u, h // 2:h // 2 + 3:2, :] for h in range(4)]
                at('sqT', 5, 5, back=True)
                at('sq', 4, 4, back=True)
                for h in range(4):
                    last = mm(psum[:, 2 + h % 2, (h // 2) * 256:(h // 2) * 256 + 256].rearrange("p (a c) -> p a c", a=2), rin[hs[h], u, BTI + h // 2, :], both[h])
                last.then_inc(R['gram_b'], 1)
                at('app', 6, 6, back=True)
                at('q', back=True)
                for h in range(4):
                    last = mm(psum[:, 4 + h % 2, (h // 2) * 256:(h // 2) * 256 + 256].rearrange("p (a c) -> p a c", a=2), rin[hs[h], u, KTI + h // 2, :], both[h])
                last.then_inc(R['gram_k'], 1)
                at('tr', 2, 2, back=True)
                at('st', 4, 4, back=True)
                for h in range(4):
                    last = mm(psum[:, 6 + h % 2, (h // 2) * P:(h // 2 + 1) * P], rin[hs[h], u, ALP + h // 2, :], rin[hs[h], u, BTI + h // 2, :])
                last.then_inc(R['gram_m'], 1)
                at('o', back=True)
                for m in range(8):
                    last = transpose(psum[:, m // 4, (m % 4) * P:(m % 4 + 1) * P], rin[:, u, 2 + m, :])
                last.then_inc(R['tok_tr'], 1)
                at('gk')
                at('tok', 6, 6)
                for h in range(4):
                    last = mm(psum[:, 1, hc[h]], gk[:, h, 1, :], tok_v[:, hc[h]])
                last.then_inc(R['kv_mm'], 1)
                at('gb')
                at('gm')
                for l in range(6):
                    mt = (lambda h: gb[:, h, 1, :]) if l == 0 else (lambda h: mpowT[:, l % 2, h, :])
                    m_ = (lambda h: mpow[:, 2, h, :]) if l == 0 else (lambda h: mpow[:, l % 2, h, :])
                    if l > 0:
                        at('sqT', l, 5)
                        if l < 5:
                            at('sq', l, 4)
                    if l < 5:
                        for h in range(4):
                            last = mm(psum[:, 2, h * P:(h + 1) * P], m_(h), mt(h))
                        last.then_inc(R['sqT_mm'], 1)
                    if l < 4:
                        for h in range(4):
                            last = mm(psum[:, 3, h * P:(h + 1) * P], mt(h), m_(h))
                        last.then_inc(R['sq_mm'], 1)
                    if l == 0:
                        at('kv')
                    else:
                        at('app', l, 6)
                    for h in range(4):
                        last = mm(psum[:, 4, h * P:(h + 1) * P], mt(h), sol[:, h, :])
                    last.then_inc(R['app_mm'], 1)
                at('app', 6, 6)
                for h in range(4):
                    last = mm(psum[hs[h], 5, (h // 2) * P:(h // 2 + 1) * P], sol[:, h, 0:64], gb[:, h, 0, :])
                last.then_inc(R['q_mm'], 1)
                for h in range(4):
                    for c in range(2):
                        x = (h // 2) * P + c * 64
                        last = mm(psum[hs[h], 6, x:x + 64], sol[:, h, 0:64], tok_b[:, c, hc[h]])
                last.then_inc(R['tr_mm'], 1)
                at('tr', 2, 2)
                at('pcur')
                for c in range(2):
                    if c == 1:
                        at('st', 2, 4)
                    elif first:
                        pe.wait_ge(state_zero, 4)
                    else:
                        at('st', 4, 4, back=True)
                    for t in range(2):
                        out = psum[:, 7, (c * 2 + t) * P:(c * 2 + t + 1) * P]
                        for h in (2 * t, 2 * t + 1):
                            mm(out[hs[h], hs[h]], tok_k[:, c, hc[h]], tok_v[:, hc[h]], True, False)
                            mm(out[hs[h], hs[h]], tok_b[:, c, hc[h]], sol[:, h, 64:P], False, False)
                        last = mm(out, trans[:, 2 * t + c, :], state[:, u * 4 + c * 2 + t, :], False, True)
                    last.then_inc(R['st_mm'], 1)
                at('q')
                for t in range(2):
                    p0 = t * P
                    for h in (2 * t, 2 * t + 1):
                        mm(psum[hs[h], 0, p0:p0 + P], tok_v[:, hc[h]], gk[:, h, 0, :], True, False)
                        mm(psum[hs[h], 0, p0:p0 + P], sol[:, h, 64:P], gb[:, h, 0, :], False, False)
                    for c in range(2):
                        last = mm(psum[:, 0, p0 + c * 64:p0 + c * 64 + 64], state[:, u * 4 + c * 2 + t, :],
                                  qT_r[:, t, c * 64:c * 64 + 64], False, True)
                last.then_inc(R['o_mm'], 1)

            rwkv_tile(0, 0, True)
            rwkv_tile(0, 1, False)
            with pe.Fori(1, TT // 2) as i:
                rwkv_tile(i, 0, False)
                rwkv_tile(i, 1, False)
            pe.wait_ge(R['st'], 4 * TT)
            pe.wait_ge(R['sqT'], 5 * TT)
            for t in range(2):
                last = transpose(psum[:, 2, t * P:(t + 1) * P], state[:, t, :])
            last.then_inc(wkv_tr, 1)
            pe.wait_ge(R['o'], TT)
            pe.wait_ge(wkv_copied, 2)
            for i in range(DEC_SEQ):
                for n in range(5):
                    pe.wait_ge(s_z, i * 5 + n + 1)
                    if i * 5 + n >= 4:
                        pe.wait_ge(s_used, i * 5 + n - 3)
                    for hf in range(2):
                        last = nc.tensor.matmul(psum[:, 2 * ((i * 5 + n) % 4) + hf, :], ones_head[:, :],
                                                z_exp[:, n, hf * 512:(hf + 1) * 512], start=True, stop=True)
                    last.then_inc(s_mm2, 1)
            pe.wait_ge(s_done, 1)
            pe.wait_ge(gn_in, 16 * 6)
            g = 0
            for k, src in enumerate((o_rw, gn_sq, g_rkk)):
                for t in range(2):
                    for c in range(CHUNKS):
                        if g >= 8:
                            pe.wait_ge(gn_read, g - 7)
                        if k == 1:
                            pe.wait_ge(gn_sq_ready, g - 9)
                        nc.tensor.matmul(psum[:, g % 8, 0:CW], ones_head[:, :], src[:, t, c * CW:(c + 1) * CW],
                                         start=True, stop=True).then_inc(gn_mm, 1)
                        g += 1

            pe.wait_ge(gn_read, 30)
            pe.wait_ge(made, DCONST + 12)
            pe.wait_ge(tot_ready, 1)
            nc.tensor.matmul(psum[:, 5, 0:256], later[:, :], tot[:, :], start=True, stop=True)
            nc.tensor.matmul(psum[:, 6, 0:256], ones_a[:, :], tot[:, :], start=True, stop=True).then_inc(D['suf_mm'], 1)
            pe.wait_ge(bias_ready, 4)

            def add_bias(t):
                for j in range(4):
                    last = nc.tensor.matmul(psum[:, 4 + t % 2, j * P:(j + 1) * P], bias_w[:, t * 4 + j, :], ident[:, :],
                                            start=False, stop=True, skip_group_check=True)
                last.then_inc(D['b_mm'], 1)

            def keys(b, first):
                for t in range(DT):
                    pe.wait_ge(k_in[t % NSLOT], b * 32 + (16 * (t // NSLOT) + 16))
                    for hf in range(2):
                        if not (first and t == 0):
                            pe.wait_ge(D[f'kT{hf}'], D0[f'kT{hf}'] + b * 8 + t)
                        for pr in range(2):
                            for j in range(4):
                                last = transpose(psum[:, 2 * hf + pr, j * P:(j + 1) * P],
                                                 k_slot[:, t % NSLOT, (hf * 4 + j) * 256 + pr * P:(hf * 4 + j) * 256 + (pr + 1) * P])
                        last.then_inc(D['k_tr'], 1)
                    if t == 0:
                        pe.wait_ge(D['prep'], D0['prep'] + b + 1)
                    if t < 2 and not first:
                        pe.wait_ge(D['pT'], D0['pT'] + b * 9)
                    if t >= 2:
                        pe.wait_ge(D['s'], D0['s'] + b * 9 + (t - 1))
                    if t > 0:
                        add_bias(t - 1)
                    for hf in range(2):
                        pe.wait_ge(D[f'kT{hf}'], D0[f'kT{hf}'] + b * 8 + (t + 1))
                        for pr in range(2):
                            g = 32 * (2 * hf + pr)
                            last = nc.tensor.matmul(psum[g:g + 8, 4 + t % 2, :], q_cur[:, pr, :], kT_d[:, hf, pr, :],
                                                    start=True, stop=False, tile_position=(0, g), skip_group_check=True)
                    last.then_inc(D['sc_mm'], 1)
                add_bias(DT - 1)
                if not first:
                    pe.wait_ge(D['neg_m'], D0['neg_m'] + b)
                nc.tensor.matmul(psum[:, 6, 0:SMP], nm_cur[:, :], ident[:, 0:SMP], start=True, stop=False, skip_group_check=True)
                for pr in range(2):
                    last = nc.tensor.matmul(psum[32 * pr:32 * pr + 8, 6, 0:SMP], q_cur[:, pr, :], kT_s[:, pr, :],
                                            start=False, stop=True, tile_position=(0, 32 * pr), skip_group_check=True)
                last.then_inc(D['new_mm'], 1)
                pe.wait_ge(D['m1'], D0['m1'] + b + 1)
                transpose(psum[0:1, 6, P:2 * P], m1[:, :]).then_inc(D['m_tr'], 1)
                pe.wait_ge(D['m_row'], D0['m_row'] + b + 1)
                nc.tensor.matmul(psum[:, 6, 256:257], m_row[:, :], ones_a[0:1, 0:1], start=True, stop=True).then_inc(D['m_mm'], 1)

            def values_of(b, first):
                pe.wait_ge(D['pT'], D0['pT'] + b * 9 + 9)
                if not first:
                    pe.wait_ge(D['pv'], D0['pv'] + b)
                for t in range(DT):
                    pe.wait_ge(v_in[t % NSLOT], b * 32 + (16 * (t // NSLOT) + 16))
                    for j in range(TJ):
                        g, n = j % 4, t * TJ + j
                        last = nc.tensor.matmul(psum[32 * g:32 * g + 16, 7, 0:256],
                                                pT_d[:, t * 4 + j % 4, 2 * (j // 4):2 * (j // 4) + 2, :].rearrange("p g x -> p (g x)"),
                                                v_slot[:, t % NSLOT, j * 256:(j + 1) * 256], start=(n < 4),
                                                stop=(n >= DT * TJ - 4 and g > 0), tile_position=(0, 32 * g), skip_group_check=True)
                    if t == DT - 1:
                        last = nc.tensor.matmul(psum[0:16, 7, 0:256], p_new[:, :], v_new[:, :], start=False, stop=True,
                                                tile_position=(0, 0), skip_group_check=True)
                    last.then_inc(D['pv_mm'], 1)
                pe.wait_ge(D['l_all'], D0['l_all'] + b + 1)
                if not first:
                    pe.wait_ge(D['o'], D0['o'] + b * 4)
                pe.wait_ge(D['pv'], D0['pv'] + b + 1)
                nc.tensor.matmul(psum[:, 7, 256:272], l_all[:, :], sel_r[:, :, :].rearrange("p a x -> p (a x)"), start=True, stop=True)
                for pr in range(2):
                    last = nc.tensor.matmul(psum[:, 7, 288 + pr * 16:304 + pr * 16], pv[:, pr * P:(pr + 1) * P], sel[:, :], start=True, stop=True)
                last.then_inc(D['o_mm'], 1)

            def turn_probs(b):
                pe.wait_ge(D['p'], D0['p'] + b + 1)
                for c in range(DT + 1):
                    if c >= 2:
                        pe.wait_ge(D['pT'], D0['pT'] + b * 9 + (c - 1))
                    if c < DT:
                        for j in range(4):
                            last = transpose(psum[:, 4 + c % 2, j * P:(j + 1) * P], s_rows[:, (c * 4 + j) * P:(c * 4 + j + 1) * P])
                    else:
                        last = transpose(psum[0:SMP, 4 + c % 2, 0:P], s_rows[:, DT * 512:DT * 512 + SMP])
                    last.then_inc(D['p_tr'], 1)

            keys(0, True)
            turn_probs(0)
            keys(1, False)
            values_of(0, True)
            turn_probs(1)
            with pe.Fori(2, DEC_BATCH) as b:
                keys(b, False)
                values_of(b - 1, False)
                turn_probs(b)
            values_of(DEC_BATCH - 1, False)

            def project(u, n=P):
                for o in range(2):
                    for e in range(8):
                        last = nc.tensor.matmul(psum[0:n, 2 * u + o, :], mt[:, u, e, 0:n], wo[:, e, o * 512:(o + 1) * 512],
                                                start=(e == 0), stop=(e == 7))
                last.then_inc(D['y_mm'], 1)

            pe.wait_ge(rows_in, 16 * (len(ROWS256) + 7 + PT) + 32)
            for u in range(2):
                pe.wait_ge(q_in[u], 16 * (TT // 2) + 16)
                project(u)
            with pe.Fori(1, TT // 2) as i:
                for u in range(2):
                    pe.wait_ge(q_in[u], 16 * (TT // 2) + i * 16 + 16)
                    pe.wait_ge(D['y_sum'], D0['y_sum'] + i * 2 + (u - 1))
                    project(u)
            pe.wait_ge(q_in[0], 16 * (TT // 2) + 16 * (TT // 2 + 1))
            pe.wait_ge(D['y_sum'], D0['y_sum'] + TT - 1)
            project(0, SMP)

        @block.scalar
        def _(act):
            def square(u, rows):
                nc.scalar.activation(zst[0:rows, u, 0:D_MODEL], xt[0:rows, u, :], ACT.Square, scale=D_MODEL ** -0.5,
                                     accum_out=ss[0:rows, u:u + 1]).then_inc(sq_done, 1)

            def root(u, rows):
                nc.scalar.activation(rstd[0:rows, u:u + 1], ss[0:rows, u:u + 1], ACT.Sqrt).then_inc(rstd_ready, 1)

            for u in range(2):
                act.wait_ge(x_in[u], 16)
                square(u, P)
            for u in range(2):
                act.wait_ge(inv_ready, u + 1)
                root(u, P)
            with act.Fori(1, TT // 2) as i:
                for u in range(2):
                    act.wait_ge(x_in[u], i * 16 + 16)
                    act.wait_ge(h_ready, i * 2 + (u - 1))
                    square(u, P)
                for u in range(2):
                    act.wait_ge(inv_ready, i * 2 + (u + 1))
                    root(u, P)
            act.wait_ge(x_in[0], 16 * (TT // 2 + 1))
            square(0, SMP)
            act.wait_ge(inv_ready, TT + 1)
            root(0, SMP)

            def pair(p):
                for u in range(2):
                    if not (isinstance(p, int) and p == 0):
                        act.wait_ge(z_stored[u], p * 16)
                    for c in range(CHUNKS):
                        act.wait_ge(z_mm, p * 10 + (5 * u + c + 1))
                        nc.scalar.copy(zst[:, u, c * CW:(c + 1) * CW], psum[:, c, 0:CW]).then_inc(z_evac, 1)
                    act.wait_ge(z_evac, p * 10 + (5 * u + 5))
                    act.dma_start(zT[bass.ds(p * 2 + u, 1)].rearrange("o p t -> p (o t)"), zst[:, u, :]).then_inc(z_stored[u], 16)

            def a_(out, in_, f, s, **kw):
                nc.scalar.activation(out, in_, f, **kw).then_inc(s, 1)

            def mix_acts():
                act.wait_ge(small_read, reads_through(9))
                for n in (2, 3):
                    act.wait_ge(sh_done, n + 1)
                    a_(ksq[:, n - 2, 0:SEQ], sh_mix[:, n % 2, 0:SEQ], ACT.Square, ksq_ready, scale=par[:, n - 2, PKK:PKK + 1])
                    a_(samples(ksq[:, n - 2]), shifted_samples(sh_mix[:, n % 2]), ACT.Square, ksq_ready, scale=par[:, n - 2, PKK:PKK + 1])
                act.wait_ge(sh_done, 7)
                for (rows, f) in ((slice(0, 64), ACT.Tanh), (slice(64, P), ACT.Copy)):
                    a_(wa[rows, 0:SEQ], sh_mix[rows, 0, 0:SEQ], f, wa_ready)
                    a_(samples(wa[rows]), shifted_samples(sh_mix[rows, 0]), f, wa_ready)

            act.wait_ge(sq_done, TT + 1)
            pair(0)
            with act.Fori(1, 5) as p:
                pair(p)
            act.wait_ge(d_in, 16 * 6)
            for t in range(2):
                a_(u2d[:, t, :], u2d[:, t, :], ACT.Sigmoid, d_sig)
            with act.Fori(5, 7) as p:
                pair(p)
            act.wait_ge(gc_in, 32)
            for t in range(2):
                a_(gate_c[:, t, :], gate_c[:, t, :], ACT.Silu, gates)
            with act.Fori(7, 9) as p:
                pair(p)
            pair(9)
            act.wait_ge(gd_in, 32)
            for t in range(2):
                a_(gate_d[:, t, :], gate_d[:, t, :], ACT.Silu, gates)
            mix_acts()
            for c in range(CHUNKS):
                cs = slice(c * CW, (c + 1) * CW)
                for t in range(2):
                    act.wait_ge(small_read, reads_through(9) + 2 * c + t + 1)
                    a_(ln_sq[:, t, cs], conv[:, t, cs], ACT.Square, d_sq)
            for c in range(CHUNKS):
                cs = slice(c * CW, (c + 1) * CW)
                act.wait_ge(d_inv, c + 1)
                a_(ln_inv[:, cs], ln_inv[:, cs], ACT.Sqrt, d_root)
            for c in range(CHUNKS):
                cs = slice(c * CW, (c + 1) * CW)
                for t in range(2):
                    act.wait_ge(d_norm, 2 * c + t + 1)
                    a_(ln_sq[:, t, cs], conv[:, t, cs], ACT.Silu, d_act, scale=par[:, t, PLG:PLG + 1], bias=par[:, t, PLB:PLB + 1])
            for t in range(2):
                for c in range(CHUNKS):
                    cs = slice(c * CW, (c + 1) * CW)
                    act.wait_ge(kinv_pre, t * CHUNKS + c + 1)
                    a_(kinv[:, t, cs], kinv[:, t, cs], ACT.Sqrt, kinv_ready)
            n = 0
            act.wait_ge(small_read, reads_through(29))
            for dst, b in ((sig_w, PW0), (rate, PA0)):
                for t in range(2):
                    for c in range(CHUNKS):
                        act.wait_ge(lora_mm, n + 1)
                        a_(dst[:, t, c * CW:(c + 1) * CW], psum[:, 5 + n % 3, 0:CW], ACT.Sigmoid, lora_read, bias=par[:, t, b:b + 1])
                        n += 1
            n = 0
            for t in range(2):
                pair(10 + t)
                for src, sc in ((rw_t, 1.0), (rw_L, 1.0), (rw_L, -1.0)):
                    act.wait_ge(L_ready, n + 1)
                    a_(rw_t[:, 0:SEQ], src[:, 0:SEQ], ACT.Exp, exp_ready, scale=sc)
                    n += 1
            pair(12)
            pair(13)
            act.wait_ge(ga_in, 32)
            for t in range(2):
                a_(gate_a[:, t, :], gate_a[:, t, :], ACT.Silu, gates)
            act.wait_ge(gates, GATE_A + 2)
            a_(gate_s[:, :, :], gate_a[:, :, SEQ:T_ALL], ACT.Copy, gates)
            act.wait_ge(f_pre, 1)
            a_(fa, fx, ACT.Abs, f_abs)
            act.wait_ge(f_abs, 1)
            a_(fa, fa, ACT.Exp, f_abs, scale=-1.0)
            act.wait_ge(f_abs, 2)
            a_(fa, fa, ACT.Ln, f_abs, bias=1.0)
            for u in range(2):
                act.wait_ge(kv_copied, u + 1)
                nc.scalar.copy(vtok[:, u, :], kvs[:, u, 256:512]).then_inc(v_kept, 1)
            with act.Fori(1, TT // 2) as i:
                for u in range(2):
                    act.wait_ge(kv_copied, i * 2 + (u + 1))
                    nc.scalar.copy(vtok[:, bass.ds(i * 2 + u, 1), :].rearrange("p o c -> p (o c)"), kvs[:, u, 256:512]).then_inc(v_kept, 1)

            def soft(i, g, j):
                w = j % 2
                act.wait_ge(s_max, i * 8 + (j + 1))
                if not (isinstance(i, int) and i == 0 and j < 2):
                    act.wait_ge(lb_ready, i * 4 + (j // 2))
                nc.scalar.activation(probs[:, w, 0:512 * (g + 1)], psum[:, 4 * w:4 * w + g + 1, :].rearrange("p b c -> p (b c)"), ACT.Exp,
                                     bias=nb[:, w:w + 1], scale=0.125, accum_out=lsum[:, w:w + 1]).then_inc(p_ready, 1)

            def transposed(i, g, j):
                w = j % 2
                act.wait_ge(p_tr, i * 8 + (j + 1))
                nc.scalar.copy(probsT[:, 0:512 * (g + 1)], psum[:, 4 * w:4 * w + g + 1, :].rearrange("p b c -> p (b c)")).then_inc(pT_ready, 1)

            def attention(i, g):
                for j in range(8):
                    if j > 0:
                        transposed(i, g, j - 1)
                    soft(i, g, j)
                transposed(i, g, 7)

            attention(0, 0)
            attention(1, 0)
            for g in range(1, 4):
                with act.Fori(2 * g, 2 * g + 2) as i:
                    attention(i, g)

            def rwkv_tile(i, u, first):
                def at(n, k=1, per=1, back=False):
                    if back and first:
                        return
                    act.wait_ge(R[n], i * (2 * per) + (u * per + k - (per if back else 0)))

                at('tok_tr')
                at('o_mm', back=True)
                n = 0
                act_src = psum[:, 0:2, :].rearrange("p a b -> p (a b)")
                if first:
                    act.wait_ge(state_zero, 4)
                for dst, m, sc in ((sol[:, :, 0:64], 0, 1.0), (tok_k, 1, 1.0), (tok_b, 2, -1.0), (tok_v[:, :], 3, 1.0)):
                    src = act_src[:, m * 256:(m + 1) * 256]
                    if m == 0:
                        src = src.rearrange("p (h c) -> p h c", h=4)
                    if m in (1, 2):
                        for c in range(2):
                            cs = slice(c * 64, c * 64 + 64)
                            nc.scalar.activation(dst[cs, c, :], src[cs, :], ACT.Copy, scale=sc).then_inc(R['tok'], 1)
                    else:
                        nc.scalar.activation(dst, src, ACT.Copy, scale=sc).then_inc(R['tok'], 1)
                for l in range(4):
                    at('sq_mm', l + 1, 4)
                    nc.scalar.copy(mpow[:, (l + 1) % 2, :, :], psum[:, 3, :].rearrange("p (h c) -> p h c", h=4)).then_inc(R['sq'], 1)
                at('o_mm')
                nc.scalar.copy(o_rw[:, :, bass.ds(i * (2 * P) + u * P, P)], psum[:, 0, 0:256].rearrange("p (t c) -> p t c", t=2)).then_inc(R['o'], 1)

            act.wait_ge(mixa_stored, 32)
            rwkv_tile(0, 0, True)
            rwkv_tile(0, 1, False)
            with act.Fori(1, TT // 2) as i:
                rwkv_tile(i, 0, False)
                rwkv_tile(i, 1, False)
            a_(smp[:, 1], smp[:, 1], ACT.Exp, s_dec)
            act.wait_ge(gn_in, 16 * 6)
            for t in range(2):
                a_(gate_b[:, t, :], gate_b[:, t, :], ACT.Silu, gates)
            n = 0
            for t in range(2):
                for c in range(CHUNKS):
                    cs = slice(c * CW, (c + 1) * CW)
                    act.wait_ge(gn_read, n + 1)
                    a_(gn_sq[:, t, cs], o_rw[:, t, cs], ACT.Square, gn_sq_ready)
                    n += 1
            n = 0
            for t in range(2):
                for c in range(CHUNKS):
                    cs = slice(c * CW, (c + 1) * CW)
                    act.wait_ge(gn_pre, n + 1)
                    a_(gn_inv[:, t, cs], gn_inv[:, t, cs], ACT.Sqrt, gn_root)
                    n += 1

            def keep_scores(b, t):
                act.wait_ge(D['b_mm'], D0['b_mm'] + b * 8 + (t + 1))
                nc.scalar.copy(s_rows[:, t * 512:(t + 1) * 512], psum[:, 4 + t % 2, :]).then_inc(D['s'], 1)

            def keys(b, first):
                for t in range(DT):
                    act.wait_ge(D['k_tr'], D0['k_tr'] + b * 16 + (2 * t + 2))
                    if not (first and t == 0):
                        act.wait_ge(D['sc_mm'], D0['sc_mm'] + b * 8 + t)
                    nc.scalar.copy(kT_d[:, 1, :, :].rearrange("p r c -> p (r c)"),
                                   psum[:, 2:4, :].rearrange("p a c -> p (a c)")).then_inc(D['kT1'], 1)
                    if t > 0:
                        keep_scores(b, t - 1)
                keep_scores(b, DT - 1)
                act.wait_ge(D['new_mm'], D0['new_mm'] + b + 1)
                nc.scalar.copy(s_rows[:, DT * 512:DT * 512 + SMP], psum[:, 6, 0:SMP]).then_inc(D['s'], 1)
                act.wait_ge(D['neg_m'], D0['neg_m'] + b + 1)
                if not first:
                    act.wait_ge(D['l_all'], D0['l_all'] + b)
                nc.scalar.activation(s_rows[:, :], s_rows[:, :], ACT.Exp, bias=neg_m[:, :], accum_out=l_row[:, :]).then_inc(D['p'], 1)

            act.wait_ge(mixb_ready, 1)
            keys(0, True)
            with act.Fori(1, DEC_BATCH) as b:
                keys(b, False)

            def norm(i, u, n=P):
                act.wait_ge(D['y_sum'], D0['y_sum'] + i * 2 + (u + 1))
                if not (isinstance(i, int) and i == 0):
                    act.wait_ge(kv_stored[u], 32 * (TT // 2) + i * 16)
                nc.scalar.activation(yb[0:n, u, :], zst[0:n, u, 0:D_MODEL], ACT.Square, scale=D_MODEL ** -0.5,
                                     accum_out=ss[0:n, u:u + 1]).then_inc(sq_done, 1)
                act.wait_ge(inv_ready, (TT + 1) + i * 2 + (u + 1))
                nc.scalar.activation(rstd[0:n, u:u + 1], ss[0:n, u:u + 1], ACT.Sqrt).then_inc(rstd_ready, 1)

            for u in range(2):
                norm(0, u)
            with act.Fori(1, TT // 2) as i:
                for u in range(2):
                    norm(i, u)
            norm(TT // 2, 0, SMP)

        @block.vector
        def _(dve):
            ch = Chain(dve, dve_chain)
            dve.wait_ge(par_tr, 1)
            v = nc.vector
            v.tensor_copy(par[:, :, :], psum[:, 5, 0:2 * NROW].rearrange("p (t r) -> p t r", t=2)).then_inc(par_ready, 1)
            v.tensor_copy(par7[:, :], psum[:, 5, 84:99]).then_inc(par_ready, 1)
            v.tensor_copy(st_shift[:, :, :], psum[:, 5, 100:156].rearrange("p (t b) -> p t b", t=7)).then_inc(par_ready, 1)
            v.tensor_copy(st_pool[:, :, :], psum[:, 5, 160:400].rearrange("p (t b) -> p t b", t=2)).then_inc(par_ready, 1)
            v.tensor_copy(st_conv[:, :, :], psum[:, 6, 0:480].rearrange("p (t b) -> p t b", t=2)).then_inc(par_ready, 1)
            dve.wait_ge(par_ready, 5)

            def prepare(u, rows):
                ch.link(v.tensor_scalar(ss[0:rows, u:u + 1], ss[0:rows, u:u + 1], RMS_EPS, None, ALU.add))
                v.reciprocal(ss[0:rows, u:u + 1], ss[0:rows, u:u + 1]).then_inc(inv_ready, 1)

            def scale(u, rows):
                v.tensor_scalar(xh[0:rows, u, :], xt[0:rows, u, :], rstd[0:rows, u:u + 1], None, ALU.mult).then_inc(h_ready, 1)

            def collect(u, rows, col):
                src = psum[:, 2 * u:2 * u + 2, :].rearrange("p b (k t) -> p (b k) t", k=4)[:, :, 0:rows]
                g = par7[:, 0:KT].unsqueeze(2).to_broadcast([P, KT, rows])
                v.tensor_tensor(hT[:, :, bass.ds(col, rows)], src, g, ALU.mult).then_inc(hT_ready, 1)

            for u in range(2):
                dve.wait_ge(sq_done, u + 1)
                prepare(u, P)
            for u in range(2):
                dve.wait_ge(rstd_ready, u + 1)
                scale(u, P)
            for u in range(2):
                dve.wait_ge(h_tr, u + 1)
                collect(u, P, u * P)
            with dve.Fori(1, TT // 2) as i:
                with ch.body(i, 1, TT // 2, 2):
                    for u in range(2):
                        dve.wait_ge(sq_done, i * 2 + (u + 1))
                        prepare(u, P)
                    for u in range(2):
                        dve.wait_ge(rstd_ready, i * 2 + (u + 1))
                        dve.wait_ge(h_tr, i * 2 + (u - 1))
                        scale(u, P)
                    for u in range(2):
                        dve.wait_ge(h_tr, i * 2 + (u + 1))
                        collect(u, P, i * (2 * P) + u * P)
            dve.wait_ge(sq_done, TT + 1)
            prepare(0, SMP)
            dve.wait_ge(rstd_ready, TT + 1)
            scale(0, SMP)
            dve.wait_ge(h_tr, TT + 1)
            collect(0, SMP, SEQ)

            dve.wait_ge(made, COUNTS + 1)
            for t in range(2):
                for h in range(2):
                    hs = slice(h * 64, h * 64 + 64)
                    ch.link(v.tensor_scalar(cnt[hs, t, :], cnt[hs, t, :], float(POOL_WINDOWS[t][h]), None, ALU.min))
            ch.link(v.reciprocal(cnt[:, :, :], cnt[:, :, :]))
            ch.link(v.tensor_scalar(one_m_ka[:, :], par[:, :, PKA], -1.0, 1.0, ALU.mult, ALU.add))

            dve.wait_ge(c_in, 64)
            dve.wait_ge(made, PADS + 4)
            for t in range(2):
                ch.link(v.tensor_copy(history(ext_c[:, t], POOL_BUF + SEQ, POOL_S)[:, :, 0:POOL_BUF],
                                      st_pool[:, t, :].rearrange("p (b s) -> p b s", b=DEC_BATCH)))
            for t in range(2):
                e, s0, s1 = ext_c[:, t], sums[:, 0], sums[:, 1]
                n = POOL_EXT

                def double(out, in_, w, rows=slice(0, P)):
                    ch.link(v.tensor_tensor(out[rows, 2 * w - 1:n], in_[rows, 2 * w - 1:n], in_[rows, w - 1:n - w], ALU.add))

                up = slice(64, P)
                double(s0, e, 1)
                if t == 0:
                    double(s1, s0, 2, up)
                else:
                    double(s1, s0, 2)
                    double(s0, s1, 4)
                    double(s1, s0, 8, up)
                for h, src in enumerate((s0, s1)):
                    hs = slice(h * 64, h * 64 + 64)
                    inv = 1.0 / POOL_WINDOWS[t][h]
                    es, ss_ = (history(x, POOL_BUF + SEQ, POOL_S)[hs, :, POOL_BUF:] for x in (e, src))
                    v.scalar_tensor_tensor(samples(pooled[:, t])[hs], ss_, inv, es, ALU.mult, ALU.subtract).then_inc(dve_chain, 1)
                    ch.n += 1
                    v.scalar_tensor_tensor(pooled[hs, t, 16:SEQ], src[hs, POOL_BUF + 16:POOL_BUF + SEQ], inv,
                                           e[hs, POOL_BUF + 16:POOL_BUF + SEQ], ALU.mult, ALU.subtract).then_inc(dve_chain, 1)
                    ch.n += 1
                    ch.link(v.tensor_tensor(fix[hs, t, :], src[hs, POOL_BUF:POOL_BUF + 16], cnt[hs, t, :], ALU.mult))
                    ch.link(v.tensor_tensor(pooled[hs, t, 0:16], fix[hs, t, :], e[hs, POOL_BUF:POOL_BUF + 16], ALU.subtract))
                dve.sem_inc(pooled_ready, 1)

            dve.wait_ge(d_in, 96)
            for t in range(2):
                v.tensor_copy(history(ext_d[:, t], CONV_BUF + SEQ, CONV_S)[:, :, 0:CONV_BUF],
                              st_conv[:, t, :].rearrange("p (b s) -> p b s", b=DEC_BATCH)).then_inc(glu_ready, 1)
                dve.wait_ge(d_sig, t + 1)
                row = ext_d[:, t, CONV_BUF:CONV_BUF + SEQ]
                v.tensor_tensor(row, row, u2d[:, t, 0:SEQ], ALU.mult).then_inc(glu_ready, 1)
                row = history(ext_d[:, t], CONV_BUF + SEQ, CONV_S)[:, :, CONV_BUF:]
                v.tensor_tensor(row, row, samples(u2d[:, t]), ALU.mult).then_inc(glu_ready, 1)
            dve.wait_ge(glu_ready, 6)
            for k in range(CONV_WIDTH):
                for t in range(2):
                    w = par[:, t, PCW + k:PCW + k + 1]
                    outs = (conv[:, t, 0:SEQ], samples(conv[:, t]))
                    ins = (ext_d[:, t, k:k + SEQ], history(ext_d[:, t], CONV_BUF + SEQ, CONV_S)[:, :, k:k + DEC_SEQ])
                    for out, in_ in zip(outs, ins):
                        if k == 0:
                            last = v.tensor_scalar(out, in_, w, par[:, t, PCB:PCB + 1], ALU.mult, ALU.add)
                        else:
                            last = v.scalar_tensor_tensor(out, in_, w, out, ALU.mult, ALU.add)
                        last.then_inc(conv_done, 1)
                if k < CONV_WIDTH - 1:
                    dve.wait_ge(conv_done, 4 * (k + 1))

            dve.wait_ge(gates, GATE_C + 2)
            g = 0
            for t in range(2):
                for c in range(CHUNKS):
                    cs = slice(c * CW, (c + 1) * CW)
                    dve.wait_ge(small_mm, g + 1)
                    v.scalar_tensor_tensor(pooled[:, t, cs], psum[:, 5 + g % 3, 0:CW], par[:, t, PPS:PPS + 1],
                                           gate_c[:, t, cs], ALU.mult, ALU.mult).then_inc(small_read, 1)
                    g += 1

            dve.wait_ge(conv_done, CONV_WIDTH * 4)
            dve.wait_ge(out_stored, 16 * 20)
            for n in range(2):
                ch.link(v.memset(sh_ext[:, n, 0:1], 0.0))
            dve.wait_ge(mix_stored, 32)
            for n in range(7):
                e, o = sh_ext[:, n % 2], sh_mix[:, n % 2]
                dve.wait_ge(sh_in[n % 2], 32 * (n // 2 + 1))
                ch.link(v.tensor_copy(history(e, SEQ + 1, SHIFT_S)[:, :, 0], st_shift[:, n, :]))
                if n >= 2:
                    dve.wait_ge(sh_stored[n % 2], 32 * (n // 2))
                if n in (4, 5):
                    dve.wait_ge(ksq_ready, 2 * (n - 3))
                ch.link(v.tensor_tensor(o[:, 0:SHIFT_EXT - 1], e[:, 0:SHIFT_EXT - 1], e[:, 1:SHIFT_EXT], ALU.subtract))
                v.scalar_tensor_tensor(o[:, 0:SHIFT_EXT - 1], o[:, 0:SHIFT_EXT - 1], par7[:, 8 + n:9 + n],
                                       e[:, 1:SHIFT_EXT], ALU.mult, ALU.add).then_inc(sh_done, 1)

            for c in range(CHUNKS):
                cs = slice(c * CW, (c + 1) * CW)
                dve.wait_ge(small_mm, g + 1)
                for t in range(2):
                    v.tensor_tensor(conv[:, t, cs], conv[:, t, cs], psum[:, 5 + g % 3, 0:CW], ALU.subtract).then_inc(small_read, 1)
                g += 1
            dve.wait_ge(sh_stored[0], 96)
            dve.wait_ge(sh_stored[1], 96)
            dve.wait_ge(wa_ready, 4)
            for c in range(CHUNKS):
                cs = slice(c * CW, (c + 1) * CW)
                dve.wait_ge(small_mm, g + 1)
                v.tensor_scalar(ln_inv[:, cs], psum[:, 5 + g % 3, 0:CW], LN_EPS, None, ALU.add).then_inc(small_read, 1)
                dve.wait_ge(small_read, reads_through(g))
                v.reciprocal(ln_inv[:, cs], ln_inv[:, cs]).then_inc(d_inv, 1)
                g += 1
            for c in range(CHUNKS):
                cs = slice(c * CW, (c + 1) * CW)
                dve.wait_ge(d_root, c + 1)
                for t in range(2):
                    v.tensor_tensor(conv[:, t, cs], conv[:, t, cs], ln_inv[:, cs], ALU.mult).then_inc(d_norm, 1)
            dve.wait_ge(gates, GATE_D + 2)
            for c in range(CHUNKS):
                cs = slice(c * CW, (c + 1) * CW)
                for o in range(2):
                    dve.wait_ge(small_mm, g + 1)
                    v.tensor_tensor(conv[:, o, cs], psum[:, 5 + g % 3, 0:CW], gate_d[:, o, cs], ALU.mult).then_inc(small_read, 1)
                    g += 1

            for t in range(2):
                for c in range(CHUNKS):
                    cs = slice(c * CW, (c + 1) * CW)
                    dve.wait_ge(small_mm, g + 1)
                    v.tensor_scalar(kinv[:, t, cs], psum[:, 5 + g % 3, 0:CW], 1e-12, None, ALU.max).then_inc(small_read, 1)
                    dve.wait_ge(small_read, reads_through(g))
                    v.reciprocal(kinv[:, t, cs], kinv[:, t, cs]).then_inc(kinv_pre, 1)
                    g += 1

            ch.link(v.memset(seg[:, :], 1.0))
            ch.link(v.memset(seg[:, :].rearrange("p (n c) -> p n c", c=CH)[:, :, 0], 0.0))
            dve.wait_ge(kinv_ready, 10)
            dve.wait_ge(lora_read, 20)
            for t in range(2):
                dve.wait_ge(rk_in, 48 * (t + 1))
                ch.link(v.tensor_scalar(sig_w[:, t], sig_w[:, t], DECAY, None, ALU.mult))
                ch.link(v.scalar_tensor_tensor(rw_kk[:, :], rw_k[:, :], par[:, t, PKK:PKK + 1], kinv[:, t], ALU.mult, ALU.mult))
                ch.link(v.tensor_scalar(rw_t[:, :], rate[:, t], par[:, t, PKA:PKA + 1], one_m_ka[:, t:t + 1], ALU.mult, ALU.add))
                ch.link(v.tensor_tensor(rw_k[:, :], rw_t[:, :], rw_k[:, :], ALU.mult))
                ch.link(v.scalar_tensor_tensor(rw_t[:, :], rw_r[:, :], par[:, t, PRK:PRK + 1], rw_k[:, :], ALU.mult, ALU.mult))
                v.tensor_tensor(rate[:, t], rw_kk[:, :], rate[:, t], ALU.mult).then_inc(rkk_ready, 1)
                dve.wait_ge(rkk_ready, t + 1)
                for m, src in ((0, rw_r), (1, sig_w[:, t]), (2, rw_k), (3, rw_kk), (4, rate[:, t])):
                    ch.mark(v.tensor_copy(smp[:, m, t, :], src[:, SEQ:T_ALL]))
                ch.link(v.tensor_tensor_scan(rw_L[:, 0:SEQ], seg[:, :], sig_w[:, t, 0:SEQ], 0.0, ALU.mult, ALU.add))
                dve.wait_ge(rkk_stored, 16 * (t + 1))
                v.tensor_tensor(rw_t[:, 0:SEQ], rw_L[:, 0:SEQ], sig_w[:, t, 0:SEQ], ALU.subtract).then_inc(L_ready, 1)
                dve.wait_ge(exp_ready, 3 * t + 1)
                v.tensor_tensor(rw_kk[:, 0:SEQ], rw_kk[:, 0:SEQ], rw_t[:, 0:SEQ], ALU.mult).then_inc(rw_ready, 1)
                dve.wait_ge(rw_ready, 4 * t + 1)
                dve.sem_inc(L_ready, 1)
                dve.wait_ge(exp_ready, 3 * t + 2)
                ch.link(v.tensor_copy(pend[:, t, :], rw_t[:, 0:SEQ].rearrange("p (n c) -> p n c", c=CH)[:, :, CH - 1]))
                v.tensor_tensor(rw_r[:, 0:SEQ], rw_r[:, 0:SEQ], rw_t[:, 0:SEQ], ALU.mult).then_inc(rw_ready, 1)
                dve.wait_ge(rw_ready, 4 * t + 2)
                dve.sem_inc(L_ready, 1)
                dve.wait_ge(exp_ready, 3 * t + 3)
                v.tensor_tensor(rw_k[:, 0:SEQ], rw_k[:, 0:SEQ], rw_t[:, 0:SEQ], ALU.mult).then_inc(rw_ready, 1)
                v.tensor_tensor(rate[:, t, 0:SEQ], rate[:, t, 0:SEQ], rw_t[:, 0:SEQ], ALU.mult).then_inc(rw_ready, 1)

            dve.wait_ge(made, LANE + 1)
            dve.wait_ge(rows_in, 16 * (len(ROWS256) + 7) + 16 * PT)
            ch.link(v.tensor_scalar(lane[:, :], lane[:, :], RT - 1, None, ALU.bitwise_and))
            ch.link(v.tensor_copy(lanef[:, :], lane[:, :]))
            ch.link(v.tensor_copy(pidf[:, :], pidx[:, :]))
            ch.link(v.tensor_scalar(pidf[:, :], pidf[:, :], float(RT), lanef[:, :], ALU.mult, ALU.add))
            v.tensor_copy(pidx[:, :], pidf[:, :]).then_inc(idx_ready, 1)
            dve.wait_ge(rw_stored, 128)
            ch.link(v.memset(ones_t, 1.0))
            v.memset(qaug[64:65, :, :, :], 8.0).then_inc(qones_ready, 1)
            dve.wait_ge(a_in, 16 * 8)
            v.tensor_scalar(fx, fx, bf_col[:, :], None, ALU.add).then_inc(f_pre, 1)
            dve.wait_ge(f_abs, 3)
            ch.link(v.tensor_scalar(fx, fx, 0.0, None, ALU.min))
            ch.link(v.tensor_tensor(fx, fa, fx, ALU.subtract))
            v.tensor_scalar(fa, fx, -1.0, None, ALU.mult).then_inc(nl_ready, 1)
            dve.sem_inc(nl_ready, 1)
            ch.mark(v.tensor_tensor_scan(nc_[:, 0:SEQ], ones_t, fx[:, 0:SEQ], 0.0, ALU.mult, ALU.add))
            ch.link(v.tensor_copy(samples(nc_)[:, :, 0], samples(fx)[:, :, 0]))
            for i in range(1, DEC_SEQ):
                ch.link(v.tensor_tensor(samples(nc_)[:, :, i], samples(nc_)[:, :, i - 1], samples(fx)[:, :, i], ALU.add))
            dve.wait_ge(nl_ready, 2)
            dve.sem_inc(nc_ready, 1)

            def kv_copy(u):
                v.tensor_copy(kvs[:, u, :], psum[:, u, :]).then_inc(kv_copied, 1)

            for u in range(2):
                dve.wait_ge(kv_tr, u + 1)
                kv_copy(u)
            with dve.Fori(1, TT // 2) as i:
                for u in range(2):
                    dve.wait_ge(kv_tr, i * 2 + (u + 1))
                    dve.wait_ge(kv_stored[u], i * 32)
                    dve.wait_ge(v_kept, i * 2 + (u - 1))
                    kv_copy(u)
            dve.wait_ge(kvs_tr, 1)
            v.tensor_copy(kv_s[:, :], psum[0:SMP, 0, :]).then_inc(kvs_copied, 1)
            dve.wait_ge(f_tr, 1)
            v.tensor_copy(lft[:, :, :], psum[:, 2, 0:64].rearrange("p (n h) -> p n h", h=4)).then_inc(f_copied, 1)
            v.tensor_copy(lf_s[:, :], psum[0:SMP, 2, 64:72]).then_inc(f_copied, 1)

            dve.wait_ge(gates, GATE_A + 2)

            def row_max(i, g, j):
                w = j % 2
                dve.wait_ge(s_mm, i * 8 + (j + 1))
                ch.link(v.reduce_max(mx[:, w:w + 1], psum[:, 4 * w:4 * w + g + 1, :].rearrange("p b c -> p (b c)"), AX.X))
                v.tensor_scalar(nb[:, w:w + 1], mx[:, w:w + 1], -0.125, None, ALU.mult).then_inc(s_max, 1)

            def inverse_sums(i, g, j):
                dve.wait_ge(p_ready, i * 8 + (j + 1))
                ch.link(v.reciprocal(linv[:, :], lsum[:, :]))
                v.tensor_copy(lbc[:, :].rearrange("p (h d) -> p h d", h=2), linv[:, :].unsqueeze(2).to_broadcast([P, 2, 64])).then_inc(lb_ready, 1)

            def copy_output(i, g, j):
                w = j % 2
                hs = slice(w * 64, w * 64 + 64)
                dve.wait_ge(o_mm, i * 8 + (j + 1))
                v.tensor_copy(oc[hs, :], psum[hs, 4 * w, 0:P]).then_inc(o_copied, 1)

            def outputs(i, g, j):
                pr, u = (j % 4) // 2, j // 4
                rows = i * (2 * P) + u * P
                gate = gate_a[:, pr, bass.ds(rows, P)]
                dve.wait_ge(lb_tr, i * 4 + (j // 2 + 1))
                v.tensor_tensor(lg[:, :], psum[:, 7, 0:P], gate, ALU.mult).then_inc(lg_ready, 1)
                dve.wait_ge(lg_ready, i * 4 + (j // 2 + 1))
                dve.wait_ge(o_copied, i * 8 + (j + 1))
                v.tensor_tensor(gate, oc[:, :], lg[:, :], ALU.mult).then_inc(o_read, 1)
                dve.wait_ge(o_read, i * 4 + (j // 2 + 1))

            def attention(i, g):
                for j in range(8):
                    row_max(i, g, j)
                    if j > 0:
                        finish(i, g, j - 1)
                finish(i, g, 7)

            def finish(i, g, j):
                if j % 2 == 1:
                    inverse_sums(i, g, j)
                copy_output(i, g, j)
                if j % 2 == 1:
                    outputs(i, g, j)

            attention(0, 0)
            attention(1, 0)
            for g in range(1, 4):
                with dve.Fori(2 * g, 2 * g + 2) as i:
                    with ch.body(i, 2 * g, 2 * g + 2, 8 + 4):
                        attention(i, g)

            dve.wait_ge(mixa_stored, 32)
            dve.wait_ge(made, RMASKS + 11)
            v.memset(state[:, 0:2, :], 0.0).then_inc(state_zero, 1)
            v.memset(trans[:, :, :], 0.0).then_inc(state_zero, 1)
            v.memset(tok_k[:, :, :], 0.0).then_inc(state_zero, 1)
            v.memset(tok_b[:, :, :], 0.0).then_inc(state_zero, 1)
            dve.wait_ge(state_zero, 4)
            v.tensor_tensor(id64[:, :], ident[:, 0:64], ident[:, 64:P], ALU.add).then_inc(id64_ready, 1)
            dve.wait_ge(id64_ready, 1)

            def rwkv_tile(i, u, first):
                def at(n, k=1, per=1, back=False):
                    if back and first:
                        return
                    dve.wait_ge(R[n], i * (2 * per) + (u * per + k - (per if back else 0)))

                def heads4(bank, n=4):
                    return psum[:, bank, 0:n * P].rearrange("p (h c) -> p h c", h=n)

                def masks(m):
                    return m[:, :, :].rearrange("p a c -> p (a c)").unsqueeze(1).unsqueeze(1).to_broadcast([P, 2, 2, 256])

                def by_parity(x):
                    return x.rearrange("p (t b) c -> p b t c", b=2)

                at('o_mm', back=True)
                at('gram_b')
                v.tensor_tensor(by_parity(gb[:, :, :, :].rearrange("p h a c -> p h (a c)")),
                                psum[:, 2:4, :].rearrange("p b (h c) -> p b h c", h=2), masks(mneg), ALU.mult).then_inc(R['gb'], 1)
                at('gram_k')
                v.tensor_tensor(by_parity(gk[:, :, :, :].rearrange("p h a c -> p h (a c)")),
                                psum[:, 4:6, :].rearrange("p b (h c) -> p b h c", h=2), masks(mpos), ALU.mult).then_inc(R['gk'], 1)
                at('gram_m')
                v.tensor_tensor(by_parity(mpow[:, 2]), psum[:, 6:8, 0:2 * P].rearrange("p b (h c) -> p b h c", h=2),
                                mrow[:, :].unsqueeze(1).unsqueeze(1).to_broadcast([P, 2, 2, P]), ALU.mult).then_inc(R['gm'], 1)
                v.tensor_copy(pcur[:, :, :], pend[:, :, bass.ds(i * 4 + 2 * u, 2)]).then_inc(R['pcur'], 1)
                at('kv_mm')
                v.tensor_copy(sol[:, :, 64:P], psum[:, 1, 0:256].rearrange("p (h c) -> p h c", h=4)).then_inc(R['kv'], 1)
                at('kv')
                at('tok', 6, 6)
                for l in range(6):
                    if l < 5:
                        at('sqT_mm', l + 1, 5)
                        v.tensor_copy(mpowT[:, (l + 1) % 2, :, :], heads4(2)).then_inc(R['sqT'], 1)
                    at('app_mm', l + 1, 6)
                    if l > 0:
                        at('app', l, 6)
                    v.tensor_tensor(sol[:, :, :], sol[:, :, :], heads4(4), ALU.add).then_inc(R['app'], 1)
                at('q_mm')
                v.tensor_tensor(qT_r[:, :, :], psum[:, 5, 0:256].rearrange("p (t c) -> p t c", t=2), rin[:, u, RHO:RHO + 2, :], ALU.add).then_inc(R['q'], 1)
                at('tr_mm')
                for hh in range(2):
                    hs = slice(hh * 64, hh * 64 + 64)
                    v.tensor_tensor(trans[hs, :, hs], psum[hs, 6, 0:256].rearrange("p (n k) -> p n k", n=4),
                                    id64[hs, :].unsqueeze(1).to_broadcast([64, 4, 64]), ALU.add).then_inc(R['tr'], 1)
                at('pcur')
                for c in range(2):
                    at('st_mm', c + 1, 2)
                    to = u * 4 + 2 if c == 0 else (1 - u) * 4
                    for t in range(2):
                        v.tensor_scalar(state[:, to + t, :], psum[:, 7, (c * 2 + t) * P:(c * 2 + t + 1) * P],
                                        pcur[:, t, c:c + 1], None, ALU.mult).then_inc(R['st'], 1)

            rwkv_tile(0, 0, True)
            rwkv_tile(0, 1, False)
            with dve.Fori(1, TT // 2) as i:
                rwkv_tile(i, 0, False)
                rwkv_tile(i, 1, False)
            dve.wait_ge(wkv_tr, 1)
            for hh in range(2):
                hs = slice(hh * 64, hh * 64 + 64)
                v.tensor_copy(wkv_o[hs, :, :], psum[hs, 2, 0:256].rearrange("p (t c) -> p t c", t=2)[:, :, hs]).then_inc(wkv_copied, 1)

            dve.wait_ge(R['o_mm'], TT)
            dve.wait_ge(s_in, 32)
            dve.wait_ge(s_dec, 1)
            BT = DEC_BATCH * 2

            def bt(x):
                return x.rearrange("p (n k) -> p n k", n=BT)

            S = s_wkv[:, :, :].rearrange("p b c -> p (b c)")

            def column(m, i):
                return smp[:, m].rearrange("p t (b i) -> p b t i", i=DEC_SEQ)[:, :, :, i]

            def rows(n):
                return psum[:, 2 * (n % 4):2 * (n % 4) + 2, :].rearrange("p a b -> p (a b)")

            for i in range(DEC_SEQ):
                for n, m in enumerate((3, 1, 4, 2, 0)):
                    if i > 0:
                        dve.wait_ge(s_mm2, i * 5 - 4 + n)
                    v.tensor_tensor(z_exp[:, n, :].rearrange("p (b t k) -> p b t k", b=DEC_BATCH, t=2),
                                    column(m, i).unsqueeze(3).to_broadcast([P, DEC_BATCH, 2, 64]),
                                    id64[:, :].unsqueeze(1).unsqueeze(1).to_broadcast([P, DEC_BATCH, 2, 64]), ALU.mult).then_inc(s_z, 1)
                k = i * 5
                dve.wait_ge(s_mm2, k + 1)
                v.tensor_tensor(s_tmp[:, :], S, rows(k), ALU.mult).then_inc(s_used, 1)
                dve.wait_ge(s_used, k + 1)
                ch.link(v.reduce_sum(s_kk[:, :], bt(s_tmp), AX.X))
                dve.wait_ge(s_mm2, k + 2)
                v.tensor_tensor(S, S, rows(k + 1), ALU.mult).then_inc(s_used, 1)
                dve.wait_ge(s_used, k + 2)
                dve.wait_ge(s_mm2, k + 3)
                v.tensor_tensor(bt(s_tmp), bt(rows(k + 2)), s_kk[:, :].unsqueeze(2).to_broadcast([P, BT, 64]), ALU.mult).then_inc(s_used, 1)
                dve.wait_ge(s_used, k + 3)
                ch.link(v.tensor_tensor(S, S, s_tmp[:, :], ALU.subtract))
                dve.wait_ge(s_mm2, k + 4)
                vcol = column(5, i).unsqueeze(3).to_broadcast([P, DEC_BATCH, 2, 64])
                b4 = "p (b t k) -> p b t k"
                v.tensor_tensor(s_tm2[:, :].rearrange(b4, b=DEC_BATCH, t=2), rows(k + 3).rearrange(b4, b=DEC_BATCH, t=2), vcol, ALU.mult).then_inc(s_used, 1)
                dve.wait_ge(s_used, k + 4)
                ch.link(v.tensor_tensor(S, S, s_tm2[:, :], ALU.add))
                dve.wait_ge(s_mm2, k + 5)
                v.tensor_tensor(s_tmp[:, :], S, rows(k + 4), ALU.mult).then_inc(s_used, 1)
                dve.wait_ge(s_used, k + 5)
                ch.link(v.reduce_sum(s_kk[:, :], bt(s_tmp), AX.X))
                ch.link(v.tensor_copy(o_rw[:, :, SEQ:T_ALL].rearrange("p t (b i) -> p b t i", i=DEC_SEQ)[:, :, :, i],
                                      s_kk[:, :].rearrange("p (b t) -> p b t", t=2)))
            dve.wait_ge(R['o'], TT)
            dve.sem_inc(s_done, 1)

            g = 0
            for t in range(2):
                for c in range(CHUNKS):
                    cs = slice(c * CW, (c + 1) * CW)
                    dve.wait_ge(gn_mm, g + 1)
                    v.scalar_tensor_tensor(o_rw[:, t, cs], psum[:, g % 8, 0:CW], -1.0 / 64, o_rw[:, t, cs], ALU.mult, ALU.add).then_inc(gn_read, 1)
                    g += 1
            for t in range(2):
                for c in range(CHUNKS):
                    cs = slice(c * CW, (c + 1) * CW)
                    dve.wait_ge(gn_mm, g + 1)
                    v.tensor_scalar(gn_inv[:, t, cs], psum[:, g % 8, 0:CW], 1.0 / 64, GN_EPS, ALU.mult, ALU.add).then_inc(gn_read, 1)
                    g += 1
                    dve.wait_ge(gn_read, g)
                    v.reciprocal(gn_inv[:, t, cs], gn_inv[:, t, cs]).then_inc(gn_pre, 1)
            dve.wait_ge(gates, GATE_B + 2)
            n = 0
            for t in range(2):
                for c in range(CHUNKS):
                    cs = slice(c * CW, (c + 1) * CW)
                    o = o_rw[:, t, cs]
                    dve.wait_ge(gn_mm, g + 1)
                    v.tensor_tensor(g_v[:, t, cs], psum[:, g % 8, 0:CW], g_v[:, t, cs], ALU.mult).then_inc(gn_read, 1)
                    dve.wait_ge(gn_root, n + 1)
                    ch.link(v.tensor_tensor(o, o, gn_inv[:, t, cs], ALU.mult))
                    ch.link(v.tensor_scalar(o, o, par[:, t, PGG:PGG + 1], par[:, t, PGB:PGB + 1], ALU.mult, ALU.add))
                    dve.wait_ge(gn_read, g + 1)
                    ch.link(v.tensor_tensor(o, o, g_v[:, t, cs], ALU.add))
                    ch.mark(v.tensor_tensor(o, o, gate_b[:, t, cs], ALU.mult))
                    g += 1
                    n += 1
            ch.join()
            dve.sem_inc(mixb_ready, 1)

            dve.wait_ge(lf_in, 16 * DEC_BATCH * DT)
            B4 = bias[:, :, :].rearrange("p n (j h) -> p n j h", h=4)
            L4 = lf_past[:, :, :].rearrange("p n (j h) -> p n j h", h=4)
            ch.link(v.memset(B4[:, :, TJ - 1, :], 0.0))
            for j in range(TJ - 2, -1, -1):
                ch.link(v.tensor_tensor(B4[:, :, j, :], B4[:, :, j + 1, :], L4[:, :, j + 1, :], ALU.add))
            dve.wait_ge(made, DCONST + 12)
            T3 = tot[:, :].rearrange("p (n h) -> p n h", h=4)
            v.tensor_tensor(T3, B4[:, :, 0, :], L4[:, :, 0, :], ALU.add).then_inc(tot_ready, 1)
            ch.link(v.memset(tsuf[:, :, DT - 1, :], 0.0))
            dve.wait_ge(D['suf_mm'], D0['suf_mm'] + 1)
            ch.link(v.tensor_copy(tsum[:, :], psum[:, 6, 0:256]))
            S4 = tsum[:, :].rearrange("p (b t h) -> p b t h", b=DEC_BATCH, t=DT)
            for t in range(DT - 2, -1, -1):
                ch.link(v.tensor_tensor(tsuf[:, :, t, :], tsuf[:, :, t + 1, :], S4[:, :, t + 1, :], ALU.add))
            ch.link(v.tensor_tensor(tsum[:, :], psum[:, 5, 0:256], tsuf[:, :, :, :].rearrange("p b t h -> p (b t h)"), ALU.add))
            v.tensor_tensor(B4, B4, tsum[:, :].rearrange("p (n h) -> p n h", h=4).unsqueeze(2).to_broadcast([P, DEC_BATCH * DT, TJ, 4]),
                            ALU.add).then_inc(bias_ready, 1)
            for h in range(2):
                hs = slice(h * 64, h * 64 + 64)
                v.tensor_scalar(qbd[hs, :, :, h * 4:h * 4 + 4], qT_s[hs, :, :].rearrange("p t (b q) -> p b t q", q=DEC_SEQ),
                                0.125, None, ALU.mult).then_inc(bias_ready, 1)
            ch.link(v.tensor_copy(v_new[0:SMP, :], kv_s[:, 256:512]))
            nm = nmask[:, :, :].rearrange("p b (h q) -> p b h q", h=4)
            ch.link(v.tensor_tensor(nm, nm, lf_s[:, 4:8].unsqueeze(1).unsqueeze(3).to_broadcast([SMP, DEC_BATCH, 4, DEC_SEQ]), ALU.add))
            ch.link(v.tensor_tensor(sel[:, :], ident[:, 0:16], ident[:, 32:48], ALU.add))
            ch.link(v.tensor_tensor(sel[:, :], sel[:, :], ident[:, 64:80], ALU.add))
            ch.link(v.tensor_tensor(sel[:, :], sel[:, :], ident[:, 96:112], ALU.add))
            rows_of = ident[:, :].rearrange("p (f r c) -> p f r c", f=2, r=2)
            ch.link(v.tensor_tensor(sel_r[:, :, :], rows_of[:, 0, :, 0:8], rows_of[:, 1, :, 0:8], ALU.add))
            ch.link(v.memset(psum[:, 4:6, :], 0.0))
            v.memset(psum[:, 7, 0:256], 0.0).then_inc(bias_ready, 1)
            dve.wait_ge(bias_ready, 4)

            def keys(b, first):
                if not first:
                    dve.wait_ge(D['new_mm'], D0['new_mm'] + b)
                by_row = bias_w[:, :, :].rearrange("p (t j) (f r x) -> p t j f r x", j=4, f=2, r=2)
                past = bias[:, bass.ds(b * 8, 8), :].rearrange("p t (f j h) -> p t f j h", f=2, h=4)
                for hf in range(2):
                    for h in range(4):
                        ch.mark(v.tensor_copy(by_row[:, :, :, hf, h // 2, (h % 2) * 4:(h % 2) * 4 + 4],
                                              past[:, :, hf, :, h].unsqueeze(3).to_broadcast([P, DT, 4, 4])))
                ch.mark(v.tensor_copy(nm_cur[0:SMP, 0:64].rearrange("p (r x) -> p r x", r=2)[:, :, 0:8],
                                      nmask[:, bass.ds(b, 1), :].rearrange("p o (r x) -> p (o r) x", r=2)))
                ch.mark(v.tensor_copy(q_cur[:, :, :], qbd[:, bass.ds(b, 1), :, :].rearrange("p o r x -> p (o r) x")))
                ch.join()
                dve.sem_inc(D['prep'], 1)
                for t in range(DT):
                    dve.wait_ge(D['k_tr'], D0['k_tr'] + b * 16 + (2 * t + 1))
                    if not (first and t == 0):
                        dve.wait_ge(D['sc_mm'], D0['sc_mm'] + b * 8 + t)
                    v.tensor_copy(kT_d[:, 0, :, :], psum[:, 0:2, :]).then_inc(D['kT0'], 1)
                    if t > 0:
                        tile_max(b, t - 1)
                tile_max(b, DT - 1)
                dve.wait_ge(D['s'], D0['s'] + b * 9 + 9)
                ch.mark(v.reduce_max(m8[:, DT:DT + 1], s_rows[:, DT * 512:DT * 512 + SMP], AX.X))
                ch.join()
                v.reduce_max(m1[:, :], m8[:, :], AX.X).then_inc(D['m1'], 1)
                dve.wait_ge(D['m_tr'], D0['m_tr'] + b + 1)
                ch.link(v.reduce_max(m_half[:, :], psum[0:1, 6, P:2 * P].rearrange("p (f c) -> p c f", f=2), AX.X))
                v.tensor_copy(m_row[:, :].rearrange("p (f c) -> p f c", f=2), m_half[:, :].unsqueeze(1).to_broadcast([1, 2, 64])).then_inc(D['m_row'], 1)
                dve.wait_ge(D['m_mm'], D0['m_mm'] + b + 1)
                v.tensor_scalar(neg_m[:, :], psum[:, 6, 256:257], -1.0, None, ALU.mult).then_inc(D['neg_m'], 1)

            def tile_max(b, t):
                dve.wait_ge(D['s'], D0['s'] + b * 9 + (t + 1))
                ch.mark(v.reduce_max(m8[:, t:t + 1], s_rows[:, t * 512:(t + 1) * 512], AX.X))

            KEYS_LINKS = 10 + DT + 1 + 1

            def values_of(b):
                dve.wait_ge(D['pv_mm'], D0['pv_mm'] + b * 8 + 8)
                v.tensor_copy(pv[:, :], psum[:, 7, 0:256]).then_inc(D['pv'], 1)
                dve.wait_ge(D['o_mm'], D0['o_mm'] + b + 1)
                v.reciprocal(li[:, :], psum[:, 7, 256:272]).then_inc(D['li'], 1)
                dve.wait_ge(D['li'], D0['li'] + b + 1)
                for pr in range(2):
                    for h in range(2):
                        hs = slice(h * 64, h * 64 + 64)
                        x = (pr * 2 + h) * 4
                        v.tensor_tensor(o_s[hs, pr, bass.ds(b * 4, 4)], psum[hs, 7, 288 + pr * 16 + x:292 + pr * 16 + x], li[hs, x:x + 4],
                                        ALU.mult).then_inc(D['o'], 1)

            def turn_probs(b):
                dve.wait_ge(D['p'], D0['p'] + b + 1)
                v.tensor_scalar(l_all[:, :], ones_a[:, :], l_row[:, :], None, ALU.mult).then_inc(D['l_all'], 1)
                for c in range(DT + 1):
                    dve.wait_ge(D['p_tr'], D0['p_tr'] + b * 9 + (c + 1))
                    if c < DT:
                        v.tensor_copy(pT_d[:, c * 4:c * 4 + 4, :, :],
                                      psum[:, 4 + c % 2, :].rearrange("p (j g x) -> p j g x", j=4, g=4)[:, :, :, 0:8]).then_inc(D['pT'], 1)
                    else:
                        v.tensor_copy(p_new[0:SMP, :].rearrange("p (r x) -> p r x", r=2),
                                      psum[0:SMP, 4 + c % 2, 0:64].rearrange("p (r x) -> p r x", r=2)[:, :, 0:8]).then_inc(D['pT'], 1)

            with ch.body(0, 0, 1, KEYS_LINKS):
                keys(0, True)
            turn_probs(0)
            with ch.body(0, 0, 1, KEYS_LINKS):
                keys(1, False)
            values_of(0)
            turn_probs(1)
            with dve.Fori(2, DEC_BATCH) as b:
                with ch.body(b, 2, DEC_BATCH, KEYS_LINKS):
                    keys(b, False)
                    values_of(b - 1)
                    turn_probs(b)
            values_of(DEC_BATCH - 1)
            dve.wait_ge(D['o'], D0['o'] + 4 * DEC_BATCH)
            dve.wait_ge(gates, GATE_S + 1)
            v.tensor_tensor(o_s[:, :, :], o_s[:, :, :], gate_s[:, :, :], ALU.mult).then_inc(mixas_ready, 1)

            dve.wait_ge(rows_in, 16 * (len(ROWS256) + 7 + PT) + 32)

            def residual(i, u, n=P):
                dve.wait_ge(D['y_mm'], D0['y_mm'] + i * 2 + (u + 1))
                dve.wait_ge(kvt_in[u], 16 * (TT // 2 + 1 - u) + i * 16 + 16)
                row = zst[0:n, u, 0:D_MODEL]
                v.tensor_tensor(row, row, psum[0:n, 2 * u:2 * u + 2, :].rearrange("p a b -> p (a b)"), ALU.add).then_inc(D['y_sum'], 1)

            def final(i, u, n=P):
                dve.wait_ge(sq_done, (TT + 1) + i * 2 + (u + 1))
                ch.link(v.tensor_scalar(ss[0:n, u:u + 1], ss[0:n, u:u + 1], RMS_EPS, None, ALU.add))
                v.reciprocal(ss[0:n, u:u + 1], ss[0:n, u:u + 1]).then_inc(inv_ready, 1)
                dve.wait_ge(rstd_ready, (TT + 1) + i * 2 + (u + 1))
                v.scalar_tensor_tensor(yb[0:n, u, :], zst[0:n, u, 0:D_MODEL], rstd[0:n, u:u + 1], gf[0:n, :], ALU.mult, ALU.mult).then_inc(h_ready, 1)

            for u in range(2):
                residual(0, u)
                final(0, u)
            with dve.Fori(1, TT // 2) as i:
                with ch.body(i, 1, TT // 2, 2):
                    for u in range(2):
                        residual(i, u)
                        final(i, u)
            residual(TT // 2, 0, SMP)
            final(TT // 2, 0, SMP)


OUTS = [('y_prompt', (1, 2048, 1024)), ('y_sample', (8, 4, 1024)),
        ('k_prompt', (1, 1, 2048, 4, 64)), ('v_prompt', (1, 1, 2048, 4, 64)), ('logf_prompt', (1, 1, 2048, 4)),
        ('wkv_prompt', (1, 1, 4, 64, 64)), ('shift_prompt', (1, 1, 896)), ('pool_prompt', (1, 1, 15, 256)),
        ('conv_prompt', (1, 1, 30, 256)),
        ('k_sample', (8, 1, 4, 4, 64)), ('v_sample', (8, 1, 4, 4, 64)), ('logf_sample', (8, 1, 4, 4)),
        ('wkv_sample', (8, 1, 4, 64, 64)), ('shift_sample', (8, 1, 896)), ('pool_sample', (8, 1, 15, 256)),
        ('conv_sample', (8, 1, 30, 256))]


def kernel(**inputs):
    import numpy as np
    import concourse.bacc as bacc
    from concourse.bass_utils import run_bass_kernel_spmd as run

    nc = bacc.Bacc("TRN2", target_bir_lowering=False, num_devices=1)
    arrays, I = {}, {}
    for name, a in inputs.items():
        a = np.ascontiguousarray(a)
        arrays["in_" + name] = a
        I[name] = nc.dram_tensor("in_" + name, a.shape, mybir.dt.from_np(a.dtype), kind="ExternalInput").ap()
    O = {n: nc.dram_tensor("out_" + n, s, F32, kind="ExternalOutput").ap() for n, s in OUTS}
    build(nc, I, O)
    r = run(nc, [arrays], core_ids=[0])
    return tuple(r.results[0]["out_" + n] for n, _ in OUTS)
```

```python
import concourse.bass as bass
from concourse import mybir
from contextlib import ExitStack, contextmanager

F32 = mybir.dt.float32
BF16 = mybir.dt.bfloat16
I32 = mybir.dt.int32
ALU = mybir.AluOpType
ACT = mybir.ActivationFunctionType
AX = mybir.AxisListType

P = 128
D_MODEL, SEQ, DEC_BATCH, DEC_SEQ = 1024, 2048, 8, 4
SMP = DEC_BATCH * DEC_SEQ
T_ALL = SEQ + SMP
KT = D_MODEL // P
TT = SEQ // P
CHUNKS = 5
CW = T_ALL // CHUNKS
RMS_EPS, LN_EPS, GN_EPS = 1e-6, 1e-5, 64e-5

UC0, GC0, U1D, U2D, GD0, R0, K0, V0, WA, GB0, FG, QA, KA, VA, GA = 0, 2, 4, 6, 8, 10, 12, 14, 16, 17, 19, 20, 22, 24, 26
N_SLOTS = 28
COL_CD, COL_B, COL_GB1, COL_F, COL_A, COL_GA = 2180, 1028, 2052, 768, 0, 772
MIX_A, MIX_B, MIX_C, MIX_D = 0, 2, 4, 6
ROWS256 = ['rw_w0', 'rw_a0', 'rw_kk', 'rw_ka', 'rw_rk', 'rw_gn_g', 'rw_gn_b', 'pool_scale', 'conv_b', 'ln_g', 'ln_b']
PW0, PA0, PKK, PKA, PRK, PGG, PGB, PPS, PCB, PLG, PLB = range(11)
PCW = 11
CONV_WIDTH, POOL_BUF = 31, 15
CONV_BUF = CONV_WIDTH - 1
POOL_WINDOWS = ((2, 4), (8, 16))
POOL_S = POOL_BUF + DEC_SEQ
CONV_S = CONV_BUF + DEC_SEQ
POOL_EXT = POOL_BUF + SEQ + DEC_BATCH * POOL_S
CONV_EXT = CONV_BUF + SEQ + DEC_BATCH * CONV_S
SHIFT_S = 1 + DEC_SEQ
SHIFT_EXT = 1 + SEQ + DEC_BATCH * SHIFT_S
RT = 16
PAGE, N_PAGES = 128, 64
PT = P // RT
TJ = PAGE // RT
DT = N_PAGES // PT
KV_ROW = TJ * 256
SC = DT * TJ * 16
CH = 64
NCH = SEQ // CH
DECAY = -0.6065306597126334
NROW = PCW + CONV_WIDTH


class Chain:

    def __init__(self, eng, sem):
        self.eng, self.sem, self.base, self.n = eng, sem, 0, 0

    def link(self, ins):
        ins.then_inc(self.sem, 1)
        self.n += 1
        self.eng.wait_ge(self.sem, self.base + self.n)

    def mark(self, ins):
        ins.then_inc(self.sem, 1)
        self.n += 1

    def join(self):
        self.eng.wait_ge(self.sem, self.base + self.n)

    @contextmanager
    def body(self, i, lo, hi, per):
        start = self.n
        assert isinstance(self.base, int)
        self.base, self.n = (i - lo) * per + (self.base + start), 0
        yield
        assert self.n == per, self.n
        self.base, self.n = 0, start + (hi - lo) * per


def build(nc, I, O):
    ctx = ExitStack()
    with ctx:
        ctx.enter_context(nc.allow_non_contiguous_dma(reason="states are small: a few rows per sequence"))

        def sb(name, shape, dt=F32):
            return ctx.enter_context(nc.sbuf_tensor(name, shape, dt))

        def sem(name):
            return ctx.enter_context(nc.semaphore(name))

        zT = nc.dram_tensor("zT", [N_SLOTS, P, T_ALL], F32, kind="Internal").ap()

        psum = ctx.enter_context(nc.psum_tensor("psum", [P, 8, 512], F32))
        mixT = nc.dram_tensor("mixT", [8, P, T_ALL], F32, kind="Internal").ap()
        rkv = nc.dram_tensor("rkv", [6, P, T_ALL], F32, kind="Internal").ap()
        rwS = nc.dram_tensor("rwS", [4, 2, P, SEQ], F32, kind="Internal").ap()
        rkk = nc.dram_tensor("rkk", [2, P, T_ALL], F32, kind="Internal").ap()
        ident = sb("ident", [P, P])
        ones_ln = sb("ones_ln", [P, P])
        ones_head = sb("ones_head", [P, P])
        pw_diag = sb("pw_diag", [P, 2, P])
        pwo = sb("pwo", [P, 2, 256])
        lora = sb("lora", [P, 2, 256])
        cnt = sb("cnt", [P, 2, 16])
        fix = sb("fix", [P, 2, 16])
        one_m_ka = sb("one_m_ka", [P, 2])
        gn_eps = sb("gn_eps", [P, 1])
        pend = sb("pend", [P, 2, NCH])
        smp = sb("smp", [P, 6, 2, SMP])
        par = sb("par", [P, 2, NROW])
        par7 = sb("par7", [P, 15])
        st_pool = sb("st_pool", [P, 2, 120])
        st_conv = sb("st_conv", [P, 2, 240])
        st_shift = sb("st_shift", [P, 7, DEC_BATCH])
        HT = KT * T_ALL
        ARENA = 26200
        big = sb("big", [P, HT + ARENA])

        def area(off, *shape):
            n = 1
            for d in shape:
                n *= d
            a = big[:, off:off + n]
            assert off + n <= HT + ARENA
            if len(shape) == 2:
                a = a.rearrange("p (a b) -> p a b", a=shape[0])
            if len(shape) == 3:
                a = a.rearrange("p (a b c) -> p a b c", a=shape[0], b=shape[1])
            return a

        hT = area(0, KT, T_ALL)
        EC, ED, PO, AC = HT, HT + 4430, HT + 9130, HT + 13330
        SA, U2 = HT + 17490, HT + 21920
        xt = area(SA, 2, D_MODEL)
        xh = area(U2, 2, D_MODEL)
        ext_c = area(EC, 2, POOL_EXT)
        sums = area(SA, 2, POOL_EXT)
        pooled = area(PO, 2, T_ALL)
        ext_d = area(ED, 2, CONV_EXT)
        u2d = area(U2, 2, T_ALL)
        conv = area(AC, 2, T_ALL)
        rows256 = area(AC, 256)[0:NROW]
        rows128 = area(AC + 256, P)[0:15]
        st_rows = area(AC + 384, 3, 256)[0:120]
        sh_rows = area(AC + 1152, 896)[0:DEC_BATCH]
        gate_c = area(SA, 2, T_ALL)
        gate_d = area(U2, 2, T_ALL)
        sh_ext = area(EC, 2, SHIFT_EXT)
        sh_mix = area(PO, 2, SHIFT_EXT)
        wa = area(ED, T_ALL)
        ksq = area(SA, 2, T_ALL)
        ln_sq = area(EC, 2, T_ALL)
        ln_inv = area(PO, T_ALL)
        kinv = area(SA, 2, T_ALL)
        sig_w = area(PO, 2, T_ALL)
        rate = area(EC, 2, T_ALL)
        rw_r = area(AC, T_ALL)
        rw_k = area(AC + T_ALL, T_ALL)
        rw_L = area(ED, T_ALL)
        rw_t = area(ED + T_ALL, T_ALL)
        rw_kk = area(U2, T_ALL)
        seg = area(U2 + T_ALL, SEQ)
        ss = sb("ss", [P, 2])
        rstd = sb("rstd", [P, 2])
        wbuf = sb("wbuf", [P, 2, KT, P])
        zst = sb("zst", [P, 2, T_ALL])

        made = sem("made")
        IDENT, ONES, COUNTS, PADS, RMASKS, MASKS, LANE, DCONST = 0, 2, 8, 9, 13, 24, 28, 29
        rows_in = sem("rows_in")
        par_tr = sem("par_tr")
        par_ready = sem("par_ready")
        x_in = [sem("x_in0"), sem("x_in1")]
        sq_done = sem("sq_done")
        inv_ready = sem("inv_ready")
        rstd_ready = sem("rstd_ready")
        h_ready = sem("h_ready")
        h_tr = sem("h_tr")
        hT_ready = sem("hT_ready")
        w_in = [sem("w_in0"), sem("w_in1")]
        z_mm = sem("z_mm")
        z_evac = sem("z_evac")
        z_stored = [sem("z_stored0"), sem("z_stored1")]
        dve_chain = sem("dve_chain")
        consts_in = sem("consts_in")
        c_in = sem("c_in")
        d_in = sem("d_in")
        pooled_ready = sem("pooled_ready")
        gc_in = sem("gc_in")
        gates = sem("gates")
        GATE_C, GATE_D, GATE_A, GATE_S, GATE_B = 0, 2, 4, 6, 7
        d_sig = sem("d_sig")
        glu_ready = sem("glu_ready")
        conv_done = sem("conv_done")
        gd_in = sem("gd_in")
        small_mm = sem("small_mm")
        small_read = sem("small_read")
        mix_stored = sem("mix_stored")
        out_stored = sem("out_stored")
        d_sq = sem("d_sq")
        d_inv = sem("d_inv")
        d_root = sem("d_root")
        d_norm = sem("d_norm")
        d_act = sem("d_act")
        sh_in = [sem("sh_in0"), sem("sh_in1")]
        sh_done = sem("sh_done")
        sh_stored = [sem("sh_stored0"), sem("sh_stored1")]
        ksq_ready = sem("ksq_ready")
        wa_ready = sem("wa_ready")
        kinv_pre = sem("kinv_pre")
        kinv_ready = sem("kinv_ready")
        lora_mm = sem("lora_mm")
        lora_read = sem("lora_read")
        rk_in = sem("rk_in")
        rkk_ready = sem("rkk_ready")
        rkk_stored = sem("rkk_stored")
        L_ready = sem("L_ready")
        exp_ready = sem("exp_ready")
        rw_ready = sem("rw_ready")
        rw_stored = sem("rw_stored")
        st_stored = sem("st_stored")

        w_v = I['w_in'][0].rearrange("(k p) c -> p k c", p=P)

        def slot_columns(p, u):
            if isinstance(p, int):
                if p == 9:
                    return (COL_GB1, COL_F)[u]
                if p == 13:
                    return COL_GA + P * u
            raise AssertionError

        def reads_through(g):
            return g + 1 + min(max(g + 1 - 10, 0), 5)

        kaug = area(0, 4, SEQ)
        vtok = area(HT + 19496, TT, 256)
        gate_a = area(4 * SEQ + TT * 256, 2, T_ALL)
        probs = zst
        probsT = (wbuf[:, :, :, :].rearrange("p a b c -> p (a b c)"), area(HT + 17448, SEQ))

        def tiles_of(i, j):
            return 2 * i + j // 4 + 1

        def bank_turned(i, g, j, k):
            return i * (8 * (g + 1)) + (j * (g + 1) + k + 1 - 8 * g * (g + 1))
        kvt = area(HT, 2, 4, P)
        kvs = area(HT + 1024, 2, 512)
        fx = area(HT + 2048, T_ALL)[0:4]
        fa = area(HT + 4128, T_ALL)[0:4]
        nc_ = area(HT + 6208, T_ALL)[0:4]
        ones_t = area(HT + 8288, SEQ)[0:4]
        qaug = area(HT + 10336, 2, 4, P)
        lg = area(HT + 11360, P)
        lbc = area(HT + 11488, P)
        lft = area(HT + 11616, TT, 4)
        kT_s = sb("kT_s", [P, 2, SMP])
        qT_s = sb("qT_s", [P, 2, SMP])
        kv_s = sb("kv_s", [SMP, 512])
        lf_s = sb("lf_s", [SMP, 8])
        bf_col = sb("bf_col", [4, 1])
        maskb = area(HT + 11700, (512 + 3 * P) // 2).bitcast(BF16)
        identb = area(HT + 12160, P // 2).bitcast(BF16)
        oc = area(HT + 12240, P)
        mx = sb("mx", [P, 2])
        nb = sb("nb", [P, 2])
        lsum = sb("lsum", [P, 2])
        linv = sb("linv", [P, 2])

        a_in = sem("a_in")
        kr_in = sem("kr_in")
        f_pre = sem("f_pre")
        f_abs = sem("f_abs")
        nl_ready = sem("nl_ready")
        nc_ready = sem("nc_ready")
        kvt_in = [sem("kvt_in0"), sem("kvt_in1")]
        kv_tr = sem("kv_tr")
        kv_copied = sem("kv_copied")
        v_kept = sem("v_kept")
        kv_stored = [sem("kv_stored0"), sem("kv_stored1")]
        f_tr = sem("f_tr")
        f_copied = sem("f_copied")
        kvs_tr = sem("kvs_tr")
        kvs_copied = sem("kvs_copied")
        q_in = [sem("q_in0"), sem("q_in1")]
        ga_in = sem("ga_in")
        qones_ready = sem("qones_ready")
        s_mm = sem("s_mm")
        s_max = sem("s_max")
        p_ready = sem("p_ready")
        p_tr = sem("p_tr")
        pT_ready = sem("pT_ready")
        o_mm = sem("o_mm")
        lb_ready = sem("lb_ready")
        lb_tr = sem("lb_tr")
        lg_ready = sem("lg_ready")
        o_read = sem("o_read")
        o_copied = sem("o_copied")
        mixa_stored = sem("mixa_stored")

        RHO, ALP, KTI, BTI, VAL = 0, 2, 4, 6, 8
        rin = area(0, 2, 10, P)
        tok_k = area(9984, 2, 256)
        tok_b = area(2560, 2, 256)
        tok_v = area(3072, 256)
        gb = area(3328, 4, 2, P)
        gk = area(4352, 4, 2, P)
        mpow = area(5376, 3, 4, P)
        mpowT = area(6912, 2, 4, P)
        sol = area(7936, 4, P)
        qT_r = area(8448, 2, P)
        trans = area(HT + 13704, 4, P)
        state = area(8960, 2 * 2 * 2, P)
        pcur = sb("pcur", [P, 2, 2])
        o_rw = area(10496, 2, T_ALL)
        mneg = area(HT + 13000, 2, P)
        mpos = area(HT + 13256, 2, P)
        mrow = area(HT + 13512, P)
        id64 = area(HT + 13640, 64)
        wkv_o = area(HT + 14216, 2, 64)
        s_wkv = area(HT + 14350, DEC_BATCH, 2 * 64)
        z_exp = area(0, 5, DEC_BATCH * 2 * 64)
        s_tmp = area(5120, DEC_BATCH * 2 * 64)
        s_tm2 = area(6144, DEC_BATCH * 2 * 64)
        s_kk = area(7168, 16)
        gn_sq = area(0, 2, T_ALL)
        gn_inv = area(4160, 2, T_ALL)
        g_rkk = area(14656, 2, T_ALL)
        g_v = area(18816, 2, T_ALL)
        gate_b = area(22976, 2, T_ALL)

        id64_ready = sem("id64_ready")
        r_in = [sem("r_in0"), sem("r_in1")]
        R = {n: sem("r_" + n) for n in ('gram_b', 'gram_k', 'gram_m', 'tok_tr', 'kv_mm', 'sqT_mm', 'sq_mm', 'app_mm', 'q_mm',
                                        'tr_mm', 'st_mm', 'o_mm', 'gb', 'gk', 'gm', 'tok', 'kv', 'sqT', 'sq', 'app', 'q',
                                        'tr', 'st', 'pcur', 'o')}
        state_zero = sem("state_zero")
        wkv_tr = sem("wkv_tr")
        wkv_copied = sem("wkv_copied")
        wkv_stored = sem("wkv_stored")
        s_in = sem("s_in")
        s_dec = sem("s_dec")
        s_z = sem("s_z")
        s_mm2 = sem("s_mm2")
        s_used = sem("s_used")
        s_done = sem("s_done")
        gn_in = sem("gn_in")
        gn_mm = sem("gn_mm")
        gn_read = sem("gn_read")
        gn_sq_ready = sem("gn_sq_ready")
        gn_pre = sem("gn_pre")
        gn_root = sem("gn_root")
        mixb_ready = sem("mixb_ready")

        NSLOT = 4
        lf_past = area(HT + 15400, DEC_BATCH * DT, TJ * 4)
        k_slot = area(HT + 17448, NSLOT, KV_ROW)
        v_slot = area(2048, NSLOT, KV_ROW)
        kT_d = area(10240, 2, 2, 512)
        s_rows = area(12288, DT * 512 + SMP)
        bias_w = area(HT + 11200, DT * 4, P)
        wo = area(HT, 8, D_MODEL)
        gf = area(HT + 8192, D_MODEL)
        mt = area(HT + 15296, 2, 8, P)
        later = area(HT + 25640, P)
        ones_a = area(HT + 25768, P)
        tot = area(HT + 25896, DEC_BATCH * DT * 4)
        zs = zst[:, :, :].rearrange("p a b -> p (a b)")
        bias = zs[:, 0:2048].rearrange("p (n c) -> p n c", c=TJ * 4)
        tsum = zs[:, 2048:2304]
        tsuf = zs[:, 2304:2560].rearrange("p (b t h) -> p b t h", b=DEC_BATCH, t=DT)
        nmask = zs[0:SMP, 2560:2688].rearrange("p (b c) -> p b c", c=16)
        v_new = zs[:, 2688:2944]
        qbd = zs[:, 2944:3072].rearrange("p (b r x) -> p b r x", r=2, x=8)
        nm_cur = zs[:, 3072:3200]
        q_cur = zs[:, 3200:3216].rearrange("p (r x) -> p r x", r=2)
        sel_r = zs[:, 3216:3232].rearrange("p (r x) -> p r x", r=2)
        p_new = zs[:, 3232:3248]
        sel = area(HT + 10752, 16)
        m8 = area(HT + 10768, DT + 1)
        m1 = area(HT + 10784, 1)
        neg_m = area(HT + 10785, 1)
        l_row = area(HT + 10786, 1)
        li = area(HT + 10817, 16)
        pv = area(HT + 10833, 256)
        o_s = area(HT + 11089, 2, SMP)
        yb = wbuf[:, :, :, :].rearrange("p a b c -> p a (b c)")
        wb = wbuf[:, :, :, :].rearrange("p a b c -> p (a b c)")
        pT_d = wb[:, 0:DT * 128].rearrange("p (c g x) -> p c g x", g=4, x=8)
        l_all = wb[:, 1024:1024 + P]
        m_row = wb[0:1, 1024 + P:1024 + 2 * P]
        m_half = wb[0:1, 1024 + 2 * P:1024 + 2 * P + 64]
        gate_s = sb("gate_s", [P, 2, SMP])
        pidx = sb("pidx", [P, DEC_BATCH * DT], I32)
        pidf = sb("pidf", [P, DEC_BATCH * DT])
        lane = sb("lane", [P, 1], I32)
        lanef = sb("lanef", [P, 1])

        idx_ready = sem("idx_ready")
        lf_in = sem("lf_in")
        k_in = [sem(f"k_in{n}") for n in range(NSLOT)]
        v_in = [sem(f"v_in{n}") for n in range(NSLOT)]
        tot_ready = sem("tot_ready")
        bias_ready = sem("bias_ready")
        after = dict(k_tr=('sqT_mm', 5), sc_mm=('sq_mm', 4), new_mm=('gram_b', 1), m_tr=('gram_k', 1), m_mm=('gram_m', 1),
                     pv_mm=('app_mm', 6), o_mm=('o_mm', 1), y_mm=('q_mm', 1), p_tr=('tok_tr', 1), b_mm=('tr_mm', 1),
                     prep=('gb', 1), pT=('gk', 1), m1=('gm', 1), m_row=('pcur', 1), neg_m=('kv', 1), l_all=('sqT', 5), pv=('app', 6),
                     li=('q', 1), o=('st', 4), y_sum=('tr', 2), s=('tok', 6), p=('sq', 4), kT1=('o', 1))
        D = {n: R[old] for n, (old, per) in after.items()}
        D0 = {n: per * TT for n, (old, per) in after.items()}
        D['kT0'], D0['kT0'] = sem("d_kT0"), 0
        mixas_ready = sem("mixas_ready")

        def samples(row):
            return row[:, SEQ:T_ALL].rearrange("p (b i) -> p b i", i=DEC_SEQ)

        def history(row, start, width):
            return row[:, start:start + DEC_BATCH * width].rearrange("p (b w) -> p b w", w=width)

        def shifted_samples(row):
            return history(row, SEQ + 1, SHIFT_S)[:, :, 0:DEC_SEQ]

        block = ctx.enter_context(nc.Block())

        @block.sync
        def _(sp):
            for r, name in enumerate(ROWS256):
                src = I[name][0].rearrange("h d -> (h d)") if name == 'rw_rk' else I[name][0]
                sp.dma_start(rows256[r:r + 1, :], src.rearrange("(o c) -> o c", o=1)).then_inc(rows_in, 16)
            sp.dma_start(rows256[PCW:NROW, :], I['conv_w'][0]).then_inc(rows_in, 16)
            sp.dma_start(rows128[0:8, :], I['norm_g'][0].rearrange("(k p) -> k p", p=P)).then_inc(rows_in, 16)
            sp.dma_start(rows128[8:15, :], I['rw_mu'][0].rearrange("(k p) -> k p", p=P)).then_inc(rows_in, 16)
            sp.dma_start(st_rows[:, 0, :], I['state_pool'].rearrange("b l s c -> (b l s) c")).then_inc(rows_in, 16)
            conv_rows = I['state_conv'].rearrange("b l s c -> (b l s) c")
            sp.dma_start(st_rows[:, 1, :], conv_rows[0:120, :]).then_inc(rows_in, 16)
            sp.dma_start(st_rows[:, 2, :], conv_rows[120:240, :]).then_inc(rows_in, 16)
            sp.dma_start(sh_rows[:, :], I['state_shift'].rearrange("b l c -> (b l) c")).then_inc(rows_in, 16)
            xp = I['x_prompt'][0]
            xs = I['x_sample'].rearrange("b t d -> (b t) d")
            for u in range(2):
                sp.dma_start(xt[:, u, :], xp[u * P:(u + 1) * P, :]).then_inc(x_in[u], 16)
            for u in range(2):
                sp.dma_start(wbuf[:, u], w_v[:, :, COL_CD + u * P:COL_CD + (u + 1) * P]).then_inc(w_in[u], 16)
            with sp.Fori(1, TT // 2) as i:
                for u in range(2):
                    sp.wait_ge(h_ready, i * 2 + (u - 1))
                    sp.dma_start(xt[:, u, :], xp[bass.ds(i * 2 * P + u * P, P), :]).then_inc(x_in[u], 16)
            sp.wait_ge(h_ready, TT - 1)
            sp.dma_start(xt[0:SMP, 0, :], xs).then_inc(x_in[0], 16)

            def weights(p, col, u):
                sp.wait_ge(z_mm, p * 10 + (5 * u - 5))
                sp.dma_start(wbuf[:, u], w_v[:, :, bass.ds(col, P)]).then_inc(w_in[u], 16)

            with sp.Fori(1, 5) as p:
                for u in range(2):
                    weights(p, p * (2 * P) + (COL_CD + P * u), u)
            with sp.Fori(5, 9) as p:
                for u in range(2):
                    weights(p, p * (2 * P) + (COL_B + P * u - 10 * P), u)
            for u in range(2):
                weights(9, slot_columns(9, u), u)
            with sp.Fori(10, 13) as p:
                for u in range(2):
                    weights(p, p * (2 * P) + (P * u - 20 * P), u)
            for u in range(2):
                weights(13, slot_columns(13, u), u)
            pt = I['page_table'].rearrange("b (t n) -> n (b t)", n=PT)
            for n in range(PT):
                sp.dma_start(pidx[n * RT:(n + 1) * RT, :], pt[n:n + 1, :].to_broadcast([RT, DEC_BATCH * DT])).then_inc(rows_in, 16)
            sp.dma_start(bf_col[:, :], I['fox_bf'][0].rearrange("(h o) -> h o", o=1)).then_inc(rows_in, 16)
            sp.wait_ge(rw_stored, 128)
            sp.dma_start(fx, zT[FG][0:4, :]).then_inc(rows_in, 16)
            for u in range(2):
                sp.wait_ge(z_stored[u], 16 * 13)

            def kv_load(col, n, u):
                sp.dma_start(kvt[:, u, :, 0:n], zT[KA:KA + 4, :, bass.ds(col, n)].rearrange("s p t -> p s t")).then_inc(kvt_in[u], 16)

            def kv_store(i, u):
                for j, name in enumerate(('k_prompt', 'v_prompt')):
                    rows = O[name][0, 0].rearrange("t h d -> t (h d)")
                    sp.dma_start(rows[bass.ds(i * (2 * P) + u * P, P), :], kvs[:, u, j * 256:(j + 1) * 256]).then_inc(kv_stored[u], 16)

            for u in range(2):
                kv_load(u * P, P, u)
            for u in range(2):
                sp.wait_ge(kv_tr, u + 1)
                kv_load((2 + u) * P, P, u)
            for u in range(2):
                sp.wait_ge(kv_copied, u + 1)
                kv_store(0, u)
            with sp.Fori(1, TT // 2 - 1) as i:
                for u in range(2):
                    sp.wait_ge(kv_tr, i * 2 + (u + 1))
                    kv_load(i * (2 * P) + (2 + u) * P, P, u)
                    sp.wait_ge(kv_copied, i * 2 + (u + 1))
                    kv_store(i, u)
            sp.wait_ge(kv_tr, TT - 1)
            kv_load(SEQ, SMP, 0)
            for u in range(2):
                sp.wait_ge(kv_copied, TT - 1 + u)
                kv_store(TT // 2 - 1, u)
            sp.wait_ge(z_mm, 10 * 14)
            for t in range(2):
                sp.dma_start(qT_s[:, t, :], zT[QA + t][:, SEQ:T_ALL]).then_inc(a_in, 16)
                sp.dma_start(kT_s[:, t, :], zT[KA + t][:, SEQ:T_ALL]).then_inc(a_in, 16)
                sp.dma_start(kaug[0:64, 2 * t:2 * t + 2, :],
                             zT[KA + t][:, 0:SEQ].rearrange("(h p) t -> p h t", p=64)).then_inc(a_in, 16)
            sp.wait_ge(nc_ready, 1)
            for h in range(4):
                sp.dma_start(kaug[64:65, h, :], nc_[h:h + 1, 0:SEQ]).then_inc(kr_in, 16)

            def q_load(col, u):
                sp.dma_start(qaug[0:64, u, :, :], zT[QA:QA + 2, :, bass.ds(col, P)].rearrange("s (h p) t -> p (s h) t", p=64)).then_inc(q_in[u], 16)

            for u in range(2):
                q_load(u * P, u)
            for t in range(2):
                sp.wait_ge(z_stored[t], 16 * 14)
                sp.dma_start(gate_a[:, t, :], zT[GA + t]).then_inc(ga_in, 16)
            sp.wait_ge(kvs_copied, 1)
            for j, name in enumerate(('k_sample', 'v_sample')):
                sp.dma_start(O[name].rearrange("b l t h d -> (b l t) (h d)"), kv_s[:, j * 256:(j + 1) * 256]).then_inc(st_stored, 16)
            sp.wait_ge(f_copied, 2)
            sp.dma_start(O['logf_prompt'][0, 0].rearrange("(n p) h -> p n h", p=P), lft[:, :, :]).then_inc(st_stored, 16)
            sp.dma_start(O['logf_sample'].rearrange("b l t h -> (b l t) h"), lf_s[:, 0:4]).then_inc(st_stored, 16)
            sp.dma_start(O['pool_sample'][:, 0, 0:POOL_BUF - DEC_SEQ, :], I['state_pool'][:, 0, DEC_SEQ:, :]).then_inc(st_stored, 16)
            sp.dma_start(O['conv_sample'][:, 0, 0:CONV_BUF - DEC_SEQ, :], I['state_conv'][:, 0, DEC_SEQ:, :]).then_inc(st_stored, 16)
            for n in range(7):
                cs = slice(n * P, (n + 1) * P)
                sp.dma_start(O['shift_prompt'][0, :, cs].rearrange("o p -> p o"), zT[R0 + n][:, SEQ - 1:SEQ]).then_inc(st_stored, 16)
                sp.dma_start(O['shift_sample'][:, 0, cs].rearrange("b p -> p b"),
                             zT[R0 + n][:, SEQ:T_ALL].rearrange("p (b i) -> p b i", i=DEC_SEQ)[:, :, DEC_SEQ - 1]).then_inc(st_stored, 16)
            with sp.Fori(1, TT // 2) as i:
                for u in range(2):
                    sp.wait_ge(s_mm, i * 8 + (4 * u - 4))
                    q_load(i * (2 * P) + u * P, u)
            sp.wait_ge(o_read, 2 * TT)
            for t in range(2):
                sp.dma_start(mixT[MIX_A + t][:, 0:SEQ], gate_a[:, t, 0:SEQ]).then_inc(mixa_stored, 16)
            sp.wait_ge(mixa_stored, 32)

            def chunk_load(col, u):
                sp.dma_start(rin[:, u, 0:8, :], rwS.rearrange("m t p c -> p (m t) c")[:, :, bass.ds(col, P)]).then_inc(r_in[u], 16)
                sp.dma_start(rin[:, u, 8:10, :], rkv[4:6].rearrange("t p c -> p t c")[:, :, bass.ds(col, P)]).then_inc(r_in[u], 16)

            for u in range(2):
                chunk_load(u * P, u)
            for t in range(2):
                sp.dma_start(s_wkv[:, :, t * 64:(t + 1) * 64],
                             I['state_wkv'][:, 0, 2 * t:2 * t + 2].rearrange("b h v k -> (h v) b k")).then_inc(s_in, 16)
                sp.dma_start(g_rkk[:, t, :], rkk[t]).then_inc(gn_in, 16)
                sp.dma_start(g_v[:, t, :], rkv[4 + t]).then_inc(gn_in, 16)
                sp.dma_start(gate_b[:, t, :], zT[GB0 + t]).then_inc(gn_in, 16)
            with sp.Fori(1, TT // 2) as i:
                for u in range(2):
                    sp.wait_ge(R['q'], i * 2 + (u - 1))
                    chunk_load(i * (2 * P) + u * P, u)
            sp.wait_ge(wkv_copied, 2)
            sp.dma_start(O['wkv_prompt'][0, 0].rearrange("(t h) v k -> (h v) t k", h=2), wkv_o[:, :, :]).then_inc(wkv_stored, 16)
            sp.wait_ge(s_done, 1)
            for t in range(2):
                sp.dma_start(O['wkv_sample'][:, 0, 2 * t:2 * t + 2].rearrange("b h v k -> (h v) b k"),
                             s_wkv[:, :, t * 64:(t + 1) * 64]).then_inc(wkv_stored, 16)
            for t in range(2):
                sp.wait_ge(mixb_ready, t + 1)
                sp.dma_start(mixT[MIX_B + t], o_rw[:, t, :]).then_inc(mixa_stored, 16)
            sp.dma_start(wo[:, :, :], I['w_out'][0].rearrange("(e p) d -> p e d", p=P)).then_inc(rows_in, 16)
            sp.dma_start(gf[:, :], I['final_norm_g'].unsqueeze(0).to_broadcast([P, D_MODEL])).then_inc(rows_in, 16)
            sp.wait_ge(mixa_stored, 32 + 32)
            sp.wait_ge(wkv_stored, 48)
            sp.wait_ge(bias_ready, 1)
            for u in range(2):
                sp.dma_start(mt[:, u], mixT.rearrange("e p t -> p e t")[:, :, u * P:(u + 1) * P]).then_inc(q_in[u], 16)
            sp.wait_ge(mixas_ready, 1)
            for u in range(2):
                sp.dma_start(zst[:, u, 0:D_MODEL], xp[u * P:(u + 1) * P, :]).then_inc(kvt_in[u], 16)
            for t in range(2):
                sp.dma_start(mixT[MIX_A + t][:, SEQ:T_ALL], o_s[:, t, :]).then_inc(mixa_stored, 16)
            sp.wait_ge(mixa_stored, 64 + 32)

            for u in range(2):
                sp.wait_ge(kv_stored[u], 32 * (TT // 2))

            def y_out(rows, u, n=P):
                sp.dma_start(rows, yb[0:n, u, :]).then_inc(kv_stored[u], 16)

            yp = O['y_prompt'][0]
            with sp.Fori(1, TT // 2) as i:
                for u in range(2):
                    sp.wait_ge(D['y_mm'], D0['y_mm'] + i * 2 + (u - 1))
                    sp.dma_start(mt[:, u], mixT.rearrange("e p t -> p e t")[:, :, bass.ds(i * (2 * P) + u * P, P)]).then_inc(q_in[u], 16)
                for u in range(2):
                    sp.wait_ge(h_ready, (TT + 1) + i * 2 + (u - 1))
                    y_out(yp[bass.ds(i * (2 * P) + (u - 2) * P, P), :], u)
                    sp.dma_start(zst[:, u, 0:D_MODEL], xp[bass.ds(i * (2 * P) + u * P, P), :]).then_inc(kvt_in[u], 16)
            sp.wait_ge(D['y_mm'], D0['y_mm'] + TT - 1)
            sp.dma_start(mt[:, 0, :, 0:SMP], mixT.rearrange("e p t -> p e t")[:, :, SEQ:T_ALL]).then_inc(q_in[0], 16)
            for u in range(2):
                sp.wait_ge(h_ready, (TT + 1) + TT - 1 + u)
                y_out(yp[SEQ - (2 - u) * P:SEQ - (1 - u) * P, :], u)
                if u == 0:
                    sp.dma_start(zst[0:SMP, 0, 0:D_MODEL], xs).then_inc(kvt_in[0], 16)
            sp.wait_ge(h_ready, (TT + 1) + TT + 1)
            y_out(O['y_sample'].rearrange("b t d -> (b t) d"), 0, SMP)
            sp.wait_ge(kv_stored[0], 32 * (TT // 2) + 16 * (TT // 2 + 1))
            sp.wait_ge(kv_stored[1], 32 * (TT // 2) + 16 * (TT // 2))
            sp.wait_ge(st_stored, 16 * 20)
            sp.wait_ge(out_stored, 16 * 20)
            sp.wait_ge(mix_stored, 64)
            sp.wait_ge(rw_stored, 128)
            sp.wait_ge(rkk_stored, 32)

        @block.gpsimd
        def _(pool):
            nc.gpsimd.memset(ident[:], 0.0).then_inc(made, 1)
            pool.wait_ge(made, IDENT + 1)
            nc.gpsimd.affine_select(out=ident[:], in_=ident[:], compare_op=ALU.not_equal, fill=1.0, base=0,
                                    pattern=[[-1, P]], channel_multiplier=1).then_inc(made, 1)
            g = nc.gpsimd
            g.memset(ones_ln[:], 1.0 / 256).then_inc(made, 1)
            g.memset(ones_head[:], 0.0).then_inc(made, 1)
            g.memset(pw_diag[:], 0.0).then_inc(made, 1)
            g.memset(lora[:], 0.0).then_inc(made, 1)
            pool.wait_ge(made, ONES + 4)
            for h in range(2):
                g.memset(ones_head[h * 64:h * 64 + 64, h * 64:h * 64 + 64], 1.0).then_inc(made, 1)
            for q in range(4):
                t, h = q // 2, q % 2
                pool.dma_start(pw_diag[h * 64:h * 64 + 64, t, h * 64:h * 64 + 64], I['pool_w'][0, q]).then_inc(consts_in, 16)
            pool.dma_start(pwo[:, :, :], I['pw_out'][0].rearrange("(t p) o -> p t o", p=P)).then_inc(consts_in, 16)
            pool.dma_start(lora[0:64, 0, :], I['rw_wup'][0]).then_inc(consts_in, 16)
            pool.dma_start(lora[64:P, 1, :], I['rw_aup'][0]).then_inc(consts_in, 16)
            pool.wait_ge(made, ONES + 6)
            g.iota(cnt[:, :, :], pattern=[[0, 2], [1, 16]], base=1, channel_multiplier=0,
                   allow_small_or_imprecise_dtypes=True).then_inc(made, 1)
            for t in range(2):
                g.memset(ext_c[:, t, 0:POOL_BUF], 0.0).then_inc(made, 1)
                g.memset(ext_d[:, t, 0:CONV_BUF], 0.0).then_inc(made, 1)

            def z_ready(slot):
                pool.wait_ge(z_stored[slot % 2], 16 * (slot // 2 + 1))

            def load_ext(dst, slot, buf, width, s):
                z_ready(slot)
                pool.dma_start(dst[:, buf:buf + SEQ], zT[slot][:, 0:SEQ]).then_inc(s, 16)
                pool.dma_start(history(dst, buf + SEQ, width)[:, :, buf:buf + DEC_SEQ], samples(zT[slot])).then_inc(s, 16)

            for t in range(2):
                load_ext(ext_c[:, t], UC0 + t, POOL_BUF, POOL_S, c_in)
            for t in range(2):
                load_ext(ext_d[:, t], U1D + t, CONV_BUF, CONV_S, d_in)
            pool.wait_ge(hT_ready, TT + 1)
            for t in range(2):
                z_ready(U2D + t)
                pool.dma_start(u2d[:, t, :], zT[U2D + t]).then_inc(d_in, 16)

            pool.wait_ge(glu_ready, 6)
            for t in range(2):
                cs = slice(t * P, (t + 1) * P)
                pool.dma_start(O['pool_prompt'][0, 0, :, cs].rearrange("s p -> p s"), ext_c[:, t, SEQ:SEQ + POOL_BUF]).then_inc(out_stored, 16)
                for i in range(DEC_SEQ):
                    pool.dma_start(O['pool_sample'][:, 0, POOL_BUF - DEC_SEQ + i, cs].rearrange("b p -> p b"),
                                   history(ext_c[:, t], POOL_BUF + SEQ, POOL_S)[:, :, POOL_BUF + i]).then_inc(out_stored, 16)
                pool.dma_start(O['conv_prompt'][0, 0, :, cs].rearrange("s p -> p s"), ext_d[:, t, SEQ:SEQ + CONV_BUF]).then_inc(out_stored, 16)
                for i in range(DEC_SEQ):
                    pool.dma_start(O['conv_sample'][:, 0, CONV_BUF - DEC_SEQ + i, cs].rearrange("b p -> p b"),
                                   history(ext_d[:, t], CONV_BUF + SEQ, CONV_S)[:, :, CONV_BUF + i]).then_inc(out_stored, 16)

            pool.wait_ge(pooled_ready, 2)
            for t in range(2):
                z_ready(GC0 + t)
                pool.dma_start(gate_c[:, t, :], zT[GC0 + t]).then_inc(gc_in, 16)
            pool.wait_ge(glu_ready, 6)
            for t in range(2):
                z_ready(GD0 + t)
                pool.dma_start(gate_d[:, t, :], zT[GD0 + t]).then_inc(gd_in, 16)
            pool.wait_ge(small_read, reads_through(9))
            for t in range(2):
                pool.dma_start(mixT[MIX_C + t], pooled[:, t, :]).then_inc(mix_stored, 16)

            pool.wait_ge(out_stored, 16 * 20)
            for n in range(9):
                if n < 7:
                    if n >= 2:
                        pool.wait_ge(sh_done, n - 1)
                    load_ext(sh_ext[:, n % 2], R0 + n, 1, SHIFT_S, sh_in[n % 2])
                if n >= 2 and n - 2 < 6:
                    m = n - 2
                    pool.wait_ge(sh_done, m + 1)
                    pool.dma_start(rkv[m][:, 0:SEQ], sh_mix[:, m % 2, 0:SEQ]).then_inc(sh_stored[m % 2], 16)
                    pool.dma_start(samples(rkv[m]), shifted_samples(sh_mix[:, m % 2])).then_inc(sh_stored[m % 2], 16)

            pool.wait_ge(small_read, reads_through(29))
            for t in range(2):
                pool.dma_start(mixT[MIX_D + t], conv[:, t, :]).then_inc(mix_stored, 16)

            pool.wait_ge(mix_stored, 64)
            pool.wait_ge(sh_stored[0], 96)
            pool.wait_ge(sh_stored[1], 96)
            for t in range(2):
                pool.dma_start(rw_r[:, :], rkv[t]).then_inc(rk_in, 16)
                pool.dma_start(rw_k[:, :], rkv[2 + t]).then_inc(rk_in, 16)
                pool.dma_start(smp[:, 5, t, :], rkv[4 + t][:, SEQ:T_ALL]).then_inc(rk_in, 16)
                pool.wait_ge(rkk_ready, t + 1)
                pool.dma_start(rkk[t], rw_t[:, :]).then_inc(rkk_stored, 16)
                for n, (m, src) in enumerate(((1, rw_kk), (0, rw_r), (2, rw_k), (3, rate[:, t]))):
                    pool.wait_ge(rw_ready, 4 * t + n + 1)
                    pool.dma_start(rwS[m, t], src[:, 0:SEQ]).then_inc(rw_stored, 16)
                pool.wait_ge(rw_stored, 64 * (t + 1))

            for m, val in ((mneg, -1.0), (mpos, 1.0)):
                g.memset(m[:, :, :], val).then_inc(made, 1)
            g.memset(mrow[:, :], -1.0).then_inc(made, 1)
            pool.wait_ge(made, RMASKS + 3)
            for m in (mneg, mpos):
                for n in range(2):
                    g.affine_select(out=m[:, n, :], in_=m[:, n, :], compare_op=ALU.is_ge, fill=0.0, base=-n,
                                    pattern=[[1, P]], channel_multiplier=-1).then_inc(made, 1)
            g.affine_select(out=mrow[:, :], in_=mrow[:, :], compare_op=ALU.is_ge, fill=0.0, base=-1,
                            pattern=[[-1, P]], channel_multiplier=1).then_inc(made, 1)
            pool.wait_ge(made, RMASKS + 8)
            for m in (mneg, mpos):
                g.memset(m[0:64, :, 64:P], 0.0).then_inc(made, 1)
            g.memset(mrow[64:P, 0:64], 0.0).then_inc(made, 1)
            pool.wait_ge(made, RMASKS + 11)
            g.memset(maskb[:, :], 0.0).then_inc(made, 1)
            pool.wait_ge(made, MASKS + 1)
            g.affine_select(out=maskb[:, :], in_=maskb[:, :], compare_op=ALU.is_ge, fill=-1e30, base=3 * P,
                            pattern=[[-1, 512 + 3 * P]], channel_multiplier=1).then_inc(made, 1)
            g.memset(identb[:, :], 0.0).then_inc(made, 1)
            pool.wait_ge(made, MASKS + 3)
            g.affine_select(out=identb[:, :], in_=identb[:, :], compare_op=ALU.not_equal, fill=1.0, base=0,
                            pattern=[[-1, P]], channel_multiplier=1).then_inc(made, 1)

            g.iota(lane[:, :], pattern=[[0, 1]], base=0, channel_multiplier=1).then_inc(made, 1)
            g.memset(later[:, :], 1.0).then_inc(made, 1)
            g.memset(ones_a[:, :], 1.0).then_inc(made, 1)
            pool.wait_ge(made, DCONST + 2)
            g.affine_select(out=later[:, :], in_=later[:, :], compare_op=ALU.is_ge, fill=0.0, base=-1,
                            pattern=[[-1, P]], channel_multiplier=1).then_inc(made, 1)
            pool.wait_ge(idx_ready, 1)

            def gather(dst, cache, bt, s):
                g.indirect_dma_start(out=dst, out_offset=None, in_=cache,
                                     in_offset=bass.IndirectOffsetOnAxis(ap=pidx[:, bt:bt + 1], axis=0)).then_inc(s, 16)

            ck = I['cache_k'].rearrange("n l (r j) h d -> (n l r) (j h d)", r=RT)
            cv = I['cache_v'].rearrange("n l (r j) h d -> (n l r) (j h d)", r=RT)
            cf = I['cache_logf'].rearrange("n l (r j) h -> (n l r) (j h)", r=RT)
            for bt in range(DEC_BATCH * DT):
                gather(lf_past[:, bt, :], cf, bt, lf_in)

            def gather_k(b, t):
                if b * DT + t >= NSLOT:
                    pool.wait_ge(D['k_tr'], D0['k_tr'] + 2 * (b * DT + t - NSLOT) + 2)
                gather(k_slot[:, t % NSLOT, :], ck, b * DT + t, k_in[t % NSLOT])

            def gather_v(b, t):
                if b * DT + t >= NSLOT:
                    pool.wait_ge(D['pv_mm'], D0['pv_mm'] + b * DT + t - NSLOT + 1)
                gather(v_slot[:, t % NSLOT, :], cv, b * DT + t, v_in[t % NSLOT])

            pool.wait_ge(mixa_stored, 32)
            for t in range(NSLOT):
                gather_k(0, t)
            g.memset(nmask[:, :, :], 0.0).then_inc(made, 1)
            g.memset(qbd[:, :, :, :], 0.0).then_inc(made, 1)
            g.memset(v_new[:, :], 0.0).then_inc(made, 1)
            g.memset(nm_cur[:, :], 0.0).then_inc(made, 1)
            g.memset(p_new[:, :], 0.0).then_inc(made, 1)
            pool.wait_ge(made, DCONST + 8)
            g.memset(nm_cur[0:SMP, 64:P], -1e30).then_inc(made, 1)
            nm = nmask[:, :, :].rearrange("p b (h q) -> p b h q", h=4)
            g.affine_select(out=nm, in_=nm, compare_op=ALU.is_ge, fill=-1e30, base=0,
                            pattern=[[-DEC_SEQ, DEC_BATCH], [0, 4], [0, DEC_SEQ]], channel_multiplier=1).then_inc(made, 1)
            pool.wait_ge(made, DCONST + 10)
            g.affine_select(out=nm, in_=nm, compare_op=ALU.is_ge, fill=-1e30, base=0,
                            pattern=[[DEC_SEQ, DEC_BATCH], [0, 4], [1, DEC_SEQ]], channel_multiplier=-1).then_inc(made, 1)
            pool.wait_ge(wkv_stored, 48)
            g.memset(bias_w[:, :, :], 0.0).then_inc(made, 1)
            for t in range(NSLOT, DT):
                gather_k(0, t)
            pool.wait_ge(mixa_stored, 32 + 32)
            for b in range(1, DEC_BATCH + 1):
                for t in range(DT + 1):
                    if t < DT and b < DEC_BATCH:
                        gather_k(b, t)
                    if t > 0:
                        gather_v(b - 1, t - 1)

        @block.tensor
        def _(pe):
            def transpose(out, in_):
                k = in_.shape[0]
                return nc.tensor.transpose(out, in_, ident[0:k, 0:k])

            pe.wait_ge(made, IDENT + 2)
            pe.wait_ge(rows_in, 16 * (len(ROWS256) + 7))
            for t in range(2):
                cs = slice(t * P, (t + 1) * P)
                transpose(psum[:, 5, t * NROW:(t + 1) * NROW], rows256[:, cs])
                transpose(psum[:, 5, 160 + t * 120:280 + t * 120], st_rows[:, 0, cs])
                for hf in range(2):
                    transpose(psum[:, 6, t * 240 + hf * 120:t * 240 + hf * 120 + 120], st_rows[:, 1 + hf, cs])
            transpose(psum[:, 5, 84:99], rows128[:, :])
            for t in range(7):
                last = transpose(psum[:, 5, 100 + 8 * t:108 + 8 * t], sh_rows[:, t * P:(t + 1) * P])
            last.then_inc(par_tr, 1)

            def h_tile(u, rows):
                for k in range(KT):
                    last = transpose(psum[:, 2 * u + k // 4, (k % 4) * P:(k % 4) * P + rows],
                                     xh[0:rows, u, k * P:(k + 1) * P])
                last.then_inc(h_tr, 1)

            for u in range(2):
                pe.wait_ge(h_ready, u + 1)
                h_tile(u, P)
            with pe.Fori(1, TT // 2) as i:
                for u in range(2):
                    pe.wait_ge(h_ready, i * 2 + (u + 1))
                    pe.wait_ge(hT_ready, i * 2 + (u - 1))
                    h_tile(u, P)
            pe.wait_ge(h_ready, TT + 1)
            pe.wait_ge(hT_ready, TT - 1)
            h_tile(0, SMP)
            pe.wait_ge(hT_ready, TT + 1)

            def chunk(p, u, c):
                if c == 0:
                    pe.wait_ge(w_in[u], p * 16 + 16)
                if not (isinstance(p, int) and p == 0 and u == 0):
                    pe.wait_ge(z_evac, p * 10 + (5 * u + c - 4))
                for k in range(KT):
                    last = nc.tensor.matmul(psum[:, c, 0:CW], wbuf[:, u, k, :],
                                            hT[:, k, c * CW:(c + 1) * CW], start=(k == 0), stop=(k == KT - 1))
                last.then_inc(z_mm, 1)

            def pair(p):
                for u in range(2):
                    for c in range(CHUNKS):
                        chunk(p, u, c)

            small = [0]

            def small_group(mms, w=CW):
                g = small[0]
                if g >= 3:
                    pe.wait_ge(small_read, reads_through(g - 3))
                elif g == 0:
                    pe.wait_ge(par_ready, 5)
                for n, (l, r) in enumerate(mms):
                    last = nc.tensor.matmul(psum[:, 5 + g % 3, 0:w], l, r, start=(n == 0), stop=(n == len(mms) - 1))
                last.then_inc(small_mm, 1)
                small[0] += 1

            def pool_post():
                pe.wait_ge(made, ONES + 6)
                pe.wait_ge(consts_in, 16 * 7)
                pe.wait_ge(pooled_ready, 2)
                for t in range(2):
                    for c in range(CHUNKS):
                        small_group([(pw_diag[:, t, :], pooled[:, t, c * CW:(c + 1) * CW])])

            def conv_post():
                pe.wait_ge(conv_done, CONV_WIDTH * 4)
                for c in range(CHUNKS):
                    small_group([(ones_ln[:, :], conv[:, t, c * CW:(c + 1) * CW]) for t in range(2)])
                for c in range(CHUNKS):
                    pe.wait_ge(d_sq, 2 * c + 2)
                    small_group([(ones_ln[:, :], ln_sq[:, t, c * CW:(c + 1) * CW]) for t in range(2)])

            def conv_out():
                for c in range(CHUNKS):
                    pe.wait_ge(d_act, 2 * c + 2)
                    for o in range(2):
                        small_group([(pwo[:, t, o * P:(o + 1) * P], ln_sq[:, t, c * CW:(c + 1) * CW]) for t in range(2)])

            def key_norm(n):
                t, c = n // CHUNKS, n % CHUNKS
                if n == 0:
                    pe.wait_ge(ksq_ready, 4)
                small_group([(ones_head[:, :], ksq[:, t, c * CW:(c + 1) * CW])])

            def loras():
                pe.wait_ge(wa_ready, 4)
                pe.wait_ge(small_read, reads_through(39))
                n = 0
                for m in range(2):
                    for t in range(2):
                        for c in range(CHUNKS):
                            if n >= 3:
                                pe.wait_ge(lora_read, n - 2)
                            nc.tensor.matmul(psum[:, 5 + n % 3, 0:CW], lora[:, m, t * P:(t + 1) * P],
                                             wa[:, c * CW:(c + 1) * CW], start=True, stop=True).then_inc(lora_mm, 1)
                            n += 1

            pair(0)
            with pe.Fori(1, 5) as p:
                pair(p)
            with pe.Fori(5, 7) as p:
                pair(p)
            pair(7)
            pool_post()
            pair(8)
            pair(9)
            conv_post()
            for c in range(CHUNKS):
                chunk(10, 0, c)
            conv_out()
            for c in range(CHUNKS):
                chunk(10, 1, c)
                key_norm(2 * c)
                key_norm(2 * c + 1)
            loras()
            with pe.Fori(11, 13) as p:
                pair(p)

            def kv_tile(u, n):
                for m in range(4):
                    last = transpose(psum[0:n, 5 + u, m * P:(m + 1) * P], kvt[:, u, m, 0:n])
                return last

            pe.wait_ge(lora_read, 20)
            for m in range(2 * CHUNKS):
                chunk(13, m // CHUNKS, m % CHUNKS)
                n = m - 2
                if n >= 0:
                    for u in range(2):
                        pe.wait_ge(kvt_in[u], n * 16 + 16)
                        if n > 0:
                            pe.wait_ge(kv_copied, n * 2 + u - 1)
                        kv_tile(u, P).then_inc(kv_tr, 1)
            pe.wait_ge(kvt_in[0], 16 * (TT // 2 + 1))
            pe.wait_ge(kv_copied, TT - 1)
            kv_tile(0, SMP).then_inc(kvs_tr, 1)
            pe.wait_ge(nl_ready, 2)
            for n in range(TT):
                transpose(psum[:, 7, 4 * n:4 * n + 4], fa[:, n * P:(n + 1) * P])
            pe.wait_ge(nc_ready, 1)
            transpose(psum[0:SMP, 7, 64:68], fa[:, SEQ:T_ALL])
            transpose(psum[0:SMP, 7, 68:72], nc_[:, SEQ:T_ALL]).then_inc(f_tr, 1)

            pe.wait_ge(z_evac, 10 * 14)
            pe.wait_ge(f_copied, 2)
            pe.wait_ge(kvs_copied, 1)
            pe.wait_ge(kv_copied, TT)
            pe.wait_ge(v_kept, TT)
            pe.wait_ge(a_in, 16 * 6)
            pe.wait_ge(kr_in, 64)
            pe.wait_ge(made, MASKS + 4)
            pe.wait_ge(qones_ready, 1)

            def scores(i, g, j):
                w, u, h = j % 2, j // 4, j % 4
                if h == 0:
                    pe.wait_ge(q_in[u], i * 16 + 16)
                n = tiles_of(i, j) * P
                for c in range(g + 1):
                    nc.tensor.matmul(psum[:, 4 * w + c, 0:min(512, n - c * 512)], qaug[0:65, u, h, :], kaug[0:65, h, c * 512:min(n, (c + 1) * 512)],
                                     start=True, stop=(c < g))
                w_ = n - g * 512
                nc.tensor.matmul(psum[:, 4 * w + g, 0:w_], identb[:, :], maskb[:, 4 * P - w_:4 * P],
                                 start=False, stop=True).then_inc(s_mm, 1)

            def turn(i, g, j):
                w = j % 2
                pe.wait_ge(p_ready, i * 8 + (j + 1))
                n = tiles_of(i, j)
                for k in range(n):
                    last = transpose(psum[:, 4 * w + k // 4, (k % 4) * P:(k % 4 + 1) * P], probs[:, w, k * P:(k + 1) * P])
                    if k % 4 == 3 or k == n - 1:
                        last.then_inc(p_tr, 1)

            def values(i, g, n):
                m = tiles_of(i, 2 * n)
                for k in range(m):
                    if k % 4 == 0:
                        pe.wait_ge(pT_ready, bank_turned(i, g, 2 * n + 1, k // 4))
                    for w in range(2):
                        h = (2 * n + w) % 4
                        last = nc.tensor.matmul(psum[w * 64:w * 64 + 64, 4, 0:P], vtok[:, k, h * 64:(h + 1) * 64],
                                                probsT[w][:, k * P:(k + 1) * P], start=(k == 0), stop=(k == m - 1),
                                                tile_position=(0, w * 64), skip_group_check=True)
                last.then_inc(o_mm, 1)
                pe.wait_ge(lb_ready, i * 4 + (n + 1))
                transpose(psum[:, 7, 0:P], lbc[:, :]).then_inc(lb_tr, 1)

            def attention(i, g, first):
                for n in range(4):
                    if n > 0:
                        pe.wait_ge(pT_ready, bank_turned(i, g, 2 * n - 2, g))
                    elif not first:
                        pe.wait_ge(o_copied, i * 4)
                    scores(i, g, 2 * n)
                    if n > 0:
                        turn(i, g, 2 * n - 1)
                        values(i, g, n - 1)
                    if not (first and n == 0):
                        pe.wait_ge(o_copied, i * 4 + n)
                        pe.wait_ge(lg_ready, i * 4 + n)
                    scores(i, g, 2 * n + 1)
                    turn(i, g, 2 * n)
                turn(i, g, 7)
                values(i, g, 3)

            for i in range(TT // 2):
                attention(i, i // 2, i == 0)

            pe.wait_ge(o_copied, 32)
            pe.wait_ge(lg_ready, 32)
            pe.wait_ge(made, DCONST + 3)
            pe.wait_ge(tot_ready, 1)
            nc.tensor.matmul(psum[:, 5, 0:256], later[:, :], tot[:, :], start=True, stop=True)
            nc.tensor.matmul(psum[:, 6, 0:256], ones_a[:, :], tot[:, :], start=True, stop=True).then_inc(f_tr, 1)

            pe.wait_ge(bias_ready, 1)
            pe.wait_ge(made, RMASKS + 11)

            def rwkv_tile(i, u, first):
                def at(n, k=1, per=1, back=False):
                    if back and first:
                        return
                    pe.wait_ge(R[n], i * (2 * per) + (u * per + k - (per if back else 0)))

                def mm(out, l, r, start=True, stop=True):
                    return nc.tensor.matmul(out, l, r, start=start, stop=stop, skip_group_check=True)

                hs = [slice((h % 2) * 64, (h % 2) * 64 + 64) for h in range(4)]
                hc = [slice(h * 64, h * 64 + 64) for h in range(4)]
                pe.wait_ge(r_in[u], i * 32 + 32)
                both = [rin[hs[h], u, h // 2:h // 2 + 3:2, :] for h in range(4)]
                at('sqT', 5, 5, back=True)
                at('sq', 4, 4, back=True)
                for h in range(4):
                    last = mm(psum[:, 2 + h % 2, (h // 2) * 256:(h // 2) * 256 + 256].rearrange("p (a c) -> p a c", a=2), rin[hs[h], u, BTI + h // 2, :], both[h])
                last.then_inc(R['gram_b'], 1)
                at('app', 6, 6, back=True)
                at('q', back=True)
                for h in range(4):
                    last = mm(psum[:, 4 + h % 2, (h // 2) * 256:(h // 2) * 256 + 256].rearrange("p (a c) -> p a c", a=2), rin[hs[h], u, KTI + h // 2, :], both[h])
                last.then_inc(R['gram_k'], 1)
                at('tr', 2, 2, back=True)
                at('st', 4, 4, back=True)
                for h in range(4):
                    last = mm(psum[:, 6 + h % 2, (h // 2) * P:(h // 2 + 1) * P], rin[hs[h], u, ALP + h // 2, :], rin[hs[h], u, BTI + h // 2, :])
                last.then_inc(R['gram_m'], 1)
                at('o', back=True)
                for m in range(8):
                    last = transpose(psum[:, m // 4, (m % 4) * P:(m % 4 + 1) * P], rin[:, u, 2 + m, :])
                last.then_inc(R['tok_tr'], 1)
                at('gk')
                at('tok', 6, 6)
                for h in range(4):
                    last = mm(psum[:, 1, hc[h]], gk[:, h, 1, :], tok_v[:, hc[h]])
                last.then_inc(R['kv_mm'], 1)
                at('gb')
                at('gm')
                for l in range(6):
                    mt = (lambda h: gb[:, h, 1, :]) if l == 0 else (lambda h: mpowT[:, l % 2, h, :])
                    m_ = (lambda h: mpow[:, 2, h, :]) if l == 0 else (lambda h: mpow[:, l % 2, h, :])
                    if l > 0:
                        at('sqT', l, 5)
                        if l < 5:
                            at('sq', l, 4)
                    if l < 5:
                        for h in range(4):
                            last = mm(psum[:, 2, h * P:(h + 1) * P], m_(h), mt(h))
                        last.then_inc(R['sqT_mm'], 1)
                    if l < 4:
                        for h in range(4):
                            last = mm(psum[:, 3, h * P:(h + 1) * P], mt(h), m_(h))
                        last.then_inc(R['sq_mm'], 1)
                    if l == 0:
                        at('kv')
                    else:
                        at('app', l, 6)
                    for h in range(4):
                        last = mm(psum[:, 4, h * P:(h + 1) * P], mt(h), sol[:, h, :])
                    last.then_inc(R['app_mm'], 1)
                at('app', 6, 6)
                for h in range(4):
                    last = mm(psum[hs[h], 5, (h // 2) * P:(h // 2 + 1) * P], sol[:, h, 0:64], gb[:, h, 0, :])
                last.then_inc(R['q_mm'], 1)
                for h in range(4):
                    for c in range(2):
                        x = (h // 2) * P + c * 64
                        last = mm(psum[hs[h], 6, x:x + 64], sol[:, h, 0:64], tok_b[:, c, hc[h]])
                last.then_inc(R['tr_mm'], 1)
                at('tr', 2, 2)
                at('pcur')
                for c in range(2):
                    if c == 1:
                        at('st', 2, 4)
                    elif first:
                        pe.wait_ge(state_zero, 4)
                    else:
                        at('st', 4, 4, back=True)
                    for t in range(2):
                        out = psum[:, 7, (c * 2 + t) * P:(c * 2 + t + 1) * P]
                        for h in (2 * t, 2 * t + 1):
                            mm(out[hs[h], hs[h]], tok_k[:, c, hc[h]], tok_v[:, hc[h]], True, False)
                            mm(out[hs[h], hs[h]], tok_b[:, c, hc[h]], sol[:, h, 64:P], False, False)
                        last = mm(out, trans[:, 2 * t + c, :], state[:, u * 4 + c * 2 + t, :], False, True)
                    last.then_inc(R['st_mm'], 1)
                at('q')
                for t in range(2):
                    p0 = t * P
                    for h in (2 * t, 2 * t + 1):
                        mm(psum[hs[h], 0, p0:p0 + P], tok_v[:, hc[h]], gk[:, h, 0, :], True, False)
                        mm(psum[hs[h], 0, p0:p0 + P], sol[:, h, 64:P], gb[:, h, 0, :], False, False)
                    for c in range(2):
                        last = mm(psum[:, 0, p0 + c * 64:p0 + c * 64 + 64], state[:, u * 4 + c * 2 + t, :],
                                  qT_r[:, t, c * 64:c * 64 + 64], False, True)
                last.then_inc(R['o_mm'], 1)

            rwkv_tile(0, 0, True)
            rwkv_tile(0, 1, False)
            with pe.Fori(1, TT // 2) as i:
                rwkv_tile(i, 0, False)
                rwkv_tile(i, 1, False)
            pe.wait_ge(R['st'], 4 * TT)
            pe.wait_ge(R['sqT'], 5 * TT)
            for t in range(2):
                last = transpose(psum[:, 2, t * P:(t + 1) * P], state[:, t, :])
            last.then_inc(wkv_tr, 1)
            pe.wait_ge(R['o'], TT)
            pe.wait_ge(wkv_copied, 2)
            for i in range(DEC_SEQ):
                for n in range(5):
                    pe.wait_ge(s_z, i * 5 + n + 1)
                    if i * 5 + n >= 4:
                        pe.wait_ge(s_used, i * 5 + n - 3)
                    for hf in range(2):
                        last = nc.tensor.matmul(psum[:, 2 * ((i * 5 + n) % 4) + hf, :], ones_head[:, :],
                                                z_exp[:, n, hf * 512:(hf + 1) * 512], start=True, stop=True)
                    last.then_inc(s_mm2, 1)
            pe.wait_ge(s_done, 1)
            pe.wait_ge(gn_in, 16 * 6)
            g = 0
            for k, src in enumerate((o_rw, gn_sq, g_rkk)):
                for t in range(2):
                    for c in range(CHUNKS):
                        if 10 <= g - 8 < 20:
                            pe.wait_ge(gn_pre, g - 17)
                        elif g >= 8:
                            pe.wait_ge(gn_read, g - 7 - (10 if g >= 28 else 0))
                        if k == 1:
                            pe.wait_ge(gn_sq_ready, g - 9)
                        nc.tensor.matmul(psum[:, g % 8, 0:CW], ones_head[:, :], src[:, t, c * CW:(c + 1) * CW],
                                         start=True, stop=True).then_inc(gn_mm, 1)
                        g += 1

            pe.wait_ge(gn_read, 20)
            pe.wait_ge(gn_pre, 10)
            pe.wait_ge(made, DCONST + 12)
            pe.wait_ge(bias_ready, 4)

            def add_bias(t):
                for j in range(4):
                    last = nc.tensor.matmul(psum[:, 4 + t % 2, j * P:(j + 1) * P], bias_w[:, t * 4 + j, :], ident[:, :],
                                            start=False, stop=True, skip_group_check=True)
                last.then_inc(D['b_mm'], 1)

            def sample(b, first, former):
                for t in range(DT):
                    pe.wait_ge(k_in[t % NSLOT], b * 32 + (16 * (t // NSLOT) + 16))
                    for hf in range(2):
                        if not (first and t == 0):
                            pe.wait_ge(D[f'kT{hf}'], D0[f'kT{hf}'] + b * 8 + t)
                        for pr in range(2):
                            for j in range(4):
                                last = transpose(psum[:, 2 * hf + pr, j * P:(j + 1) * P],
                                                 k_slot[:, t % NSLOT, (hf * 4 + j) * 256 + pr * P:(hf * 4 + j) * 256 + (pr + 1) * P])
                        last.then_inc(D['k_tr'], 1)
                    if t == 0:
                        pe.wait_ge(D['prep'], D0['prep'] + b + 1)
                    if t == 0 and not first:
                        pe.wait_ge(D['s'], D0['s'] + b * 9)
                    if t == 1 and not first:
                        pe.wait_ge(D['pT'], D0['pT'] + b * 9)
                    if t >= 2:
                        pe.wait_ge(D['s'], D0['s'] + b * 9 + (t - 1))
                    if t > 0:
                        add_bias(t - 1)
                    for hf in range(2):
                        pe.wait_ge(D[f'kT{hf}'], D0[f'kT{hf}'] + b * 8 + (t + 1))
                        for pr in range(2):
                            g = 32 * (2 * hf + pr)
                            last = nc.tensor.matmul(psum[g:g + 8, 4 + t % 2, :], q_cur[:, pr, :], kT_d[:, hf, pr, :],
                                                    start=True, stop=False, tile_position=(0, g), skip_group_check=True)
                    last.then_inc(D['sc_mm'], 1)
                    if former and t == 0:
                        turn_probs(b - 1)
                    elif former:
                        value_tile(b - 1, t - 1, former == "first")
                add_bias(DT - 1)
                if not first:
                    pe.wait_ge(D['neg_m'], D0['neg_m'] + b)
                nc.tensor.matmul(psum[:, 6, 0:SMP], nm_cur[:, :], ident[:, 0:SMP], start=True, stop=False, skip_group_check=True)
                for pr in range(2):
                    last = nc.tensor.matmul(psum[32 * pr:32 * pr + 8, 6, 0:SMP], q_cur[:, pr, :], kT_s[:, pr, :],
                                            start=False, stop=True, tile_position=(0, 32 * pr), skip_group_check=True)
                last.then_inc(D['new_mm'], 1)
                if former:
                    value_tile(b - 1, DT - 1, former == "first")
                pe.wait_ge(D['m1'], D0['m1'] + b + 1)
                transpose(psum[0:1, 6, P:2 * P], m1[:, :]).then_inc(D['m_tr'], 1)
                pe.wait_ge(D['m_row'], D0['m_row'] + b + 1)
                nc.tensor.matmul(psum[:, 6, 256:257], m_row[:, :], ones_a[0:1, 0:1], start=True, stop=True).then_inc(D['m_mm'], 1)
                if former:
                    combine(b - 1, former == "first")

            def value_tile(b, t, first):
                if t == 0:
                    pe.wait_ge(D['pT'], D0['pT'] + b * 9 + 9)
                    if not first:
                        pe.wait_ge(D['pv'], D0['pv'] + b)
                pe.wait_ge(v_in[t % NSLOT], b * 32 + (16 * (t // NSLOT) + 16))
                for j in range(TJ):
                    g, n = j % 4, t * TJ + j
                    last = nc.tensor.matmul(psum[32 * g:32 * g + 16, 7, 0:256],
                                            pT_d[:, t * 4 + j % 4, 2 * (j // 4):2 * (j // 4) + 2, :].rearrange("p g x -> p (g x)"),
                                            v_slot[:, t % NSLOT, j * 256:(j + 1) * 256], start=(n < 4),
                                            stop=(n >= DT * TJ - 4 and g > 0), tile_position=(0, 32 * g), skip_group_check=True)
                if t == DT - 1:
                    last = nc.tensor.matmul(psum[0:16, 7, 0:256], p_new[:, :], v_new[:, :], start=False, stop=True,
                                            tile_position=(0, 0), skip_group_check=True)
                last.then_inc(D['pv_mm'], 1)

            def combine(b, first):
                pe.wait_ge(D['l_all'], D0['l_all'] + b + 1)
                if not first:
                    pe.wait_ge(D['o'], D0['o'] + b * 4)
                pe.wait_ge(D['pv'], D0['pv'] + b + 1)
                nc.tensor.matmul(psum[:, 7, 256:272], l_all[:, :], sel_r[:, :, :].rearrange("p a x -> p (a x)"), start=True, stop=True)
                for pr in range(2):
                    last = nc.tensor.matmul(psum[:, 7, 288 + pr * 16:304 + pr * 16], pv[:, pr * P:(pr + 1) * P], sel[:, :], start=True, stop=True)
                last.then_inc(D['o_mm'], 1)

            def turn_probs(b):
                pe.wait_ge(D['p'], D0['p'] + b + 1)
                for c in range(DT + 1):
                    if c >= 2:
                        pe.wait_ge(D['pT'], D0['pT'] + b * 9 + (c - 1))
                    if c < DT:
                        for j in range(4):
                            last = transpose(psum[:, 5 + c % 2, j * P:(j + 1) * P], s_rows[:, (c * 4 + j) * P:(c * 4 + j + 1) * P])
                    else:
                        last = transpose(psum[0:SMP, 5 + c % 2, 0:P], s_rows[:, DT * 512:DT * 512 + SMP])
                    last.then_inc(D['p_tr'], 1)

            sample(0, True, None)
            sample(1, False, "first")
            with pe.Fori(2, DEC_BATCH) as b:
                sample(b, False, "later")
            turn_probs(DEC_BATCH - 1)
            for t in range(DT):
                value_tile(DEC_BATCH - 1, t, False)
            combine(DEC_BATCH - 1, False)

            def project(u, n=P):
                for o in range(2):
                    for e in range(8):
                        last = nc.tensor.matmul(psum[0:n, 2 * u + o, :], mt[:, u, e, 0:n], wo[:, e, o * 512:(o + 1) * 512],
                                                start=(e == 0), stop=(e == 7))
                last.then_inc(D['y_mm'], 1)

            pe.wait_ge(rows_in, 16 * (len(ROWS256) + 7 + PT + 2) + 32)
            for u in range(2):
                pe.wait_ge(q_in[u], 16 * (TT // 2) + 16)
                project(u)
            with pe.Fori(1, TT // 2) as i:
                for u in range(2):
                    pe.wait_ge(q_in[u], 16 * (TT // 2) + i * 16 + 16)
                    pe.wait_ge(D['y_sum'], D0['y_sum'] + i * 2 + (u - 1))
                    project(u)
            pe.wait_ge(q_in[0], 16 * (TT // 2) + 16 * (TT // 2 + 1))
            pe.wait_ge(D['y_sum'], D0['y_sum'] + TT - 1)
            project(0, SMP)

        @block.scalar
        def _(act):
            def square(u, rows):
                nc.scalar.activation(zst[0:rows, u, 0:D_MODEL], xt[0:rows, u, :], ACT.Square, scale=D_MODEL ** -0.5,
                                     accum_out=ss[0:rows, u:u + 1]).then_inc(sq_done, 1)

            def root(u, rows):
                nc.scalar.activation(rstd[0:rows, u:u + 1], ss[0:rows, u:u + 1], ACT.Sqrt).then_inc(rstd_ready, 1)

            for u in range(2):
                act.wait_ge(x_in[u], 16)
                square(u, P)
            for u in range(2):
                act.wait_ge(inv_ready, u + 1)
                root(u, P)
            with act.Fori(1, TT // 2) as i:
                for u in range(2):
                    act.wait_ge(x_in[u], i * 16 + 16)
                    act.wait_ge(h_ready, i * 2 + (u - 1))
                    square(u, P)
                for u in range(2):
                    act.wait_ge(inv_ready, i * 2 + (u + 1))
                    root(u, P)
            act.wait_ge(x_in[0], 16 * (TT // 2 + 1))
            square(0, SMP)
            act.wait_ge(inv_ready, TT + 1)
            root(0, SMP)

            def chunk(p, u, c):
                if c == 0 and not (isinstance(p, int) and p == 0):
                    act.wait_ge(z_stored[u], p * 16)
                act.wait_ge(z_mm, p * 10 + (5 * u + c + 1))
                nc.scalar.copy(zst[:, u, c * CW:(c + 1) * CW], psum[:, c, 0:CW]).then_inc(z_evac, 1)
                if c == CHUNKS - 1:
                    act.wait_ge(z_evac, p * 10 + (5 * u + 5))
                    act.dma_start(zT[bass.ds(p * 2 + u, 1)].rearrange("o p t -> p (o t)"), zst[:, u, :]).then_inc(z_stored[u], 16)

            def tile(p, u):
                for c in range(CHUNKS):
                    chunk(p, u, c)

            def pair(p):
                for u in range(2):
                    tile(p, u)

            def a_(out, in_, f, s, **kw):
                nc.scalar.activation(out, in_, f, **kw).then_inc(s, 1)

            def key_squares():
                act.wait_ge(small_read, reads_through(9))
                for n in (2, 3):
                    act.wait_ge(sh_done, n + 1)
                    a_(ksq[:, n - 2, 0:SEQ], sh_mix[:, n % 2, 0:SEQ], ACT.Square, ksq_ready, scale=par[:, n - 2, PKK:PKK + 1])
                    a_(samples(ksq[:, n - 2]), shifted_samples(sh_mix[:, n % 2]), ACT.Square, ksq_ready, scale=par[:, n - 2, PKK:PKK + 1])

            def lora_inputs():
                act.wait_ge(sh_done, 7)
                for (rows, f) in ((slice(0, 64), ACT.Tanh), (slice(64, P), ACT.Copy)):
                    a_(wa[rows, 0:SEQ], sh_mix[rows, 0, 0:SEQ], f, wa_ready)
                    a_(samples(wa[rows]), shifted_samples(sh_mix[rows, 0]), f, wa_ready)

            act.wait_ge(sq_done, TT + 1)
            pair(0)
            with act.Fori(1, 5) as p:
                pair(p)
            act.wait_ge(d_in, 16 * 6)
            for t in range(2):
                a_(u2d[:, t, :], u2d[:, t, :], ACT.Sigmoid, d_sig)
            with act.Fori(5, 7) as p:
                pair(p)
            act.wait_ge(gc_in, 32)
            for t in range(2):
                a_(gate_c[:, t, :], gate_c[:, t, :], ACT.Silu, gates)
            with act.Fori(7, 9) as p:
                pair(p)
            key_squares()
            pair(9)
            act.wait_ge(gd_in, 32)
            for t in range(2):
                a_(gate_d[:, t, :], gate_d[:, t, :], ACT.Silu, gates)
            lora_inputs()
            for c in range(CHUNKS):
                cs = slice(c * CW, (c + 1) * CW)
                for t in range(2):
                    act.wait_ge(small_read, reads_through(9) + 2 * c + t + 1)
                    a_(ln_sq[:, t, cs], conv[:, t, cs], ACT.Square, d_sq)
            for c in range(CHUNKS):
                cs = slice(c * CW, (c + 1) * CW)
                act.wait_ge(d_inv, c + 1)
                a_(ln_inv[:, cs], ln_inv[:, cs], ACT.Sqrt, d_root)
            for c in range(CHUNKS):
                cs = slice(c * CW, (c + 1) * CW)
                for t in range(2):
                    act.wait_ge(d_norm, 2 * c + t + 1)
                    a_(ln_sq[:, t, cs], conv[:, t, cs], ACT.Silu, d_act, scale=par[:, t, PLG:PLG + 1], bias=par[:, t, PLB:PLB + 1])
            tile(10, 0)
            for m in range(CHUNKS):
                chunk(10, 1, m)
                for n in (2 * m, 2 * m + 1):
                    t, cs = n // CHUNKS, slice(n % CHUNKS * CW, (n % CHUNKS + 1) * CW)
                    act.wait_ge(kinv_pre, n + 1)
                    a_(kinv[:, t, cs], kinv[:, t, cs], ACT.Sqrt, kinv_ready)
            n = 0
            act.wait_ge(small_read, reads_through(29))
            for dst, b in ((sig_w, PW0), (rate, PA0)):
                for t in range(2):
                    for c in range(CHUNKS):
                        act.wait_ge(lora_mm, n + 1)
                        a_(dst[:, t, c * CW:(c + 1) * CW], psum[:, 5 + n % 3, 0:CW], ACT.Sigmoid, lora_read, bias=par[:, t, b:b + 1])
                        n += 1
            n = 0
            for t in range(2):
                tile(11 + t, 0)
                for src, sc in ((rw_t, 1.0), (rw_L, 1.0), (rw_L, -1.0)):
                    act.wait_ge(L_ready, n + 1)
                    a_(rw_t[:, 0:SEQ], src[:, 0:SEQ], ACT.Exp, exp_ready, scale=sc)
                    n += 1
                tile(11 + t, 1)
            act.wait_ge(f_pre, 1)
            a_(fa, fx, ACT.Abs, f_abs)
            act.wait_ge(f_abs, 1)
            a_(fa, fa, ACT.Exp, f_abs, scale=-1.0)
            act.wait_ge(f_abs, 2)
            a_(fa, fa, ACT.Ln, f_abs, bias=1.0)
            for m in range(2 * CHUNKS):
                chunk(13, m // CHUNKS, m % CHUNKS)
                n = m - 2
                if n >= 0:
                    for u in range(2):
                        act.wait_ge(kv_copied, 2 * n + u + 1)
                        nc.scalar.copy(vtok[:, 2 * n + u, :], kvs[:, u, 256:512]).then_inc(v_kept, 1)
            def soft(i, g, j):
                w = j % 2
                act.wait_ge(s_max, i * 8 + (j + 1))
                if not (isinstance(i, int) and i == 0 and j < 2):
                    act.wait_ge(lb_ready, i * 4 + (j // 2))
                n = tiles_of(i, j) * P
                nc.scalar.activation(probs[:, w, 0:n], psum[:, 4 * w:4 * w + g + 1, :].rearrange("p b c -> p (b c)")[:, 0:n], ACT.Exp,
                                     bias=nb[:, w:w + 1], scale=0.125, accum_out=lsum[:, w:w + 1]).then_inc(p_ready, 1)

            def gate_rows():
                act.wait_ge(ga_in, 32)
                for t in range(2):
                    a_(gate_a[:, t, :], gate_a[:, t, :], ACT.Silu, gates)
                act.wait_ge(gates, GATE_A + 2)
                a_(gate_s[:, :, :], gate_a[:, :, SEQ:T_ALL], ACT.Copy, gates)

            def turned(i, g, j):
                w = j % 2
                for k in range(g + 1):
                    act.wait_ge(p_tr, bank_turned(i, g, j, k))
                    n = min(512, tiles_of(i, j) * P - 512 * k)
                    nc.scalar.copy(probsT[w][:, 512 * k:512 * k + n], psum[:, 4 * w + k, 0:n]).then_inc(pT_ready, 1)

            def attention(i, g):
                for n in range(4):
                    if n > 0:
                        turned(i, g, 2 * n - 1)
                    soft(i, g, 2 * n)
                    turned(i, g, 2 * n)
                    soft(i, g, 2 * n + 1)
                    if isinstance(i, int) and i == 0 and n == 0:
                        gate_rows()
                turned(i, g, 7)

            for u in range(2):
                act.wait_ge(z_stored[u], 16 * 14)
            for i in range(TT // 2):
                attention(i, i // 2)

            def rwkv_tile(i, u, first):
                def at(n, k=1, per=1, back=False):
                    if back and first:
                        return
                    act.wait_ge(R[n], i * (2 * per) + (u * per + k - (per if back else 0)))

                at('tok_tr')
                at('o_mm', back=True)
                n = 0
                act_src = psum[:, 0:2, :].rearrange("p a b -> p (a b)")
                if first:
                    act.wait_ge(state_zero, 4)
                for dst, m, sc in ((sol[:, :, 0:64], 0, 1.0), (tok_k, 1, 1.0), (tok_b, 2, -1.0), (tok_v[:, :], 3, 1.0)):
                    src = act_src[:, m * 256:(m + 1) * 256]
                    if m == 0:
                        src = src.rearrange("p (h c) -> p h c", h=4)
                    if m in (1, 2):
                        for c in range(2):
                            cs = slice(c * 64, c * 64 + 64)
                            nc.scalar.activation(dst[cs, c, :], src[cs, :], ACT.Copy, scale=sc).then_inc(R['tok'], 1)
                    else:
                        nc.scalar.activation(dst, src, ACT.Copy, scale=sc).then_inc(R['tok'], 1)
                for l in range(4):
                    at('sq_mm', l + 1, 4)
                    nc.scalar.copy(mpow[:, (l + 1) % 2, :, :], psum[:, 3, :].rearrange("p (h c) -> p h c", h=4)).then_inc(R['sq'], 1)
                at('o_mm')
                nc.scalar.copy(o_rw[:, :, bass.ds(i * (2 * P) + u * P, P)], psum[:, 0, 0:256].rearrange("p (t c) -> p t c", t=2)).then_inc(R['o'], 1)

            act.wait_ge(mixa_stored, 32)
            rwkv_tile(0, 0, True)
            rwkv_tile(0, 1, False)
            with act.Fori(1, TT // 2) as i:
                rwkv_tile(i, 0, False)
                rwkv_tile(i, 1, False)
            a_(smp[:, 1], smp[:, 1], ACT.Exp, s_dec)
            act.wait_ge(gn_in, 16 * 6)
            for t in range(2):
                a_(gate_b[:, t, :], gate_b[:, t, :], ACT.Silu, gates)
            n = 0
            for t in range(2):
                for c in range(CHUNKS):
                    cs = slice(c * CW, (c + 1) * CW)
                    act.wait_ge(gn_read, n + 1)
                    a_(gn_sq[:, t, cs], o_rw[:, t, cs], ACT.Square, gn_sq_ready)
                    n += 1
            for n in range(2 * CHUNKS):
                t, cs = n // CHUNKS, slice(n % CHUNKS * CW, (n % CHUNKS + 1) * CW)
                act.wait_ge(gn_mm, 2 * CHUNKS + n + 1)
                a_(gn_inv[:, t, cs], psum[:, (2 * CHUNKS + n) % 8, 0:CW], ACT.Ln, gn_pre, scale=1.0 / 64, bias=gn_eps[:, :])
            for n in range(2 * CHUNKS):
                t, cs = n // CHUNKS, slice(n % CHUNKS * CW, (n % CHUNKS + 1) * CW)
                act.wait_ge(gn_pre, n + 1)
                a_(gn_inv[:, t, cs], gn_inv[:, t, cs], ACT.Exp, gn_root, scale=-0.5)

            def keep_scores(b, t):
                act.wait_ge(D['b_mm'], D0['b_mm'] + b * 8 + (t + 1))
                nc.scalar.copy(s_rows[:, t * 512:(t + 1) * 512], psum[:, 4 + t % 2, :]).then_inc(D['s'], 1)

            def keys(b, first):
                for t in range(1, DT):
                    act.wait_ge(D['k_tr'], D0['k_tr'] + b * 16 + (2 * t + 2))
                    act.wait_ge(D['sc_mm'], D0['sc_mm'] + b * 8 + t)
                    nc.scalar.copy(kT_d[:, 1, :, :].rearrange("p r c -> p (r c)"),
                                   psum[:, 2:4, :].rearrange("p a c -> p (a c)")).then_inc(D['kT1'], 1)
                    keep_scores(b, t - 1)
                keep_scores(b, DT - 1)
                act.wait_ge(D['new_mm'], D0['new_mm'] + b + 1)
                nc.scalar.copy(s_rows[:, DT * 512:DT * 512 + SMP], psum[:, 6, 0:SMP]).then_inc(D['s'], 1)
                act.wait_ge(D['neg_m'], D0['neg_m'] + b + 1)
                if not first:
                    act.wait_ge(D['l_all'], D0['l_all'] + b)
                nc.scalar.activation(s_rows[:, :], s_rows[:, :], ACT.Exp, bias=neg_m[:, :], accum_out=l_row[:, :]).then_inc(D['p'], 1)

            act.wait_ge(mixa_stored, 32 + 32)
            keys(0, True)
            with act.Fori(1, DEC_BATCH) as b:
                keys(b, False)

            def norm(i, u, n=P):
                act.wait_ge(D['y_sum'], D0['y_sum'] + i * 2 + (u + 1))
                if not (isinstance(i, int) and i == 0):
                    act.wait_ge(kv_stored[u], 32 * (TT // 2) + i * 16)
                nc.scalar.activation(yb[0:n, u, :], zst[0:n, u, 0:D_MODEL], ACT.Square, scale=D_MODEL ** -0.5,
                                     accum_out=ss[0:n, u:u + 1]).then_inc(sq_done, 1)
                act.wait_ge(inv_ready, (TT + 1) + i * 2 + (u + 1))
                nc.scalar.activation(rstd[0:n, u:u + 1], ss[0:n, u:u + 1], ACT.Sqrt).then_inc(rstd_ready, 1)

            for u in range(2):
                norm(0, u)
            with act.Fori(1, TT // 2) as i:
                for u in range(2):
                    norm(i, u)
            norm(TT // 2, 0, SMP)

        @block.vector
        def _(dve):
            ch = Chain(dve, dve_chain)
            dve.wait_ge(par_tr, 1)
            v = nc.vector
            v.tensor_copy(par[:, :, :], psum[:, 5, 0:2 * NROW].rearrange("p (t r) -> p t r", t=2)).then_inc(par_ready, 1)
            v.tensor_copy(par7[:, :], psum[:, 5, 84:99]).then_inc(par_ready, 1)
            v.tensor_copy(st_shift[:, :, :], psum[:, 5, 100:156].rearrange("p (t b) -> p t b", t=7)).then_inc(par_ready, 1)
            v.tensor_copy(st_pool[:, :, :], psum[:, 5, 160:400].rearrange("p (t b) -> p t b", t=2)).then_inc(par_ready, 1)
            v.tensor_copy(st_conv[:, :, :], psum[:, 6, 0:480].rearrange("p (t b) -> p t b", t=2)).then_inc(par_ready, 1)
            dve.wait_ge(par_ready, 5)

            def prepare(u, rows):
                ch.link(v.tensor_scalar(ss[0:rows, u:u + 1], ss[0:rows, u:u + 1], RMS_EPS, None, ALU.add))
                v.reciprocal(ss[0:rows, u:u + 1], ss[0:rows, u:u + 1]).then_inc(inv_ready, 1)

            def scale(u, rows):
                v.tensor_scalar(xh[0:rows, u, :], xt[0:rows, u, :], rstd[0:rows, u:u + 1], None, ALU.mult).then_inc(h_ready, 1)

            def collect(u, rows, col):
                src = psum[:, 2 * u:2 * u + 2, :].rearrange("p b (k t) -> p (b k) t", k=4)[:, :, 0:rows]
                g = par7[:, 0:KT].unsqueeze(2).to_broadcast([P, KT, rows])
                v.tensor_tensor(hT[:, :, bass.ds(col, rows)], src, g, ALU.mult).then_inc(hT_ready, 1)

            for u in range(2):
                dve.wait_ge(sq_done, u + 1)
                prepare(u, P)
            for u in range(2):
                dve.wait_ge(rstd_ready, u + 1)
                scale(u, P)
            for u in range(2):
                dve.wait_ge(h_tr, u + 1)
                collect(u, P, u * P)
            with dve.Fori(1, TT // 2) as i:
                with ch.body(i, 1, TT // 2, 2):
                    for u in range(2):
                        dve.wait_ge(sq_done, i * 2 + (u + 1))
                        prepare(u, P)
                    for u in range(2):
                        dve.wait_ge(rstd_ready, i * 2 + (u + 1))
                        dve.wait_ge(h_tr, i * 2 + (u - 1))
                        scale(u, P)
                    for u in range(2):
                        dve.wait_ge(h_tr, i * 2 + (u + 1))
                        collect(u, P, i * (2 * P) + u * P)
            dve.wait_ge(sq_done, TT + 1)
            prepare(0, SMP)
            dve.wait_ge(rstd_ready, TT + 1)
            scale(0, SMP)
            dve.wait_ge(h_tr, TT + 1)
            collect(0, SMP, SEQ)

            dve.wait_ge(made, COUNTS + 1)
            for t in range(2):
                for h in range(2):
                    hs = slice(h * 64, h * 64 + 64)
                    ch.link(v.tensor_scalar(cnt[hs, t, :], cnt[hs, t, :], float(POOL_WINDOWS[t][h]), None, ALU.min))
            ch.link(v.reciprocal(cnt[:, :, :], cnt[:, :, :]))
            ch.link(v.tensor_scalar(one_m_ka[:, :], par[:, :, PKA], -1.0, 1.0, ALU.mult, ALU.add))

            dve.wait_ge(c_in, 64)
            dve.wait_ge(made, PADS + 4)
            for t in range(2):
                ch.link(v.tensor_copy(history(ext_c[:, t], POOL_BUF + SEQ, POOL_S)[:, :, 0:POOL_BUF],
                                      st_pool[:, t, :].rearrange("p (b s) -> p b s", b=DEC_BATCH)))
            for t in range(2):
                e, s0, s1 = ext_c[:, t], sums[:, 0], sums[:, 1]
                n = POOL_EXT

                def double(out, in_, w, rows=slice(0, P)):
                    ch.link(v.tensor_tensor(out[rows, 2 * w - 1:n], in_[rows, 2 * w - 1:n], in_[rows, w - 1:n - w], ALU.add))

                up = slice(64, P)
                double(s0, e, 1)
                if t == 0:
                    double(s1, s0, 2, up)
                else:
                    double(s1, s0, 2)
                    double(s0, s1, 4)
                    double(s1, s0, 8, up)
                for h, src in enumerate((s0, s1)):
                    hs = slice(h * 64, h * 64 + 64)
                    inv = 1.0 / POOL_WINDOWS[t][h]
                    es, ss_ = (history(x, POOL_BUF + SEQ, POOL_S)[hs, :, POOL_BUF:] for x in (e, src))
                    v.scalar_tensor_tensor(samples(pooled[:, t])[hs], ss_, inv, es, ALU.mult, ALU.subtract).then_inc(dve_chain, 1)
                    ch.n += 1
                    v.scalar_tensor_tensor(pooled[hs, t, 16:SEQ], src[hs, POOL_BUF + 16:POOL_BUF + SEQ], inv,
                                           e[hs, POOL_BUF + 16:POOL_BUF + SEQ], ALU.mult, ALU.subtract).then_inc(dve_chain, 1)
                    ch.n += 1
                    ch.link(v.tensor_tensor(fix[hs, t, :], src[hs, POOL_BUF:POOL_BUF + 16], cnt[hs, t, :], ALU.mult))
                    ch.link(v.tensor_tensor(pooled[hs, t, 0:16], fix[hs, t, :], e[hs, POOL_BUF:POOL_BUF + 16], ALU.subtract))
                dve.sem_inc(pooled_ready, 1)

            dve.wait_ge(d_in, 96)
            for t in range(2):
                v.tensor_copy(history(ext_d[:, t], CONV_BUF + SEQ, CONV_S)[:, :, 0:CONV_BUF],
                              st_conv[:, t, :].rearrange("p (b s) -> p b s", b=DEC_BATCH)).then_inc(glu_ready, 1)
                dve.wait_ge(d_sig, t + 1)
                row = ext_d[:, t, CONV_BUF:CONV_BUF + SEQ]
                v.tensor_tensor(row, row, u2d[:, t, 0:SEQ], ALU.mult).then_inc(glu_ready, 1)
                row = history(ext_d[:, t], CONV_BUF + SEQ, CONV_S)[:, :, CONV_BUF:]
                v.tensor_tensor(row, row, samples(u2d[:, t]), ALU.mult).then_inc(glu_ready, 1)
            dve.wait_ge(glu_ready, 6)
            for k in range(CONV_WIDTH):
                for t in range(2):
                    w = par[:, t, PCW + k:PCW + k + 1]
                    outs = (conv[:, t, 0:SEQ], samples(conv[:, t]))
                    ins = (ext_d[:, t, k:k + SEQ], history(ext_d[:, t], CONV_BUF + SEQ, CONV_S)[:, :, k:k + DEC_SEQ])
                    for out, in_ in zip(outs, ins):
                        if k == 0:
                            last = v.tensor_scalar(out, in_, w, par[:, t, PCB:PCB + 1], ALU.mult, ALU.add)
                        else:
                            last = v.scalar_tensor_tensor(out, in_, w, out, ALU.mult, ALU.add)
                        last.then_inc(conv_done, 1)
                if k < CONV_WIDTH - 1:
                    dve.wait_ge(conv_done, 4 * (k + 1))

            dve.wait_ge(gates, GATE_C + 2)
            g = 0
            for t in range(2):
                for c in range(CHUNKS):
                    cs = slice(c * CW, (c + 1) * CW)
                    dve.wait_ge(small_mm, g + 1)
                    v.scalar_tensor_tensor(pooled[:, t, cs], psum[:, 5 + g % 3, 0:CW], par[:, t, PPS:PPS + 1],
                                           gate_c[:, t, cs], ALU.mult, ALU.mult).then_inc(small_read, 1)
                    g += 1

            dve.wait_ge(conv_done, CONV_WIDTH * 4)
            dve.wait_ge(out_stored, 16 * 20)
            for n in range(2):
                ch.link(v.memset(sh_ext[:, n, 0:1], 0.0))
            dve.wait_ge(mix_stored, 32)
            for n in range(7):
                e, o = sh_ext[:, n % 2], sh_mix[:, n % 2]
                dve.wait_ge(sh_in[n % 2], 32 * (n // 2 + 1))
                ch.link(v.tensor_copy(history(e, SEQ + 1, SHIFT_S)[:, :, 0], st_shift[:, n, :]))
                if n >= 2:
                    dve.wait_ge(sh_stored[n % 2], 32 * (n // 2))
                if n in (4, 5):
                    dve.wait_ge(ksq_ready, 2 * (n - 3))
                ch.link(v.tensor_tensor(o[:, 0:SHIFT_EXT - 1], e[:, 0:SHIFT_EXT - 1], e[:, 1:SHIFT_EXT], ALU.subtract))
                v.scalar_tensor_tensor(o[:, 0:SHIFT_EXT - 1], o[:, 0:SHIFT_EXT - 1], par7[:, 8 + n:9 + n],
                                       e[:, 1:SHIFT_EXT], ALU.mult, ALU.add).then_inc(sh_done, 1)

            for c in range(CHUNKS):
                cs = slice(c * CW, (c + 1) * CW)
                dve.wait_ge(small_mm, g + 1)
                for t in range(2):
                    v.tensor_tensor(conv[:, t, cs], conv[:, t, cs], psum[:, 5 + g % 3, 0:CW], ALU.subtract).then_inc(small_read, 1)
                g += 1
            dve.wait_ge(sh_stored[0], 96)
            dve.wait_ge(sh_stored[1], 96)
            dve.wait_ge(wa_ready, 4)
            for c in range(CHUNKS):
                cs = slice(c * CW, (c + 1) * CW)
                dve.wait_ge(small_mm, g + 1)
                v.tensor_scalar(ln_inv[:, cs], psum[:, 5 + g % 3, 0:CW], LN_EPS, None, ALU.add).then_inc(small_read, 1)
                dve.wait_ge(small_read, reads_through(g))
                v.reciprocal(ln_inv[:, cs], ln_inv[:, cs]).then_inc(d_inv, 1)
                g += 1
            for c in range(CHUNKS):
                cs = slice(c * CW, (c + 1) * CW)
                dve.wait_ge(d_root, c + 1)
                for t in range(2):
                    v.tensor_tensor(conv[:, t, cs], conv[:, t, cs], ln_inv[:, cs], ALU.mult).then_inc(d_norm, 1)
            dve.wait_ge(gates, GATE_D + 2)
            for c in range(CHUNKS):
                cs = slice(c * CW, (c + 1) * CW)
                for o in range(2):
                    dve.wait_ge(small_mm, g + 1)
                    v.tensor_tensor(conv[:, o, cs], psum[:, 5 + g % 3, 0:CW], gate_d[:, o, cs], ALU.mult).then_inc(small_read, 1)
                    g += 1

            for t in range(2):
                for c in range(CHUNKS):
                    cs = slice(c * CW, (c + 1) * CW)
                    dve.wait_ge(small_mm, g + 1)
                    v.tensor_scalar(kinv[:, t, cs], psum[:, 5 + g % 3, 0:CW], 1e-12, None, ALU.max).then_inc(small_read, 1)
                    dve.wait_ge(small_read, reads_through(g))
                    v.reciprocal(kinv[:, t, cs], kinv[:, t, cs]).then_inc(kinv_pre, 1)
                    g += 1

            ch.link(v.memset(seg[:, :], 1.0))
            ch.link(v.memset(seg[:, :].rearrange("p (n c) -> p n c", c=CH)[:, :, 0], 0.0))
            dve.wait_ge(kinv_ready, 10)
            dve.wait_ge(lora_read, 20)
            for t in range(2):
                dve.wait_ge(rk_in, 48 * (t + 1))
                ch.link(v.tensor_scalar(sig_w[:, t], sig_w[:, t], DECAY, None, ALU.mult))
                ch.link(v.scalar_tensor_tensor(rw_kk[:, :], rw_k[:, :], par[:, t, PKK:PKK + 1], kinv[:, t], ALU.mult, ALU.mult))
                ch.link(v.tensor_scalar(rw_t[:, :], rate[:, t], par[:, t, PKA:PKA + 1], one_m_ka[:, t:t + 1], ALU.mult, ALU.add))
                ch.link(v.tensor_tensor(rw_k[:, :], rw_t[:, :], rw_k[:, :], ALU.mult))
                ch.link(v.scalar_tensor_tensor(rw_t[:, :], rw_r[:, :], par[:, t, PRK:PRK + 1], rw_k[:, :], ALU.mult, ALU.mult))
                v.tensor_tensor(rate[:, t], rw_kk[:, :], rate[:, t], ALU.mult).then_inc(rkk_ready, 1)
                dve.wait_ge(rkk_ready, t + 1)
                for m, src in ((0, rw_r), (1, sig_w[:, t]), (2, rw_k), (3, rw_kk), (4, rate[:, t])):
                    ch.mark(v.tensor_copy(smp[:, m, t, :], src[:, SEQ:T_ALL]))
                ch.link(v.tensor_tensor_scan(rw_L[:, 0:SEQ], seg[:, :], sig_w[:, t, 0:SEQ], 0.0, ALU.mult, ALU.add))
                dve.wait_ge(rkk_stored, 16 * (t + 1))
                v.tensor_tensor(rw_t[:, 0:SEQ], rw_L[:, 0:SEQ], sig_w[:, t, 0:SEQ], ALU.subtract).then_inc(L_ready, 1)
                dve.wait_ge(exp_ready, 3 * t + 1)
                v.tensor_tensor(rw_kk[:, 0:SEQ], rw_kk[:, 0:SEQ], rw_t[:, 0:SEQ], ALU.mult).then_inc(rw_ready, 1)
                dve.wait_ge(rw_ready, 4 * t + 1)
                dve.sem_inc(L_ready, 1)
                dve.wait_ge(exp_ready, 3 * t + 2)
                ch.link(v.tensor_copy(pend[:, t, :], rw_t[:, 0:SEQ].rearrange("p (n c) -> p n c", c=CH)[:, :, CH - 1]))
                v.tensor_tensor(rw_r[:, 0:SEQ], rw_r[:, 0:SEQ], rw_t[:, 0:SEQ], ALU.mult).then_inc(rw_ready, 1)
                dve.wait_ge(rw_ready, 4 * t + 2)
                dve.sem_inc(L_ready, 1)
                dve.wait_ge(exp_ready, 3 * t + 3)
                v.tensor_tensor(rw_k[:, 0:SEQ], rw_k[:, 0:SEQ], rw_t[:, 0:SEQ], ALU.mult).then_inc(rw_ready, 1)
                v.tensor_tensor(rate[:, t, 0:SEQ], rate[:, t, 0:SEQ], rw_t[:, 0:SEQ], ALU.mult).then_inc(rw_ready, 1)

            dve.wait_ge(made, LANE + 1)
            dve.wait_ge(rows_in, 16 * (len(ROWS256) + 7 + PT + 2))
            ch.link(v.tensor_scalar(lane[:, :], lane[:, :], RT - 1, None, ALU.bitwise_and))
            ch.link(v.tensor_copy(lanef[:, :], lane[:, :]))
            ch.link(v.tensor_copy(pidf[:, :], pidx[:, :]))
            ch.link(v.tensor_scalar(pidf[:, :], pidf[:, :], float(RT), lanef[:, :], ALU.mult, ALU.add))
            v.tensor_copy(pidx[:, :], pidf[:, :]).then_inc(idx_ready, 1)
            dve.wait_ge(rw_stored, 128)
            ch.link(v.memset(ones_t, 1.0))
            v.memset(qaug[64:65, :, :, :], 8.0).then_inc(qones_ready, 1)
            v.tensor_scalar(fx, fx, bf_col[:, :], None, ALU.add).then_inc(f_pre, 1)
            dve.wait_ge(f_abs, 3)
            ch.link(v.tensor_scalar(fx, fx, 0.0, None, ALU.min))
            ch.link(v.tensor_tensor(fx, fa, fx, ALU.subtract))
            v.tensor_scalar(fa, fx, -1.0, None, ALU.mult).then_inc(nl_ready, 1)
            dve.sem_inc(nl_ready, 1)
            ch.mark(v.tensor_tensor_scan(nc_[:, 0:SEQ], ones_t, fx[:, 0:SEQ], 0.0, ALU.mult, ALU.add))
            ch.link(v.tensor_copy(samples(nc_)[:, :, 0], samples(fx)[:, :, 0]))
            for i in range(1, DEC_SEQ):
                ch.link(v.tensor_tensor(samples(nc_)[:, :, i], samples(nc_)[:, :, i - 1], samples(fx)[:, :, i], ALU.add))
            dve.wait_ge(nl_ready, 2)
            dve.sem_inc(nc_ready, 1)

            def kv_copy(u):
                v.tensor_copy(kvs[:, u, :], psum[:, 5 + u, :]).then_inc(kv_copied, 1)

            for u in range(2):
                dve.wait_ge(kv_tr, u + 1)
                kv_copy(u)
            with dve.Fori(1, TT // 2) as i:
                for u in range(2):
                    dve.wait_ge(kv_tr, i * 2 + (u + 1))
                    dve.wait_ge(kv_stored[u], i * 32)
                    dve.wait_ge(v_kept, i * 2 + (u - 1))
                    kv_copy(u)
            dve.wait_ge(kvs_tr, 1)
            v.tensor_copy(kv_s[:, :], psum[0:SMP, 5, :]).then_inc(kvs_copied, 1)
            dve.wait_ge(f_tr, 1)
            v.tensor_copy(lft[:, :, :], psum[:, 7, 0:64].rearrange("p (n h) -> p n h", h=4)).then_inc(f_copied, 1)
            v.tensor_copy(lf_s[:, :], psum[0:SMP, 7, 64:72]).then_inc(f_copied, 1)


            def row_max(i, g, j):
                w = j % 2
                dve.wait_ge(s_mm, i * 8 + (j + 1))
                ch.link(v.reduce_max(mx[:, w:w + 1], psum[:, 4 * w:4 * w + g + 1, :].rearrange("p b c -> p (b c)")[:, 0:tiles_of(i, j) * P], AX.X))
                v.tensor_scalar(nb[:, w:w + 1], mx[:, w:w + 1], -0.125, None, ALU.mult).then_inc(s_max, 1)

            def inverse_sums(i, g, j):
                dve.wait_ge(p_ready, i * 8 + (j + 1))
                ch.link(v.reciprocal(linv[:, :], lsum[:, :]))
                v.tensor_copy(lbc[:, :].rearrange("p (h d) -> p h d", h=2), linv[:, :].unsqueeze(2).to_broadcast([P, 2, 64])).then_inc(lb_ready, 1)

            def finish(i, n):
                pr, u = n % 2, n // 2
                rows = i * (2 * P) + u * P
                gate = gate_a[:, pr, bass.ds(rows, P)]
                dve.wait_ge(o_mm, i * 4 + (n + 1))
                v.tensor_copy(oc[:, :], psum[:, 4, 0:P]).then_inc(o_copied, 1)
                dve.wait_ge(lb_tr, i * 4 + (n + 1))
                v.tensor_tensor(lg[:, :], psum[:, 7, 0:P], gate, ALU.mult).then_inc(lg_ready, 1)
                dve.wait_ge(lg_ready, i * 4 + (n + 1))
                dve.wait_ge(o_copied, i * 4 + (n + 1))
                v.tensor_tensor(gate, oc[:, :], lg[:, :], ALU.mult).then_inc(o_read, 1)
                dve.wait_ge(o_read, i * 4 + (n + 1))

            def attention(i, g):
                for n in range(4):
                    row_max(i, g, 2 * n)
                    if isinstance(i, int) and i == 0 and n == 1:
                        dve.wait_ge(gates, GATE_A + 2)
                    if n > 0:
                        finish(i, n - 1)
                    row_max(i, g, 2 * n + 1)
                    inverse_sums(i, g, 2 * n + 1)
                finish(i, 3)

            for i in range(TT // 2):
                attention(i, i // 2)

            dve.wait_ge(lf_in, 16 * DEC_BATCH * DT)
            B4 = bias[:, :, :].rearrange("p n (j h) -> p n j h", h=4)
            L4 = lf_past[:, :, :].rearrange("p n (j h) -> p n j h", h=4)
            ch.link(v.memset(B4[:, :, TJ - 1, :], 0.0))
            for j in range(TJ - 2, -1, -1):
                ch.link(v.tensor_tensor(B4[:, :, j, :], B4[:, :, j + 1, :], L4[:, :, j + 1, :], ALU.add))
            T3 = tot[:, :].rearrange("p (n h) -> p n h", h=4)
            v.tensor_tensor(T3, B4[:, :, 0, :], L4[:, :, 0, :], ALU.add).then_inc(tot_ready, 1)
            ch.link(v.memset(tsuf[:, :, DT - 1, :], 0.0))
            dve.wait_ge(f_tr, 2)
            ch.link(v.tensor_copy(tsum[:, :], psum[:, 6, 0:256]))
            S4 = tsum[:, :].rearrange("p (b t h) -> p b t h", b=DEC_BATCH, t=DT)
            for t in range(DT - 2, -1, -1):
                ch.link(v.tensor_tensor(tsuf[:, :, t, :], tsuf[:, :, t + 1, :], S4[:, :, t + 1, :], ALU.add))
            ch.link(v.tensor_tensor(tsum[:, :], psum[:, 5, 0:256], tsuf[:, :, :, :].rearrange("p b t h -> p (b t h)"), ALU.add))
            v.tensor_tensor(B4, B4, tsum[:, :].rearrange("p (n h) -> p n h", h=4).unsqueeze(2).to_broadcast([P, DEC_BATCH * DT, TJ, 4]),
                            ALU.add).then_inc(bias_ready, 1)
            dve.wait_ge(mixa_stored, 32)
            dve.wait_ge(made, RMASKS + 11)
            v.memset(state[:, 0:2, :], 0.0).then_inc(state_zero, 1)
            v.memset(trans[:, :, :], 0.0).then_inc(state_zero, 1)
            v.memset(tok_k[:, :, :], 0.0).then_inc(state_zero, 1)
            v.memset(tok_b[:, :, :], 0.0).then_inc(state_zero, 1)
            dve.wait_ge(state_zero, 4)
            v.tensor_tensor(id64[:, :], ident[:, 0:64], ident[:, 64:P], ALU.add).then_inc(id64_ready, 1)
            dve.wait_ge(id64_ready, 1)
            ch.link(v.memset(gn_eps[:, :], GN_EPS))
            dve.wait_ge(made, DCONST + 11)
            for h in range(2):
                hs = slice(h * 64, h * 64 + 64)
                v.tensor_scalar(qbd[hs, :, :, h * 4:h * 4 + 4], qT_s[hs, :, :].rearrange("p t (b q) -> p b t q", q=DEC_SEQ),
                                0.125, None, ALU.mult).then_inc(bias_ready, 1)
            ch.link(v.tensor_copy(v_new[0:SMP, :], kv_s[:, 256:512]))
            nm = nmask[:, :, :].rearrange("p b (h q) -> p b h q", h=4)
            ch.link(v.tensor_tensor(nm, nm, lf_s[:, 4:8].unsqueeze(1).unsqueeze(3).to_broadcast([SMP, DEC_BATCH, 4, DEC_SEQ]), ALU.add))
            ch.link(v.tensor_tensor(sel[:, :], ident[:, 0:16], ident[:, 32:48], ALU.add))
            ch.link(v.tensor_tensor(sel[:, :], sel[:, :], ident[:, 64:80], ALU.add))
            ch.link(v.tensor_tensor(sel[:, :], sel[:, :], ident[:, 96:112], ALU.add))
            rows_of = ident[:, :].rearrange("p (f r c) -> p f r c", f=2, r=2)
            ch.link(v.tensor_tensor(sel_r[:, :, :], rows_of[:, 0, :, 0:8], rows_of[:, 1, :, 0:8], ALU.add))

            def rwkv_tile(i, u, first):
                def at(n, k=1, per=1, back=False):
                    if back and first:
                        return
                    dve.wait_ge(R[n], i * (2 * per) + (u * per + k - (per if back else 0)))

                def heads4(bank, n=4):
                    return psum[:, bank, 0:n * P].rearrange("p (h c) -> p h c", h=n)

                def masks(m):
                    return m[:, :, :].rearrange("p a c -> p (a c)").unsqueeze(1).unsqueeze(1).to_broadcast([P, 2, 2, 256])

                def by_parity(x):
                    return x.rearrange("p (t b) c -> p b t c", b=2)

                at('o_mm', back=True)
                at('gram_b')
                v.tensor_tensor(by_parity(gb[:, :, :, :].rearrange("p h a c -> p h (a c)")),
                                psum[:, 2:4, :].rearrange("p b (h c) -> p b h c", h=2), masks(mneg), ALU.mult).then_inc(R['gb'], 1)
                at('gram_k')
                v.tensor_tensor(by_parity(gk[:, :, :, :].rearrange("p h a c -> p h (a c)")),
                                psum[:, 4:6, :].rearrange("p b (h c) -> p b h c", h=2), masks(mpos), ALU.mult).then_inc(R['gk'], 1)
                at('gram_m')
                v.tensor_tensor(by_parity(mpow[:, 2]), psum[:, 6:8, 0:2 * P].rearrange("p b (h c) -> p b h c", h=2),
                                mrow[:, :].unsqueeze(1).unsqueeze(1).to_broadcast([P, 2, 2, P]), ALU.mult).then_inc(R['gm'], 1)
                v.tensor_copy(pcur[:, :, :], pend[:, :, bass.ds(i * 4 + 2 * u, 2)]).then_inc(R['pcur'], 1)
                at('kv_mm')
                v.tensor_copy(sol[:, :, 64:P], psum[:, 1, 0:256].rearrange("p (h c) -> p h c", h=4)).then_inc(R['kv'], 1)
                at('kv')
                at('tok', 6, 6)
                for l in range(6):
                    if l < 5:
                        at('sqT_mm', l + 1, 5)
                        v.tensor_copy(mpowT[:, (l + 1) % 2, :, :], heads4(2)).then_inc(R['sqT'], 1)
                    at('app_mm', l + 1, 6)
                    if l > 0:
                        at('app', l, 6)
                    v.tensor_tensor(sol[:, :, :], sol[:, :, :], heads4(4), ALU.add).then_inc(R['app'], 1)
                at('q_mm')
                v.tensor_tensor(qT_r[:, :, :], psum[:, 5, 0:256].rearrange("p (t c) -> p t c", t=2), rin[:, u, RHO:RHO + 2, :], ALU.add).then_inc(R['q'], 1)
                at('tr_mm')
                for hh in range(2):
                    hs = slice(hh * 64, hh * 64 + 64)
                    v.tensor_tensor(trans[hs, :, hs], psum[hs, 6, 0:256].rearrange("p (n k) -> p n k", n=4),
                                    id64[hs, :].unsqueeze(1).to_broadcast([64, 4, 64]), ALU.add).then_inc(R['tr'], 1)
                at('pcur')
                for c in range(2):
                    at('st_mm', c + 1, 2)
                    to = u * 4 + 2 if c == 0 else (1 - u) * 4
                    for t in range(2):
                        v.tensor_scalar(state[:, to + t, :], psum[:, 7, (c * 2 + t) * P:(c * 2 + t + 1) * P],
                                        pcur[:, t, c:c + 1], None, ALU.mult).then_inc(R['st'], 1)

            rwkv_tile(0, 0, True)
            rwkv_tile(0, 1, False)
            with dve.Fori(1, TT // 2) as i:
                rwkv_tile(i, 0, False)
                rwkv_tile(i, 1, False)
            dve.wait_ge(wkv_tr, 1)
            for hh in range(2):
                hs = slice(hh * 64, hh * 64 + 64)
                v.tensor_copy(wkv_o[hs, :, :], psum[hs, 2, 0:256].rearrange("p (t c) -> p t c", t=2)[:, :, hs]).then_inc(wkv_copied, 1)

            dve.wait_ge(R['o_mm'], TT)
            dve.wait_ge(s_in, 32)
            dve.wait_ge(s_dec, 1)
            BT = DEC_BATCH * 2

            def bt(x):
                return x.rearrange("p (n k) -> p n k", n=BT)

            S = s_wkv[:, :, :].rearrange("p b c -> p (b c)")

            def column(m, i):
                return smp[:, m].rearrange("p t (b i) -> p b t i", i=DEC_SEQ)[:, :, :, i]

            def rows(n):
                return psum[:, 2 * (n % 4):2 * (n % 4) + 2, :].rearrange("p a b -> p (a b)")

            for i in range(DEC_SEQ):
                for n, m in enumerate((3, 1, 4, 2, 0)):
                    if i > 0:
                        dve.wait_ge(s_mm2, i * 5 - 4 + n)
                    v.tensor_tensor(z_exp[:, n, :].rearrange("p (b t k) -> p b t k", b=DEC_BATCH, t=2),
                                    column(m, i).unsqueeze(3).to_broadcast([P, DEC_BATCH, 2, 64]),
                                    id64[:, :].unsqueeze(1).unsqueeze(1).to_broadcast([P, DEC_BATCH, 2, 64]), ALU.mult).then_inc(s_z, 1)
                k = i * 5
                dve.wait_ge(s_mm2, k + 1)
                v.tensor_tensor(s_tmp[:, :], S, rows(k), ALU.mult).then_inc(s_used, 1)
                dve.wait_ge(s_used, k + 1)
                ch.link(v.reduce_sum(s_kk[:, :], bt(s_tmp), AX.X))
                dve.wait_ge(s_mm2, k + 2)
                v.tensor_tensor(S, S, rows(k + 1), ALU.mult).then_inc(s_used, 1)
                dve.wait_ge(s_used, k + 2)
                dve.wait_ge(s_mm2, k + 3)
                v.tensor_tensor(bt(s_tmp), bt(rows(k + 2)), s_kk[:, :].unsqueeze(2).to_broadcast([P, BT, 64]), ALU.mult).then_inc(s_used, 1)
                dve.wait_ge(s_used, k + 3)
                ch.link(v.tensor_tensor(S, S, s_tmp[:, :], ALU.subtract))
                dve.wait_ge(s_mm2, k + 4)
                vcol = column(5, i).unsqueeze(3).to_broadcast([P, DEC_BATCH, 2, 64])
                b4 = "p (b t k) -> p b t k"
                v.tensor_tensor(s_tm2[:, :].rearrange(b4, b=DEC_BATCH, t=2), rows(k + 3).rearrange(b4, b=DEC_BATCH, t=2), vcol, ALU.mult).then_inc(s_used, 1)
                dve.wait_ge(s_used, k + 4)
                ch.link(v.tensor_tensor(S, S, s_tm2[:, :], ALU.add))
                dve.wait_ge(s_mm2, k + 5)
                v.tensor_tensor(s_tmp[:, :], S, rows(k + 4), ALU.mult).then_inc(s_used, 1)
                dve.wait_ge(s_used, k + 5)
                ch.link(v.reduce_sum(s_kk[:, :], bt(s_tmp), AX.X))
                ch.link(v.tensor_copy(o_rw[:, :, SEQ:T_ALL].rearrange("p t (b i) -> p b t i", i=DEC_SEQ)[:, :, :, i],
                                      s_kk[:, :].rearrange("p (b t) -> p b t", t=2)))
            dve.wait_ge(R['o'], TT)
            dve.sem_inc(s_done, 1)

            g = 0
            for t in range(2):
                for c in range(CHUNKS):
                    cs = slice(c * CW, (c + 1) * CW)
                    dve.wait_ge(gn_mm, g + 1)
                    v.scalar_tensor_tensor(o_rw[:, t, cs], psum[:, g % 8, 0:CW], -1.0 / 64, o_rw[:, t, cs], ALU.mult, ALU.add).then_inc(gn_read, 1)
                    g += 1
            g += 2 * CHUNKS
            for t in range(2):
                for c in range(CHUNKS):
                    cs = slice(c * CW, (c + 1) * CW)
                    dve.wait_ge(gn_mm, g + 1)
                    v.tensor_tensor(g_v[:, t, cs], psum[:, g % 8, 0:CW], g_v[:, t, cs], ALU.mult).then_inc(gn_read, 1)
                    g += 1
            dve.wait_ge(gn_read, 4 * CHUNKS)
            dve.wait_ge(gates, GATE_B + 2)
            for t in range(2):
                for c in range(CHUNKS):
                    cs = slice(c * CW, (c + 1) * CW)
                    dve.wait_ge(gn_root, t * CHUNKS + c + 1)
                    ch.mark(v.tensor_tensor(o_rw[:, t, cs], o_rw[:, t, cs], gn_inv[:, t, cs], ALU.mult))
                ch.join()
                o = o_rw[:, t, :]
                ch.link(v.scalar_tensor_tensor(o, o, par[:, t, PGG:PGG + 1], g_v[:, t, :], ALU.mult, ALU.add))
                v.scalar_tensor_tensor(o, o, par[:, t, PGB:PGB + 1], gate_b[:, t, :], ALU.add, ALU.mult).then_inc(mixb_ready, 1)

            ch.link(v.memset(psum[:, 4:6, :], 0.0))
            v.memset(psum[:, 7, 0:256], 0.0).then_inc(bias_ready, 1)
            dve.wait_ge(bias_ready, 4)
            dve.wait_ge(made, DCONST + 12)
            dve.wait_ge(mixa_stored, 32 + 32)

            def sample(b, first, former):
                if not first:
                    dve.wait_ge(D['new_mm'], D0['new_mm'] + b)
                by_row = bias_w[:, :, :].rearrange("p (t j) (f r x) -> p t j f r x", j=4, f=2, r=2)
                past = bias[:, bass.ds(b * 8, 8), :].rearrange("p t (f j h) -> p t f j h", f=2, h=4)
                for hf in range(2):
                    for h in range(4):
                        ch.mark(v.tensor_copy(by_row[:, :, :, hf, h // 2, (h % 2) * 4:(h % 2) * 4 + 4],
                                              past[:, :, hf, :, h].unsqueeze(3).to_broadcast([P, DT, 4, 4])))
                ch.mark(v.tensor_copy(nm_cur[0:SMP, 0:64].rearrange("p (r x) -> p r x", r=2)[:, :, 0:8],
                                      nmask[:, bass.ds(b, 1), :].rearrange("p o (r x) -> p (o r) x", r=2)))
                ch.mark(v.tensor_copy(q_cur[:, :, :], qbd[:, bass.ds(b, 1), :, :].rearrange("p o r x -> p (o r) x")))
                ch.join()
                dve.sem_inc(D['prep'], 1)
                for t in range(DT):
                    dve.wait_ge(D['k_tr'], D0['k_tr'] + b * 16 + (2 * t + 1))
                    if not (first and t == 0):
                        dve.wait_ge(D['sc_mm'], D0['sc_mm'] + b * 8 + t)
                    v.tensor_copy(kT_d[:, 0, :, :], psum[:, 0:2, :]).then_inc(D['kT0'], 1)
                    if t == 0:
                        dve.wait_ge(D['k_tr'], D0['k_tr'] + b * 16 + 2)
                        v.tensor_copy(kT_d[:, 1, :, :], psum[:, 2:4, :]).then_inc(D['kT1'], 1)
                        if former:
                            turn_probs(b - 1)
                    if t > 0:
                        tile_max(b, t - 1)
                tile_max(b, DT - 1)
                dve.wait_ge(D['s'], D0['s'] + b * 9 + 9)
                ch.mark(v.reduce_max(m8[:, DT:DT + 1], s_rows[:, DT * 512:DT * 512 + SMP], AX.X))
                ch.join()
                v.reduce_max(m1[:, :], m8[:, :], AX.X).then_inc(D['m1'], 1)
                if former:
                    keep_values(b - 1)
                dve.wait_ge(D['m_tr'], D0['m_tr'] + b + 1)
                ch.link(v.reduce_max(m_half[:, :], psum[0:1, 6, P:2 * P].rearrange("p (f c) -> p c f", f=2), AX.X))
                v.tensor_copy(m_row[:, :].rearrange("p (f c) -> p f c", f=2), m_half[:, :].unsqueeze(1).to_broadcast([1, 2, 64])).then_inc(D['m_row'], 1)
                dve.wait_ge(D['m_mm'], D0['m_mm'] + b + 1)
                v.tensor_scalar(neg_m[:, :], psum[:, 6, 256:257], -1.0, None, ALU.mult).then_inc(D['neg_m'], 1)
                if former:
                    outputs_of(b - 1)

            def tile_max(b, t):
                dve.wait_ge(D['s'], D0['s'] + b * 9 + (t + 1))
                ch.mark(v.reduce_max(m8[:, t:t + 1], s_rows[:, t * 512:(t + 1) * 512], AX.X))

            KEYS_LINKS = 10 + DT + 1 + 1

            def keep_values(b):
                dve.wait_ge(D['pv_mm'], D0['pv_mm'] + b * 8 + 8)
                v.tensor_copy(pv[:, :], psum[:, 7, 0:256]).then_inc(D['pv'], 1)

            def outputs_of(b):
                dve.wait_ge(D['o_mm'], D0['o_mm'] + b + 1)
                v.reciprocal(li[:, :], psum[:, 7, 256:272]).then_inc(D['li'], 1)
                dve.wait_ge(D['li'], D0['li'] + b + 1)
                for pr in range(2):
                    for h in range(2):
                        hs = slice(h * 64, h * 64 + 64)
                        x = (pr * 2 + h) * 4
                        v.tensor_tensor(o_s[hs, pr, bass.ds(b * 4, 4)], psum[hs, 7, 288 + pr * 16 + x:292 + pr * 16 + x], li[hs, x:x + 4],
                                        ALU.mult).then_inc(D['o'], 1)

            def turn_probs(b):
                dve.wait_ge(D['p'], D0['p'] + b + 1)
                v.tensor_scalar(l_all[:, :], ones_a[:, :], l_row[:, :], None, ALU.mult).then_inc(D['l_all'], 1)
                for c in range(DT + 1):
                    dve.wait_ge(D['p_tr'], D0['p_tr'] + b * 9 + (c + 1))
                    if c < DT:
                        v.tensor_copy(pT_d[:, c * 4:c * 4 + 4, :, :],
                                      psum[:, 5 + c % 2, :].rearrange("p (j g x) -> p j g x", j=4, g=4)[:, :, :, 0:8]).then_inc(D['pT'], 1)
                    else:
                        v.tensor_copy(p_new[0:SMP, :].rearrange("p (r x) -> p r x", r=2),
                                      psum[0:SMP, 5 + c % 2, 0:64].rearrange("p (r x) -> p r x", r=2)[:, :, 0:8]).then_inc(D['pT'], 1)

            with ch.body(0, 0, 1, KEYS_LINKS):
                sample(0, True, False)
            with ch.body(0, 0, 1, KEYS_LINKS):
                sample(1, False, True)
            with dve.Fori(2, DEC_BATCH) as b:
                with ch.body(b, 2, DEC_BATCH, KEYS_LINKS):
                    sample(b, False, True)
            turn_probs(DEC_BATCH - 1)
            keep_values(DEC_BATCH - 1)
            outputs_of(DEC_BATCH - 1)
            dve.wait_ge(D['o'], D0['o'] + 4 * DEC_BATCH)
            dve.wait_ge(gates, GATE_S + 1)
            v.tensor_tensor(o_s[:, :, :], o_s[:, :, :], gate_s[:, :, :], ALU.mult).then_inc(mixas_ready, 1)

            dve.wait_ge(rows_in, 16 * (len(ROWS256) + 7 + PT + 2) + 32)

            def residual(i, u, n=P):
                dve.wait_ge(D['y_mm'], D0['y_mm'] + i * 2 + (u + 1))
                dve.wait_ge(kvt_in[u], 16 * (TT // 2 + 1 - u) + i * 16 + 16)
                row = zst[0:n, u, 0:D_MODEL]
                v.tensor_tensor(row, row, psum[0:n, 2 * u:2 * u + 2, :].rearrange("p a b -> p (a b)"), ALU.add).then_inc(D['y_sum'], 1)

            def final(i, u, n=P):
                dve.wait_ge(sq_done, (TT + 1) + i * 2 + (u + 1))
                ch.link(v.tensor_scalar(ss[0:n, u:u + 1], ss[0:n, u:u + 1], RMS_EPS, None, ALU.add))
                v.reciprocal(ss[0:n, u:u + 1], ss[0:n, u:u + 1]).then_inc(inv_ready, 1)
                dve.wait_ge(rstd_ready, (TT + 1) + i * 2 + (u + 1))
                v.scalar_tensor_tensor(yb[0:n, u, :], zst[0:n, u, 0:D_MODEL], rstd[0:n, u:u + 1], gf[0:n, :], ALU.mult, ALU.mult).then_inc(h_ready, 1)

            for u in range(2):
                residual(0, u)
                final(0, u)
            with dve.Fori(1, TT // 2) as i:
                with ch.body(i, 1, TT // 2, 2):
                    for u in range(2):
                        residual(i, u)
                        final(i, u)
            residual(TT // 2, 0, SMP)
            final(TT // 2, 0, SMP)


OUTS = [('y_prompt', (1, 2048, 1024)), ('y_sample', (8, 4, 1024)),
        ('k_prompt', (1, 1, 2048, 4, 64)), ('v_prompt', (1, 1, 2048, 4, 64)), ('logf_prompt', (1, 1, 2048, 4)),
        ('wkv_prompt', (1, 1, 4, 64, 64)), ('shift_prompt', (1, 1, 896)), ('pool_prompt', (1, 1, 15, 256)),
        ('conv_prompt', (1, 1, 30, 256)),
        ('k_sample', (8, 1, 4, 4, 64)), ('v_sample', (8, 1, 4, 4, 64)), ('logf_sample', (8, 1, 4, 4)),
        ('wkv_sample', (8, 1, 4, 64, 64)), ('shift_sample', (8, 1, 896)), ('pool_sample', (8, 1, 15, 256)),
        ('conv_sample', (8, 1, 30, 256))]


def kernel(**inputs):
    import numpy as np
    import concourse.bacc as bacc
    from concourse.bass_utils import run_bass_kernel_spmd as run

    nc = bacc.Bacc("TRN2", target_bir_lowering=False, num_devices=1)
    arrays, I = {}, {}
    for name, a in inputs.items():
        a = np.ascontiguousarray(a)
        arrays["in_" + name] = a
        I[name] = nc.dram_tensor("in_" + name, a.shape, mybir.dt.from_np(a.dtype), kind="ExternalInput").ap()
    O = {n: nc.dram_tensor("out_" + n, s, F32, kind="ExternalOutput").ap() for n, s in OUTS}
    build(nc, I, O)
    r = run(nc, [arrays], core_ids=[0])
    return tuple(r.results[0]["out_" + n] for n, _ in OUTS)
```
